# Optimizing a Trainium2 kernel written in Bass

```python
import jax, jax.numpy as jnp
from jax import lax
import numpy as np

D_MODEL = 1024
BATCH = 1
SEQ = 512
DEPTH = 2

GRID_W = 64
CTX_LEN = 256
BRANCH = 256
MIX_WIDTH = 4 * BRANCH
CONV_K = 3
ATT_HEADS = 4
ATT_KV_HEADS = 2
HEAD_DIM = 64
ROPE_THETA = 10000.0
Q_BLOCK = 128
HG_HEADS = 4
HG_DK = BRANCH // HG_HEADS
HG_DV = BRANCH // HG_HEADS
HG_CHUNK = 64
FN_GROUPS = 4
FN_DIM = BRANCH // FN_GROUPS
EPS = 1e-6

IN_SPLITS = (256, 256, 256, 256,
             256, 128, 128, 256,
             256, 256, 256, 256, 256,
             256, 256)
IN_COLS = 3584


def rms_norm(x, g):
    xf = x.astype(jnp.float32)
    y = xf * lax.rsqrt(jnp.mean(xf * xf, axis=-1, keepdims=True) + EPS)
    return (y * g.astype(jnp.float32)).astype(x.dtype)

def split_cols(t):
    points = [int(p) for p in np.cumsum(IN_SPLITS)[:-1]]
    return jnp.split(t, points, axis=-1)

def axial_rope_tables(rows, dtype):
    r, cidx = jnp.meshgrid(jnp.arange(rows), jnp.arange(GRID_W), indexing="ij")
    r = r.reshape(-1).astype(jnp.float32)
    cidx = cidx.reshape(-1).astype(jnp.float32)
    n_pairs = HEAD_DIM // 4
    freqs = ROPE_THETA ** (-jnp.arange(n_pairs, dtype=jnp.float32) / n_pairs)
    ang = jnp.concatenate([r[:, None] * freqs, cidx[:, None] * freqs], axis=-1)
    return jnp.cos(ang).astype(dtype), jnp.sin(ang).astype(dtype)

def apply_rope(x, cos, sin):
    x1, x2 = x[..., 0::2], x[..., 1::2]
    return jnp.stack([x1 * cos - x2 * sin, x1 * sin + x2 * cos], axis=-1).reshape(x.shape)

def to_heads(t, n_heads):
    b, n, _ = t.shape
    return t.reshape(b, n, n_heads, -1).transpose(0, 2, 1, 3)

def from_heads(t):
    b, h, n, d = t.shape
    return t.transpose(0, 2, 1, 3).reshape(b, n, h * d)

def short_conv(u, w):
    up = jnp.pad(u, ((0, 0), (1, 1), (0, 0)))
    return up[:, :-2] * w[0] + up[:, 1:-1] * w[1] + up[:, 2:] * w[2]

def attend(qb, k, v):
    s = jnp.einsum("bhgqd,bhkd->bhgqk", qb, k).astype(jnp.float32) * (HEAD_DIM ** -0.5)
    p = jax.nn.softmax(s, axis=-1).astype(v.dtype)
    return jnp.einsum("bhgqk,bhkd->bhgqd", p, v)

def gqa_branch(q_l, k_l, v_l, q_c, k_c, v_c, q_g, k_g, cos, sin, need_ctx):
    b, n, _ = q_l.shape
    g = ATT_HEADS // ATT_KV_HEADS
    ql = apply_rope(rms_norm(to_heads(q_l, ATT_HEADS), q_g), cos, sin)
    kl = apply_rope(rms_norm(to_heads(k_l, ATT_KV_HEADS), k_g), cos, sin)
    vl = to_heads(v_l, ATT_KV_HEADS)
    kc = rms_norm(to_heads(k_c, ATT_KV_HEADS), k_g)
    vc = to_heads(v_c, ATT_KV_HEADS)
    k_all = jnp.concatenate([kl, kc], axis=2)
    v_all = jnp.concatenate([vl, vc], axis=2)
    nb = n // Q_BLOCK
    qb = ql.reshape(b, ATT_KV_HEADS, g, nb, Q_BLOCK, HEAD_DIM).transpose(3, 0, 1, 2, 4, 5)
    ob = lax.map(lambda blk: attend(blk, k_all, v_all), qb)
    o_lat = ob.transpose(1, 0, 4, 2, 3, 5).reshape(b, n, ATT_HEADS * HEAD_DIM)
    o_ctx = None
    if need_ctx:
        nc = q_c.shape[1]
        qc = rms_norm(to_heads(q_c, ATT_HEADS), q_g).reshape(b, ATT_KV_HEADS, g, nc, HEAD_DIM)
        oc = attend(qc, kc, vc)
        o_ctx = oc.transpose(0, 3, 1, 2, 4).reshape(b, nc, ATT_HEADS * HEAD_DIM)
    return o_lat, o_ctx

def hgrn_lower_bounds(lb_param):
    p = jax.nn.softmax(lb_param.astype(jnp.float32), axis=1)
    cs = jnp.cumsum(p, axis=1)
    return cs - cs[:, :1]

def hgrn_gates(fx, lb):
    fx = fx.astype(jnp.float32)
    log_f = jnp.logaddexp(jnp.log(lb), jnp.log1p(-lb) + jax.nn.log_sigmoid(fx))
    k = (1.0 - lb) * jax.nn.sigmoid(-fx)
    return log_f, k

def hgrn_scan(q, k, v, log_f, s0, with_output):
    b, h, t, _ = q.shape
    n = t // HG_CHUNK

    def chunks(a):
        return a.astype(jnp.float32).reshape(b, h, n, HG_CHUNK, a.shape[-1]).transpose(2, 0, 1, 3, 4)

    causal = jnp.tril(jnp.ones((HG_CHUNK, HG_CHUNK), dtype=bool))[:, :, None]

    def step(state, inp):
        qc, kc, vc, lf = inp
        a = jnp.cumsum(lf, axis=2)
        a_last = a[:, :, -1:, :]
        s_new = jnp.exp(a_last)[:, :, 0, :, None] * state + jnp.einsum(
            "bhsk,bhsv->bhkv", kc * jnp.exp(a_last - a), vc)
        if not with_output:
            return s_new, None
        inter = jnp.einsum("bhtk,bhkv->bhtv", qc * jnp.exp(a), state)
        diff = a[:, :, :, None, :] - a[:, :, None, :, :]
        dec = jnp.exp(jnp.where(causal, diff, -jnp.inf))
        scores = jnp.einsum("bhtk,bhsk,bhtsk->bhts", qc, kc, dec)
        intra = jnp.einsum("bhts,bhsv->bhtv", scores, vc)
        return s_new, inter + intra

    s_fin, out = lax.scan(step, s0, (chunks(q), chunks(k), chunks(v), chunks(log_f)))
    if with_output:
        out = out.transpose(1, 2, 0, 3, 4).reshape(b, h, t, v.shape[-1])
    return s_fin, out

def hgrn_branch(q_l, ff_l, fb_l, i_l, q_c, ff_c, fb_c, i_c, lb, hg_g, need_ctx):
    b = q_l.shape[0]
    ql = to_heads(jax.nn.silu(q_l), HG_HEADS)
    il = to_heads(i_l, HG_HEADS)
    qc = to_heads(jax.nn.silu(q_c), HG_HEADS)
    ic = to_heads(i_c, HG_HEADS)
    o_lat, o_ctx = 0.0, 0.0
    for d, (f_l, f_c) in enumerate(((ff_l, ff_c), (fb_l, fb_c))):
        flip = (lambda a: a[:, :, ::-1]) if d == 1 else (lambda a: a)
        logf_l, k_l = hgrn_gates(f_l, lb[d])
        logf_c, k_c = hgrn_gates(f_c, lb[d])
        s0 = jnp.zeros((b, HG_HEADS, HG_DK, HG_DV), jnp.float32)
        s_ctx, oc = hgrn_scan(flip(qc), flip(to_heads(k_c, HG_HEADS)), flip(ic),
                              flip(to_heads(logf_c, HG_HEADS)), s0, need_ctx)
        _, ol = hgrn_scan(flip(ql), flip(to_heads(k_l, HG_HEADS)), flip(il),
                          flip(to_heads(logf_l, HG_HEADS)), s_ctx, True)
        o_lat = o_lat + flip(ol)
        if need_ctx:
            o_ctx = o_ctx + flip(oc)
    gain = hg_g.reshape(HG_HEADS, 1, HG_DV)
    out_l = from_heads(rms_norm(o_lat, gain)).astype(q_l.dtype)
    out_c = from_heads(rms_norm(o_ctx, gain)).astype(q_l.dtype) if need_ctx else None
    return out_l, out_c

def fourier_mix(u):
    b, t, _ = u.shape
    uf = u.astype(jnp.float32).reshape(b, t, FN_GROUPS, FN_DIM)
    y = jnp.fft.fft2(uf, axes=(1, 3), norm="ortho").real
    return y.reshape(b, t, BRANCH).astype(u.dtype)

def mix_stream(parts, conv_w):
    cb, cc, cv, cz, _, _, _, az, _, _, _, _, hz, fu, fz = parts
    y_conv = cb * short_conv(cc * cv, conv_w) * jax.nn.silu(cz)
    y_four = fourier_mix(fu) * jax.nn.silu(fz)
    return y_conv, y_four, jax.nn.silu(az), jax.nn.silu(hz)

def hybrid_layer(h, hc, c_act, cc_act, norm_g, w_mod, b_mod, w_in, conv_w, q_g, k_g, lb, hg_g,
                 w_out, cos, sin, need_ctx):
    shift, scale, gate = jnp.split((c_act @ w_mod + b_mod)[:, None, :], 3, axis=-1)
    shift_c, scale_c, gate_c = jnp.split(cc_act @ w_mod + b_mod, 3, axis=-1)
    lat = split_cols((rms_norm(h, norm_g) * (1.0 + scale) + shift) @ w_in)
    cx = split_cols((rms_norm(hc, norm_g) * (1.0 + scale_c) + shift_c) @ w_in)

    att_l, att_c = gqa_branch(lat[4], lat[5], lat[6], cx[4], cx[5], cx[6], q_g, k_g, cos, sin, need_ctx)
    hg_l, hg_c = hgrn_branch(lat[8], lat[9], lat[10], lat[11], cx[8], cx[9], cx[10], cx[11],
                             lb, hg_g, need_ctx)

    y_conv, y_four, g_att, g_hg = mix_stream(lat, conv_w)
    y = jnp.concatenate([y_conv, att_l * g_att, hg_l * g_hg, y_four], axis=-1) @ w_out
    h_new = h + gate * y
    hc_new = None
    if need_ctx:
        yc_conv, yc_four, gc_att, gc_hg = mix_stream(cx, conv_w)
        yc = jnp.concatenate([yc_conv, att_c * gc_att, hg_c * gc_hg, yc_four], axis=-1) @ w_out
        hc_new = hc + gate_c * yc
    return h_new, hc_new

def first_inputs(seed: int = 0) -> dict:
    key = jax.random.key(seed)
    ks = jax.random.split(key, 16)
    f32 = jnp.float32
    nrm = lambda k, shape: jax.random.normal(k, shape, f32)
    return {
        "x": nrm(ks[0], (BATCH, SEQ, D_MODEL)),
        "c": nrm(ks[1], (BATCH, D_MODEL)),
        "ctx": nrm(ks[2], (BATCH, CTX_LEN, D_MODEL)),
        "c_ctx": nrm(ks[3], (D_MODEL,)),
        "norm_g": 1.0 + 0.1 * nrm(ks[4], (DEPTH, D_MODEL)),
        "w_mod": nrm(ks[5], (DEPTH, D_MODEL, 3 * D_MODEL)) * (0.5 * D_MODEL ** -0.5),
        "b_mod": 0.02 * nrm(ks[6], (DEPTH, 3 * D_MODEL)),
        "w_in": nrm(ks[7], (DEPTH, D_MODEL, IN_COLS)) * (D_MODEL ** -0.5),
        "conv_w": nrm(ks[8], (DEPTH, CONV_K, BRANCH)) * (CONV_K ** -0.5),
        "q_norm_g": 1.0 + 0.1 * nrm(ks[9], (DEPTH, HEAD_DIM)),
        "k_norm_g": 1.0 + 0.1 * nrm(ks[10], (DEPTH, HEAD_DIM)),
        "hgrn_lb": nrm(ks[11], (2, DEPTH, BRANCH)),
        "hgrn_norm_g": 1.0 + 0.1 * nrm(ks[12], (DEPTH, BRANCH)),
        "w_out": nrm(ks[13], (DEPTH, MIX_WIDTH, D_MODEL)) * (MIX_WIDTH ** -0.5),
        "final_g": 1.0 + 0.1 * nrm(ks[14], (D_MODEL,)),
    }

def first_block(x, c, ctx, c_ctx, norm_g, w_mod, b_mod, w_in, conv_w, q_norm_g, k_norm_g,
              hgrn_lb, hgrn_norm_g, w_out, final_g):
    rows = x.shape[1] // GRID_W
    cos, sin = axial_rope_tables(rows, x.dtype)
    lb_all = hgrn_lower_bounds(hgrn_lb)
    c_act = jax.nn.silu(c)
    cc_act = jax.nn.silu(c_ctx)
    h, hc = x, ctx
    for layer in range(DEPTH):
        h, hc = hybrid_layer(h, hc, c_act, cc_act, norm_g[layer], w_mod[layer], b_mod[layer],
                             w_in[layer], conv_w[layer], q_norm_g[layer], k_norm_g[layer],
                             lb_all[:, layer], hgrn_norm_g[layer], w_out[layer], cos, sin,
                             need_ctx=layer < DEPTH - 1)
    return rms_norm(h, final_g)


DEPTH_2 = 1

MEM_LEN = 256
ATTN_HEADS = 8
ATTN_KV_HEADS = 2
ATTN_HEAD_DIM = 64
ATTN_GROUP = ATTN_HEADS // ATTN_KV_HEADS
WINDOW = 128
ATTN_BLOCK = 128
DN_HEADS = 4
DN_HEAD_K = 128
DN_HEAD_V = 128
DN_CONV = 5
DN_CHUNK = 64
N_DIRS = 2
CROSS_HEADS = 4
CROSS_HEAD_DIM = D_MODEL // CROSS_HEADS
D_FF = -(-8 * D_MODEL // (3 * 256)) * 256
ATTN_WIDTH = ATTN_HEADS * ATTN_HEAD_DIM
DN_WIDTH = DN_HEADS * DN_HEAD_V
MIX_WIDTH_2 = ATTN_WIDTH + DN_WIDTH
DN_QKV = DN_HEADS * (2 * DN_HEAD_K + DN_HEAD_V)
IN_SIZES = [ATTN_WIDTH, ATTN_KV_HEADS * ATTN_HEAD_DIM, ATTN_KV_HEADS * ATTN_HEAD_DIM,
            DN_QKV, DN_WIDTH, N_DIRS * DN_HEADS, N_DIRS * DN_HEADS]
IN_COLS_2 = int(np.sum(IN_SIZES))
IN_SPLITS_2 = [int(v) for v in np.cumsum(IN_SIZES)[:-1]]


def _rms_norm(x, gain):
    xf = x.astype(jnp.float32)
    y = xf * lax.rsqrt(jnp.mean(xf * xf, axis=-1, keepdims=True) + EPS)
    return (y * gain.astype(jnp.float32)).astype(x.dtype)

def _l2norm(x):
    return x * lax.rsqrt(jnp.sum(x * x, axis=-1, keepdims=True) + EPS)

def _rope(x, positions):
    half = x.shape[-1] // 2
    inv_freq = ROPE_THETA ** (-jnp.arange(half, dtype=jnp.float32) / half)
    ang = positions.astype(jnp.float32)[..., None] * inv_freq
    cos = jnp.cos(ang)[:, :, None, :]
    sin = jnp.sin(ang)[:, :, None, :]
    xf = x.astype(jnp.float32)
    x1, x2 = xf[..., :half], xf[..., half:]
    return jnp.concatenate([x1 * cos - x2 * sin, x2 * cos + x1 * sin], axis=-1)

def _window_attention(q, k, v, sink):
    b, s = q.shape[0], q.shape[1]
    nb = s // ATTN_BLOCK
    qb = q.reshape(b, nb, ATTN_BLOCK, ATTN_KV_HEADS, ATTN_GROUP, ATTN_HEAD_DIM)

    def band(t):
        tp = t.reshape(b, nb, ATTN_BLOCK, ATTN_KV_HEADS, ATTN_HEAD_DIM)
        tp = jnp.pad(tp, ((0, 0), (1, 1), (0, 0), (0, 0), (0, 0)))
        return jnp.concatenate([tp[:, :-2], tp[:, 1:-1], tp[:, 2:]], axis=2)

    kw, vw = band(k), band(v)
    scores = jnp.einsum('bnqhgd,bnkhd->bnhgqk', qb, kw) * (ATTN_HEAD_DIM ** -0.5)
    qi = jnp.arange(ATTN_BLOCK)[:, None]
    ki = jnp.arange(3 * ATTN_BLOCK)[None, :]
    in_band = jnp.abs(ki - ATTN_BLOCK - qi) <= WINDOW
    kpos = (jnp.arange(nb)[:, None] - 1) * ATTN_BLOCK + jnp.arange(3 * ATTN_BLOCK)[None, :]
    in_seq = (kpos >= 0) & (kpos < s)
    mask = in_band[None, :, :] & in_seq[:, None, :]
    scores = jnp.where(mask[None, :, None, None], scores, -jnp.inf)
    sk = sink.astype(jnp.float32).reshape(ATTN_KV_HEADS, ATTN_GROUP)[None, None, :, :, None, None]
    m = jnp.maximum(jnp.max(scores, axis=-1, keepdims=True), sk)
    p = jnp.exp(scores - m)
    denom = jnp.sum(p, axis=-1, keepdims=True) + jnp.exp(sk - m)
    o = jnp.einsum('bnhgqk,bnkhd->bnqhgd', p / denom, vw)
    return o.reshape(b, s, ATTN_WIDTH)

def _gated_delta_chunked(q, k, v, g, beta):
    b, h, s, dk = q.shape
    dv = v.shape[-1]
    c = DN_CHUNK
    n = s // c
    q = q.reshape(b, h, n, c, dk)
    k = k.reshape(b, h, n, c, dk)
    v = v.reshape(b, h, n, c, dv)
    g = jnp.cumsum(g.reshape(b, h, n, c), axis=-1)
    beta = beta.reshape(b, h, n, c)
    incl = jnp.tril(jnp.ones((c, c), dtype=bool))
    strict = jnp.tril(jnp.ones((c, c), dtype=bool), k=-1)
    decay = jnp.exp(jnp.where(incl, g[..., :, None] - g[..., None, :], -jnp.inf))
    kb = k * beta[..., None]
    lower = jnp.where(strict, jnp.einsum('bhnid,bhnjd->bhnij', kb, k) * decay, 0.0)
    tmat = lower + jnp.eye(c, dtype=jnp.float32)
    rhs = jnp.concatenate([v * beta[..., None], kb * jnp.exp(g)[..., None]], axis=-1)
    sol = lax.linalg.triangular_solve(tmat, rhs, left_side=True, lower=True, unit_diagonal=True)
    u, w = sol[..., :dv], sol[..., dv:]
    qk = jnp.einsum('bhnid,bhnjd->bhnij', q, k) * decay
    qg = q * jnp.exp(g)[..., None]
    kg = k * jnp.exp(g[..., -1:] - g)[..., None]
    g_last = jnp.exp(g[..., -1])

    def step(state, inp):
        qg_i, kg_i, u_i, w_i, qk_i, gl_i = inp
        v_new = u_i - jnp.einsum('bhck,bhkv->bhcv', w_i, state)
        o_i = jnp.einsum('bhck,bhkv->bhcv', qg_i, state) + jnp.einsum('bhij,bhjv->bhiv', qk_i, v_new)
        state = state * gl_i[..., None, None] + jnp.einsum('bhck,bhcv->bhkv', kg_i, v_new)
        return state, o_i

    xs = tuple(jnp.moveaxis(t, 2, 0) for t in (qg, kg, u, w, qk, g_last))
    state0 = jnp.zeros((b, h, dk, dv), jnp.float32)
    _, o = lax.scan(step, state0, xs)
    return jnp.moveaxis(o, 0, 2).reshape(b, h, s, dv)

def _gated_deltanet(qkv, gate, a, bt, conv_w, a_log, dt_bias, g_out):
    b, s = qkv.shape[0], qkv.shape[1]
    ch = qkv.shape[-1]
    pad = DN_CONV // 2
    conv = lax.conv_general_dilated(qkv, conv_w.reshape(DN_CONV, 1, ch).astype(qkv.dtype),
                                    window_strides=(1,), padding=[(pad, pad)],
                                    dimension_numbers=('NWC', 'WIO', 'NWC'), feature_group_count=ch)
    conv = jax.nn.silu(conv.astype(jnp.float32))
    nq = DN_HEADS * DN_HEAD_K
    q = conv[..., :nq].reshape(b, s, DN_HEADS, DN_HEAD_K)
    k = conv[..., nq:2 * nq].reshape(b, s, DN_HEADS, DN_HEAD_K)
    v = conv[..., 2 * nq:].reshape(b, s, DN_HEADS, DN_HEAD_V)
    q = (_l2norm(q) * (DN_HEAD_K ** -0.5)).transpose(0, 2, 1, 3)
    k = _l2norm(k).transpose(0, 2, 1, 3)
    v = v.transpose(0, 2, 1, 3)
    a = a.astype(jnp.float32).reshape(b, s, N_DIRS, DN_HEADS)
    bt = bt.astype(jnp.float32).reshape(b, s, N_DIRS, DN_HEADS)
    g = -jnp.exp(a_log.astype(jnp.float32)) * jax.nn.softplus(a + dt_bias.astype(jnp.float32))
    g = g.transpose(2, 0, 3, 1)
    beta = jax.nn.sigmoid(bt).transpose(2, 0, 3, 1)
    o_fwd = _gated_delta_chunked(q, k, v, g[0], beta[0])
    flip = lambda t: jnp.flip(t, axis=2)
    o_bwd = flip(_gated_delta_chunked(flip(q), flip(k), flip(v), flip(g[1]), flip(beta[1])))
    o = (o_fwd + o_bwd).transpose(0, 2, 1, 3)
    o = o * lax.rsqrt(jnp.mean(o * o, axis=-1, keepdims=True) + EPS) * g_out.astype(jnp.float32)
    o = o * jax.nn.silu(gate.astype(jnp.float32).reshape(b, s, DN_HEADS, DN_HEAD_V))
    return o.reshape(b, s, DN_WIDTH)

def _memory_cross_attention(h, mem_n, w_q, w_kv, w_o):
    b, s = h.shape[0], h.shape[1]
    m = mem_n.shape[1]
    q = (h @ w_q).reshape(b, s, CROSS_HEADS, CROSS_HEAD_DIM).astype(jnp.float32)
    kv = mem_n @ w_kv
    k = kv[..., :D_MODEL].reshape(b, m, CROSS_HEADS, CROSS_HEAD_DIM).astype(jnp.float32)
    v = kv[..., D_MODEL:].reshape(b, m, CROSS_HEADS, CROSS_HEAD_DIM).astype(jnp.float32)
    p = jax.nn.softmax(jnp.einsum('bqhd,bkhd->bhqk', q, k) * (CROSS_HEAD_DIM ** -0.5), axis=-1)
    o = jnp.einsum('bhqk,bkhd->bqhd', p, v).reshape(b, s, D_MODEL).astype(h.dtype)
    return o @ w_o

def _swiglu(h, w_gate_up, w_down):
    gu = h @ w_gate_up
    return (jax.nn.silu(gu[..., :D_FF]) * gu[..., D_FF:]) @ w_down

def second_inputs(seed: int = 0) -> dict:
    key = jax.random.key(seed)
    ks = jax.random.split(key, 24)
    f32 = jnp.float32

    def dense(k, fan_in, fan_out):
        return jax.random.normal(k, (DEPTH_2, fan_in, fan_out), f32) * fan_in ** -0.5

    def gain(k, n):
        return 1.0 + 0.02 * jax.random.normal(k, (DEPTH_2, n), f32)

    x = jax.random.normal(ks[0], (BATCH, SEQ, D_MODEL), f32)
    mem = jax.random.normal(ks[1], (BATCH, MEM_LEN, D_MODEL), f32)
    offsets = jax.random.randint(ks[2], (BATCH, 1), 0, 4096, dtype=jnp.int32)
    positions = jnp.arange(SEQ, dtype=jnp.int32)[None, :] + offsets
    dt = jnp.exp(jax.random.uniform(ks[3], (DEPTH_2, N_DIRS, DN_HEADS), f32)
                 * (np.log(0.1) - np.log(0.001)) + np.log(0.001))
    return {
        'x': x,
        'mem': mem,
        'positions': positions,
        'g_mix_pre': gain(ks[4], D_MODEL),
        'w_in': dense(ks[5], D_MODEL, IN_COLS_2),
        'conv_w': jax.random.normal(ks[6], (DEPTH_2, DN_CONV, DN_QKV), f32) * DN_CONV ** -0.5,
        'a_log': jnp.log(jax.random.uniform(ks[7], (DEPTH_2, N_DIRS, DN_HEADS), f32, 1.0, 16.0)),
        'dt_bias': dt + jnp.log(-jnp.expm1(-dt)),
        'g_dn_out': gain(ks[8], DN_HEAD_V),
        'attn_sink': 0.5 * jax.random.normal(ks[9], (DEPTH_2, ATTN_HEADS), f32),
        'w_out': dense(ks[10], MIX_WIDTH_2, D_MODEL),
        'g_mix_post': gain(ks[11], D_MODEL),
        'g_cross_pre': gain(ks[12], D_MODEL),
        'g_mem': gain(ks[13], D_MODEL),
        'w_cq': dense(ks[14], D_MODEL, D_MODEL),
        'w_ckv': dense(ks[15], D_MODEL, 2 * D_MODEL),
        'w_co': dense(ks[16], D_MODEL, D_MODEL),
        'g_cross_post': gain(ks[17], D_MODEL),
        'g_ffn_pre': gain(ks[18], D_MODEL),
        'w_gate_up': dense(ks[19], D_MODEL, 2 * D_FF),
        'w_down': dense(ks[20], D_FF, D_MODEL),
        'g_ffn_post': gain(ks[21], D_MODEL),
    }

def second_block(x, mem, positions, g_mix_pre, w_in, conv_w, a_log, dt_bias, g_dn_out, attn_sink,
              w_out, g_mix_post, g_cross_pre, g_mem, w_cq, w_ckv, w_co, g_cross_post,
              g_ffn_pre, w_gate_up, w_down, g_ffn_post):
    b, s = x.shape[0], x.shape[1]
    for l in range(DEPTH_2):
        h = _rms_norm(x, g_mix_pre[l])
        proj = h @ w_in[l]
        aq, ak, av, dqkv, dgate, dalpha, dbeta = jnp.split(proj, IN_SPLITS_2, axis=-1)
        aq = _rope(aq.reshape(b, s, ATTN_HEADS, ATTN_HEAD_DIM), positions)
        ak = _rope(ak.reshape(b, s, ATTN_KV_HEADS, ATTN_HEAD_DIM), positions)
        av = av.reshape(b, s, ATTN_KV_HEADS, ATTN_HEAD_DIM).astype(jnp.float32)
        attn_o = _window_attention(aq, ak, av, attn_sink[l]).astype(x.dtype)
        dn_o = _gated_deltanet(dqkv, dgate, dalpha, dbeta, conv_w[l], a_log[l], dt_bias[l],
                               g_dn_out[l]).astype(x.dtype)
        mix = jnp.concatenate([attn_o, dn_o], axis=-1) @ w_out[l]
        x = x + _rms_norm(mix, g_mix_post[l])
        c = _memory_cross_attention(_rms_norm(x, g_cross_pre[l]), _rms_norm(mem, g_mem[l]),
                                    w_cq[l], w_ckv[l], w_co[l])
        x = x + _rms_norm(c, g_cross_post[l])
        f = _swiglu(_rms_norm(x, g_ffn_pre[l]), w_gate_up[l], w_down[l])
        x = x + _rms_norm(f, g_ffn_post[l])
    return x


def setup_inputs(seed=0):
    out = dict(first_inputs(seed))
    for name, value in second_inputs(seed + 1).items():
        if name != "x":
            out[name + "_2"] = value
    return out


def reference(
    x, c, ctx, c_ctx, norm_g, w_mod, b_mod, w_in, conv_w, q_norm_g, k_norm_g, hgrn_lb,
    hgrn_norm_g, w_out, final_g, mem_2, positions_2, g_mix_pre_2, w_in_2, conv_w_2, a_log_2,
    dt_bias_2, g_dn_out_2, attn_sink_2, w_out_2, g_mix_post_2, g_cross_pre_2, g_mem_2, w_cq_2,
    w_ckv_2, w_co_2, g_cross_post_2, g_ffn_pre_2, w_gate_up_2, w_down_2, g_ffn_post_2,
):
    x = first_block(
        x, c, ctx, c_ctx, norm_g, w_mod, b_mod, w_in, conv_w, q_norm_g, k_norm_g, hgrn_lb,
        hgrn_norm_g, w_out, final_g,
    )
    return second_block(
        x, mem_2, positions_2, g_mix_pre_2, w_in_2, conv_w_2, a_log_2, dt_bias_2, g_dn_out_2,
        attn_sink_2, w_out_2, g_mix_post_2, g_cross_pre_2, g_mem_2, w_cq_2, w_ckv_2, w_co_2,
        g_cross_post_2, g_ffn_pre_2, w_gate_up_2, w_down_2, g_ffn_post_2,
    )


_drawn_inputs = setup_inputs


def setup_inputs(seed=0):
    import zlib

    import numpy as np

    out = dict(_drawn_inputs(seed))
    spreads = {}
    factors = {'ctx': 6.41,
     'q_norm_g': 8.0,
     'k_norm_g': 8.0,
     'hgrn_lb': 4.22,
     'hgrn_norm_g': 2.711,
     'g_dn_out_2': 4.08,
     'attn_sink_2': 41.129,
     'g_mix_post_2': 3.407,
     'g_cross_pre_2': 4.478,
     'g_mem_2': 2.889,
     'g_cross_post_2': 12.92,
     'g_ffn_pre_2': 10.842,
     'g_ffn_post_2': 22.671}
    for name, (base, spread) in spreads.items():
        noise = np.random.default_rng([zlib.crc32(name.encode()), seed]).standard_normal(out[name].shape)
        drawn = base * np.exp(spread * noise) if base else spread * noise
        out[name] = __import__('jax').numpy.asarray(drawn.astype(out[name].dtype))
    for name, factor in factors.items():
        out[name] = (out[name] * factor).astype(out[name].dtype)
    return out
```

```python
from contextlib import ExitStack

import numpy as np

import concourse.bass as bass
from concourse import mybir

F32 = mybir.dt.float32
I32 = mybir.dt.int32
ALU = mybir.AluOpType
ACT = mybir.ActivationFunctionType
AX = mybir.AxisListType

P = 128
D = 1024
KT = D // P
LAT, CTX = 512, 256
TOK = LAT + CTX
CH = 128
NCH, NLAT = TOK // CH, LAT // CH
EPS = 1e-6
DEPTH = 2
HD = 64
RING = 6
CHUNK = KT * P
LEVELS = 7
NEG = -1e30

HQ, HZ, FF, FB, HI, AQ, AK, AV, AZ, FU, FZ, CZ, CB, CC, CV = 0, 2, 4, 6, 8, 10, 12, 13, 14, 16, 18, 20, 22, 24, 26
NPROJ = 28
MIX = [CB, CB + 1, AZ, AZ + 1, HZ, HZ + 1, FZ, FZ + 1]
CTX_TILES_LAST = (FF, FF + 1, FB, FB + 1, HI, HI + 1, AK, AV)

N_MOD = 3 * KT
FOURIER_CHUNKS = {0: NLAT + 1, 1: NLAT}


def chunk_plan():
    at, plan = 0, {}
    for name, n in ([("mod0", N_MOD), ("mod1", N_MOD)]
                    + [x for ly in range(DEPTH) for x in ((f"proj{ly}", NPROJ), (f"dft{ly}", FOURIER_CHUNKS[ly]),
                                                          (f"out{ly}", KT))]
                    + [("ck", KT), ("cv", KT), ("proj_2", 22), ("ab_2", 1), ("out_2", KT), ("cq", KT), ("co", KT),
                       ("gu", 44), ("down", 3 * KT)]):
        plan[name] = at
        at += n
    plan["end"] = at
    return plan


PLAN = chunk_plan()


def table(entries):
    at, out = 0, {}
    for name, n in entries:
        out[name] = (at, at + n)
        at += n
    return out, at


CONST_COLS, N_CONST = table([("ident", P), ("ones", P), ("ones_head", P), ("rot_pair", P), ("cos", LAT), ("sin", LAT),
                             ("dft_ch", 2 * P), ("level0", LEVELS * 64), ("level1", LEVELS * 64)])
CONST2_COLS, N_CONST2 = table([("tri0", P), ("tri1", P), ("inv0", LEVELS * P), ("inv1", LEVELS * P),
                               ("window", 3 * P), ("rot_half", P), ("inv_freq", 1)])
PAR_COLS, N_PAR = table([("c", 2 * KT), ("norm_g", DEPTH * KT), ("b_mod", DEPTH * N_MOD), ("conv_w", DEPTH * 6),
                         ("q_g", DEPTH), ("k_g", DEPTH), ("lb", 8), ("hg_g", DEPTH * 2), ("final_g", KT),
                         ("g_mix_pre", KT), ("conv2", 60), ("a_log", 8), ("dt_bias", 8), ("g_dn", 1), ("sink", 8),
                         ("g_mix_post", KT), ("g_cross_pre", KT), ("g_mem", KT), ("g_cross_post", KT),
                         ("g_ffn_pre", KT), ("g_ffn_post", KT)])


def evacuation_plan():
    at, plan = 0, {}
    for name, n in [("proj0", NPROJ), ("out0", KT), ("proj1", NPROJ), ("out1", KT), ("ck", KT), ("cv", KT),
                    ("proj_2", 22), ("ab_2", 1), ("out_2", KT), ("cq", KT), ("co", KT), ("gu", 44), ("down", KT)]:
        plan[name] = at
        at += n
    return plan


EVAC = evacuation_plan()
N_LAYER0, N_LAYER1, N_FINAL, N_MEM, N_MIX_PRE, N_MIX_POST, N_CROSS_PRE, N_CROSS_POST, N_FFN_PRE, N_FFN_POST = range(10)


def order(back, with_latent=True):
    return [5, 4, 3, 2, 1, 0] if back else [4, 5, 0, 1, 2, 3]


def halves(ap, b):
    return ap.rearrange("p (n two b) -> p n two b", two=2, b=b)


def build(nc, tokens, mem, positions, weights, const_d, const2_d, par_d, out):
    with ExitStack() as ctx:
        def sb(name, shape, dt=F32):
            return ctx.enter_context(nc.sbuf_tensor(name, shape, dt))

        def sem(name):
            return ctx.enter_context(nc.semaphore(name))

        h = sb("h", [P, KT, TOK])
        xn = sb("xn", [P, KT * TOK])
        proj = sb("proj", [P, NPROJ, TOK])
        ring = sb("ring", [P, RING, CHUNK])
        const = sb("const_sb", [P, N_CONST])
        par = sb("par_sb", [P, N_PAR])
        work = sb("work", [P, 8, TOK])
        masked = sb("masked", [P, 4, LEVELS * 64])
        state = sb("state", [P, NCH, HD])
        conv_tmp = sb("conv_tmp", [P, TOK])
        zero = sb("zero", [P, P])
        eps = sb("eps", [P, 1])
        small = sb("small", [P, 640])
        wide_ps = ctx.enter_context(nc.psum_tensor("wide_ps", [P, 2, 1024], F32))
        pair_ps = ctx.enter_context(nc.psum_tensor("pair_ps", [P, 1024], F32))
        duo_ps = ctx.enter_context(nc.psum_tensor("duo_ps", [P, 1024], F32))

        xn_t = xn[:, :].rearrange("p (k t) -> p k t", k=KT)
        cst = {n: const[:, a:b] for n, (a, b) in CONST_COLS.items()}
        prm = {n: par[:, a:b] for n, (a, b) in PAR_COLS.items()}
        c_act = small[:, 0:16]
        mod = small[:, 16:112].rearrange("p (l n s) -> p l n s", l=DEPTH, n=N_MOD)
        mod_scale = small[:, 112:144].rearrange("p (l n s) -> p l n s", l=DEPTH, n=KT)
        lb_e, lb_log, lb_log1m, lb_neg = (small[:, 144 + 4 * n:148 + 4 * n] for n in range(4))
        f_last = small[:, 160:166]
        row_max, neg_max, row_sum, row_inv = (small[:, 168 + 8 * n:176 + 8 * n] for n in range(4))
        sq = work[:, 0:2]
        root = work[:, 2]
        resid = work[:, 3:5]
        lf_b, a_b, e_b, m_b, ke_b, kt_b = (work[:, n] for n in range(6))
        v_tok = work[:, 6:8].rearrange("p j t -> p (j t)").rearrange("p (j c f) -> p j c f", j=2, c=NCH)
        k_tok = kt_b.rearrange("p (c f) -> p c f", c=NCH)
        decay = xn[:, 0:LEVELS * TOK].rearrange("p (l t) -> p l t", l=LEVELS)
        qe_b = xn[:, LEVELS * TOK:KT * TOK]

        setup_landed = sem("setup_landed")
        tokens_landed = sem("tokens_landed")
        landed = [sem(f"chunk_landed{n}") for n in range(RING)]
        chunk_used = sem("chunk_used")
        evacuated = sem("evacuated")
        dve_chain, act_chain, pool_chain = sem("dve_chain"), sem("act_chain"), sem("pool_chain")
        ready = sem("fixed_ready")
        c_ready = sem("c_ready")
        mod_ready = sem("mod_ready")
        lb_ready = sem("lb_ready")
        sq_ready, sq_used = sem("sq_ready"), sem("sq_used")
        root_ready, inv_ready = sem("root_ready"), sem("inv_ready")
        scaled = sem("scaled")
        xn_ready = sem("xn_ready")
        h_ready = sem("h_ready")
        gates_ready = sem("gates_ready")
        vt_ps, vt_ready = sem("vt_ps"), sem("vt_ready")
        hg_soft, hg_lf, hg_k, hg_lb, hg_a = sem("hg_soft"), sem("hg_lf"), sem("hg_k"), sem("hg_lb"), sem("hg_a")
        hg_abs = sem("hg_abs")
        hg_ea, hg_qe, hg_ed0, hg_ed, hg_ke = sem("hg_ea"), sem("hg_qe"), sem("hg_ed0"), sem("hg_ed"), sem("hg_ke")
        hg_kt_ps, hg_kt, hg_u, hg_s = sem("hg_kt_ps"), sem("hg_kt"), sem("hg_u"), sem("hg_s")
        lev_diff, lev_exp, lev_ready = sem("lev_diff"), sem("lev_exp"), sem("lev_ready")
        sc_ps, sc_ready, sc_used = sem("sc_ps"), sem("sc_ready"), sem("sc_used")
        hg_o_ps, hg_qk, hg_diag, hg_o, hg_sq, hg_ms, hg_rt, hg_out = (
            sem(n) for n in ("hg_o_ps", "hg_qk", "hg_diag", "hg_o", "hg_sq", "hg_ms", "hg_rt", "hg_out"))
        qk_sq, qk_ms, qk_rt, qk_norm, qk_rot, qk_ready = (
            sem(n) for n in ("qk_sq", "qk_ms", "qk_rt", "qk_norm", "qk_rot", "qk_ready"))
        at_s, at_max, at_exp, at_p, at_pt_ps, at_pt, at_o_ps, at_out = (
            sem(n) for n in ("at_s", "at_max", "at_exp", "at_p", "at_pt_ps", "at_pt", "at_o_ps", "at_out"))
        ft_a_ps, ft_a, ft_y_ps, ft_out = (sem(n) for n in ("ft_a_ps", "ft_a", "ft_y_ps", "ft_out"))
        conv_out = sem("conv_out")
        final_ready = sem("final_ready")
        stored = sem("stored")

        def width(ly, tile):
            return TOK if ly == 0 or tile in CTX_TILES_LAST else LAT

        def pieces(w):
            return [(0, w)] if w <= LAT else [(0, LAT), (LAT, TOK)]

        def chunk_list(ly):
            return range(NCH) if ly == 0 else range(NLAT)

        def att_units(ly):
            return [(i, r, c) for i in range(2) for r in range(2) for c in chunk_list(ly)]

        def keys_of(c):
            return (0, TOK) if c < NLAT else (LAT, TOK)

        ATT0 = {0: 0, 1: len(att_units(0))}
        SC0 = {u: sum(2 * len(chunk_list(v // 4)) for v in range(u)) for u in range(9)}
        def qk_tiles(ly):
            return [(AQ, width(ly, AQ)), (AQ + 1, width(ly, AQ)), (AK, TOK)]

        def hg_units(ly):
            return [(ly * 4 + 2 * j + d, j, d) for j in range(2) for d in range(2)]

        probs = lambda m: xn[:, TOK * (m % 2):TOK * (m % 2) + TOK]
        probs_t = lambda m: xn[:, TOK * (2 + m % 2):TOK * (3 + m % 2)]
        ft_buf = xn[:, 4 * TOK:4 * TOK + 2048].rearrange("p (t j f) -> p t j f", t=NLAT, j=2)

        def ft_steps(ly):
            return [(tt, j) for s in (0, 1)[:2 - ly] for tt in range((NLAT, 2)[s]) for j in range(2)]

        FT0 = {0: 0, 1: 12}


        masked_2 = masked[:, :, :].rearrange("p n t -> p (n t)")
        flat = proj[:, :, :].rearrange("p n t -> p (n t)")
        spot = [0]

        def place(n):
            spot[0] += n
            return flat[:, spot[0] - n:spot[0]]

        x_2 = h[:, :, 0:LAT]
        mem_x = h[:, :, LAT:TOK]
        tile_2 = place(22 * LAT).rearrange("p (n t) -> p n t", t=LAT)
        const2 = place(N_CONST2)
        cst2 = {n: const2[:, a:b] for n, (a, b) in CONST2_COLS.items()}
        key_c = place(KT * CTX).rearrange("p (k t) -> p k t", k=KT)
        val_c = place(2 * D).rearrange("p (t n) -> p t n", t=2)
        cos_2, sin_2 = place(LAT), place(LAT)
        o_dn = place(4 * LAT).rearrange("p (h t) -> p h t", h=4)
        q_c, o_c = tile_2[:, 0:KT, :], tile_2[:, KT:2 * KT, :]
        y_2 = xn_t[:, :, 0:LAT]
        pos_i = conv_tmp[:, 0:LAT].bitcast(I32)
        conv_y = masked_2[:, 0:1024].rearrange("p (n t) -> p n t", n=2)
        half_pi = small[:, 210:211]
        row_max2, neg_max2, row_sum2, row_inv2, sink_e = (small[:, 212 + 4 * n:216 + 4 * n] for n in range(5))
        ab = small[:, 240:304].rearrange("p (c n) -> p c n", c=NLAT)
        g_tok, g_soft, beta, g_cum, g_exp, beta_g = (
            small[:, 304 + 32 * n:336 + 32 * n].rearrange("p (c n) -> p c n", c=NLAT) for n in range(6))
        a_exp = small[:, 496:504]
        g_end = small[:, 504:512].rearrange("p (d n) -> p d n", d=2)
        s_decay = small[:, 512:520].rearrange("p (d n) -> p d n", d=2)
        dn_store = [xn[:, :].rearrange("p (n h t) -> p n h t", n=12, h=4),
                    work[:, :, :].rearrange("p n t -> p (n t)").rearrange("p (n h t) -> p n h t", n=12, h=4)]
        XT, T, R, Y, XM, QK, KBG, VB, KG, WT, VN, QG = range(12)
        s_dn = masked_2[:, 0:1024].rearrange("p (d h v) -> p d h v", d=2, h=4)

        def dn(d, name):
            return dn_store[d][:, name]

        def dn_bank(d, n):
            ps = (wide_ps[:, n // 2, 512 * (n % 2):512 * (n % 2) + 512] if d == 0
                  else (pair_ps, duo_ps)[n // 2][:, 512 * (n % 2):512 * (n % 2) + 512])
            return ps.rearrange("p (h t) -> p h t", h=4)

        def chunk_at(d, s):
            return s if d == 0 else NLAT - 1 - s

        AQ2, AK2, AV2, DQ2, DK2, DV2, DG2 = 0, 4, 5, 6, 10, 14, 18
        MIX2 = [0, 1, 2, 3, DG2, DG2 + 1, DG2 + 2, DG2 + 3]
        WIN = [(i, r, c) for i in range(4) for r in range(2) for c in range(NLAT)]
        CROSS = [(hd, c) for hd in range(4) for c in range(NLAT)]

        def window_keys(c):
            a, b = max(c - 1, 0), min(c + 2, NLAT)
            return a * P, b * P, (a - c + 1) * P, (b - c + 1) * P

        const2_landed, mem_landed, pos_landed = sem("const2_landed"), sem("mem_landed"), sem("pos_landed")
        x_ready = sem("x_ready")
        rope_arg, rope_table = sem("rope_arg"), sem("rope_table")
        cv_sum, cv_ready, dgate_ready = sem("cv_sum"), sem("cv_ready"), sem("dgate_ready")
        l2_sq, l2_ss, l2_rt, l2_ready = sem("l2_sq"), sem("l2_ss"), sem("l2_rt"), sem("l2_ready")
        rp_rot, rp_ready = sem("rp_rot"), sem("rp_ready")
        v2_ps, v2_ready = sem("v2_ps"), sem("v2_ready")
        w_s, w_max, w_exp, w_p, w_pt_ps, w_pt, w_o_ps, w_out_s = (
            sem(n) for n in ("w_s", "w_max", "w_exp", "w_p", "w_pt_ps", "w_pt", "w_o_ps", "w_out"))
        g_x, g_l, g_ready, g_ps, g_c, g_e, g_b = (sem(n) for n in ("g_x", "g_l", "g_ready", "g_ps", "g_c", "g_e", "g_b"))
        dn_a, dn_diff, dn_exp, dn_x, dn_row, dn_tok_ps, dn_tok = (
            sem(n) for n in ("dn_a", "dn_diff", "dn_exp", "dn_x", "dn_row", "dn_tok_ps", "dn_tok"))
        dn_qg, dn_xm, dn_y_ps, dn_y, dn_z_ps, dn_t = (sem(n) for n in ("dn_qg", "dn_xm", "dn_y_ps", "dn_y", "dn_z_ps", "dn_t"))
        dn_w_ps, dn_w, dn_v_ps, dn_v, dn_o_ps, dn_s = (sem(n) for n in ("dn_w_ps", "dn_w", "dn_v_ps", "dn_v", "dn_o_ps", "dn_s"))
        do_sq, do_ss, do_rt, do_out = (sem(n) for n in ("do_sq", "do_ss", "do_rt", "do_out"))
        c_s, c_max, c_exp, c_p, c_pt_ps, c_pt, c_o_ps, c_out = (
            sem(n) for n in ("c_s", "c_max", "c_exp", "c_p", "c_pt_ps", "c_pt", "c_o_ps", "c_out"))
        ffn_ready = sem("ffn_ready")

        block = ctx.enter_context(nc.Block())

        @block.sync
        def _(sp):
            sp.dma_start(par[:, :], par_d).then_inc(setup_landed, 16)
            sp.dma_start(const[:, :], const_d).then_inc(setup_landed, 16)
            sp.dma_start(h[:, :, :], tokens).then_inc(tokens_landed, 16)
            for c in range(RING):
                sp.dma_start(ring[:, c, :], weights[c]).then_inc(landed[c], 16)
            turns = (PLAN["end"] - RING) // RING
            with sp.Fori(0, turns) as turn:
                for s in range(RING):
                    sp.wait_ge(chunk_used, turn * RING + (s + 1))
                    sp.dma_start(ring[:, s, :], weights[turn * RING + (RING + s)]).then_inc(landed[s], 16)
            for c in range((turns + 1) * RING, PLAN["end"]):
                sp.wait_ge(chunk_used, c - RING + 1)
                sp.dma_start(ring[:, c % RING, :], weights[c]).then_inc(landed[c % RING], 16)
            sp.wait_ge(final_ready, KT)
            sp.dma_start(out, h[:, :, 0:LAT]).then_inc(stored, 16)
            sp.wait_ge(stored, 16)

        @block.gpsimd
        def _(pool):
            def link(ins):
                pool_count[0] += 1
                ins.then_inc(pool_chain, 1)
                pool.wait_ge(pool_chain, pool_count[0])

            pool_count = [0]
            pool.memset(zero[:, :], 0.0).then_inc(ready, 1)
            pool.memset(eps[:, :], EPS).then_inc(ready, 1)

            def conv(ly):
                w = width(ly, CB)
                taps = prm["conv_w"].rearrange("p (l t j) -> p l t j", l=DEPTH, t=3)
                for j in range(2):
                    cb, cc, cv, cz, tmp = proj[:, CB + j, 0:w], proj[:, CC + j, 0:w], proj[:, CV + j, 0:w], proj[:, CZ + j, 0:w], conv_tmp[:, 0:w]
                    pool.wait_ge(evacuated, EVAC[f"proj{ly}"] + NPROJ)
                    pool.wait_ge(gates_ready, 2 * ly + 2)
                    link(pool.tensor_tensor(cc, cc, cv, ALU.mult))
                    link(pool.tensor_scalar(cv, cc, taps[:, ly, 1, j:j + 1], None, ALU.mult))
                    for tap, to, frm in ((0, 1, 0), (2, 0, 1)):
                        link(pool.tensor_scalar(tmp, cc, taps[:, ly, tap, j:j + 1], None, ALU.mult))
                        for a, b in pieces(w):
                            n = b - a - 1
                            link(pool.tensor_tensor(cv[:, a + to:a + to + n], cv[:, a + to:a + to + n],
                                                    tmp[:, a + frm:a + frm + n], ALU.add))
                    link(pool.tensor_tensor(cv, cv, cb, ALU.mult))
                    pool.tensor_tensor(cb, cv, cz, ALU.mult).then_inc(conv_out, 1)

            def level_differences(u, d, ly):
                w = TOK if ly == 0 else LAT
                pool.wait_ge(hg_a, u + 1)
                if u:
                    pool.wait_ge(sc_ps, SC0[u])
                for l in range(LEVELS):
                    b = 1 << l
                    a, o = halves(a_b[:, 0:w], b), halves(decay[:, l, 0:w], b)
                    q, k = (1, 0) if d == 0 else (0, 1)
                    ref = a[:, :, 0, b - 1:b] if d == 0 else a[:, :, 1, 0:1]
                    ref = ref.broadcast_to([P, w // (2 * b), b])
                    pool.tensor_tensor(o[:, :, q, :], a[:, :, q, :], ref, ALU.subtract).then_inc(lev_diff, 1)
                    pool.tensor_tensor(o[:, :, k, :], ref, a[:, :, k, :], ALU.subtract).then_inc(lev_diff, 1)

            def diagonal(ly, j):
                w = width(ly, HQ)
                u = ly * 4 + 2 * j + 1
                pool.wait_ge(lev_ready, LEVELS * (u + 1))
                pool.wait_ge(hg_ke, u + 1)
                link(pool.tensor_tensor(proj[:, FF + j, 0:w], proj[:, FF + j, 0:w], proj[:, FB + j, 0:w], ALU.add))
                pool.tensor_tensor(proj[:, FF + j, 0:w], proj[:, FF + j, 0:w], proj[:, HQ + j, 0:w], ALU.mult).then_inc(hg_qk, 1)

            for ly in range(DEPTH):
                for u, j, d in hg_units(ly):
                    level_differences(u, d, ly)
                    if d == 1:
                        diagonal(ly, j)
                conv(ly)
            for s in range(NLAT):
                for l in range(LEVELS):
                    for d in range(2):
                        g, c = 2 * s + d, chunk_at(d, s)
                        if l == 0:
                            pool.wait_ge(dn_x, 2 * g + 2)
                        elif l == 1:
                            pool.wait_ge(dn_t, 2 * (LEVELS * s) + d + 1)
                        else:
                            pool.wait_ge(dn_y_ps, 2 * (6 * s + l - 2) + d + 1)
                        mask = cst2[f"inv{d}"][:, l * P:(l + 1) * P].unsqueeze(1).broadcast_to([P, 4, CH])
                        pool.tensor_tensor(dn(d, XM), dn(d, XT), mask, ALU.mult).then_inc(dn_xm, 1)
                        if l == 0:
                            q = tile_2[:, DQ2:DQ2 + 4, c * CH:(c + 1) * CH]
                            pool.tensor_tensor(dn(d, QG), dn(d, QG), q, ALU.mult).then_inc(dn_qg, 1)
                            pool.tensor_tensor(dn(d, QK), dn(d, QK), cst2[f"tri{d}"].unsqueeze(1).broadcast_to([P, 4, CH]),
                                               ALU.mult).then_inc(dn_qg, 1)

        @block.scalar
        def _(act):
            act_count = [0]

            def link(ins):
                act_count[0] += 1
                ins.then_inc(act_chain, 1)
                act.wait_ge(act_chain, act_count[0])

            def norm_root(n, src, w, source_ready):
                for k in range(KT):
                    source_ready(k)
                    if 8 * n + k >= 2:
                        act.wait_ge(sq_used, 8 * n + k - 1)
                    act.activation(sq[:, k % 2, 0:w], src(k), ACT.Square).then_inc(sq_ready, 1)
                act.wait_ge(sq_used, 8 * (n + 1))
                if n:
                    act.wait_ge(scaled, 8 * n)
                act.activation(root[:, 0:w], pair_ps[:, 0:w], ACT.Sqrt, bias=eps[:, 0:1],
                               scale=1.0 / D).then_inc(root_ready, 1)

            def evacuate(stage, tile, chunks, w, dst, func=ACT.Copy):
                g = EVAC[stage] + tile
                act.wait_ge(chunk_used, chunks)
                act.activation(dst, wide_ps[:, g % 2, 0:w], func).then_inc(evacuated, 1)
                act.wait_ge(evacuated, g + 1)

            def modulate(ly):
                act.wait_ge(mod_ready, 2 * (ly + 1))
                for k in range(KT):
                    act.wait_ge(scaled, 8 * ly + k + 1)
                    for s, (a, b) in enumerate(pieces(TOK)):
                        act.activation(xn_t[:, k, a:b], xn_t[:, k, a:b], ACT.Identity, bias=mod[:, ly, k, s:s + 1],
                                       scale=mod_scale[:, ly, k, s:s + 1]).then_inc(xn_ready, 1)

            def lower_bounds():
                act.wait_ge(lb_ready, 1)
                link(act.activation(lb_log, lb_e, ACT.Abs))
                link(act.activation(lb_log, lb_log, ACT.Exp, scale=-1.0))
                act.activation(lb_log, lb_log, ACT.Ln, bias=1.0).then_inc(lb_ready, 1)

            def hgrn_unit(ly, u, j, d):
                z = proj[:, (FF, FB)[d] + j, :]
                if u % 4:
                    act.wait_ge(hg_ke, u)
                link(act.activation(e_b, z, ACT.Abs))
                link(act.activation(e_b, e_b, ACT.Exp, scale=-1.0))
                act.activation(e_b, e_b, ACT.Ln, bias=1.0).then_inc(hg_soft, 1)
                act.wait_ge(hg_lf, u + 1)
                bias = 0.0 if ly == 0 else lb_log1m[:, 2 * d + j:2 * d + j + 1]
                act.activation(z, m_b, ACT.Exp, bias=bias, scale=-1.0).then_inc(hg_k, 1)
                if ly == 1:
                    act.wait_ge(hg_lb, 2 * (u - 4) + 1)
                    link(act.activation(e_b, lf_b, ACT.Abs, bias=lb_neg[:, 2 * d + j:2 * d + j + 1]))
                    link(act.activation(e_b, e_b, ACT.Exp, scale=-1.0))
                    act.activation(e_b, e_b, ACT.Ln, bias=1.0).then_inc(hg_abs, 1)
                act.wait_ge(hg_a, u + 1)
                act.wait_ge(hg_k, u + 1)
                act.activation(m_b, a_b, ACT.Exp).then_inc(hg_ea, 1)
                last = a_b.rearrange("p (c t) -> p c t", t=CH)[:, :, CH - 1 if d == 0 else 0]
                act.activation(f_last, last, ACT.Exp).then_inc(hg_ea, 1)
                act.wait_ge(hg_ed0, u + 1)
                act.activation(e_b, e_b, ACT.Exp).then_inc(hg_ed, 1)
                w = TOK if ly == 0 else LAT
                for l in range(LEVELS):
                    act.wait_ge(lev_diff, 2 * (LEVELS * u + l + 1))
                    act.activation(decay[:, l, 0:w], decay[:, l, 0:w], ACT.Exp).then_inc(lev_exp, 1)
                act.wait_ge(hg_kt_ps, u + 1)
                act.activation(kt_b, duo_ps[:, 0:TOK], ACT.Copy).then_inc(hg_kt, 1)

            def hgrn_norm(ly, j):
                n = 2 * ly + j
                w = width(ly, HQ)
                act.wait_ge(hg_o, n + 1)
                act.activation(m_b[:, 0:w], ke_b[:, 0:w], ACT.Square).then_inc(hg_sq, 1)
                act.wait_ge(hg_ms, n + 1)
                act.activation(e_b[:, 0:w], duo_ps[:, 0:w], ACT.Sqrt, bias=eps[:, 0:1], scale=1.0 / HD).then_inc(hg_rt, 1)

            def attention(ly):
                for n, (t, w) in enumerate(qk_tiles(ly)):
                    m = 3 * ly + n
                    if n:
                        act.wait_ge(qk_norm, m)
                    else:
                        act.wait_ge(hg_out, 2 * ly + 2)
                    act.activation(e_b[:, 0:w], proj[:, t, 0:w], ACT.Square).then_inc(qk_sq, 1)
                    act.wait_ge(qk_ms, m + 1)
                    act.activation(m_b[:, 0:w], pair_ps[:, 0:w], ACT.Sqrt, bias=eps[:, 0:1], scale=1.0 / HD).then_inc(qk_rt, 1)
                act.wait_ge(vt_ps, 3 * ly + 3)
                act.activation(v_tok[:, 0], pair_ps[:, 0:TOK].rearrange("p (c f) -> p c f", c=NCH), ACT.Copy).then_inc(vt_ready, 1)
                units = att_units(ly)
                for n, (i, r, c) in enumerate(units):
                    m = ATT0[ly] + n
                    a, b = keys_of(c)
                    act.wait_ge(at_max, m + 1)
                    act.activation(probs(m)[:, a:b], wide_ps[:, m % 2, a:b], ACT.Exp, bias=neg_max[:, m % 4:m % 4 + 1],
                                   scale=HD ** -0.5, accum_out=row_sum[:, m % 4:m % 4 + 1]).then_inc(at_exp, 1)
                    if n:
                        probs_transposed(m - 1, keys_of(units[n - 1][2]))
                probs_transposed(ATT0[ly] + len(units) - 1, keys_of(units[-1][2]))

            def probs_transposed(m, keys):
                a, b = keys
                act.wait_ge(at_pt_ps, m + 1)
                if m >= 2:
                    act.wait_ge(at_o_ps, m - 1)
                act.activation(probs_t(m)[:, a:b], pair_ps[:, a:b], ACT.Copy).then_inc(at_pt, 1)

            def fourier(ly):
                for n, (tt, j) in enumerate(ft_steps(ly)):
                    m = FT0[ly] + n
                    act.wait_ge(ft_a_ps, m + 1)
                    act.activation(ft_buf[:, tt, j, :], pair_ps[:, 512 * (m % 2):512 * (m % 2) + 256], ACT.Copy).then_inc(ft_a, 1)

            def output(ly):
                for n in range(KT):
                    g = EVAC[f"out{ly}"] + n
                    act.wait_ge(chunk_used, PLAN[f"out{ly}"] + n + 1)
                    if 8 * ly + n >= 2:
                        act.wait_ge(h_ready, 8 * ly + n - 1)
                    w = width(ly, HQ)
                    for s, (a, b) in enumerate(pieces(w)):
                        ins = act.activation(resid[:, n % 2, a:b], wide_ps[:, g % 2, a:b], ACT.Copy,
                                             scale=mod[:, ly, 2 * KT + n, s:s + 1])
                        if b == w:
                            ins.then_inc(evacuated, 1)

            act.wait_ge(setup_landed, 32)
            act.wait_ge(ready, 2)
            act.activation(c_act, prm["c"], ACT.Silu).then_inc(c_ready, 1)
            lower_bounds()
            for ly in range(DEPTH):
                w = TOK
                norm_root(ly, lambda k: h[:, k, :], TOK,
                          (lambda k: act.wait_ge(tokens_landed, 16)) if ly == 0 else (lambda k: act.wait_ge(h_ready, k + 1)))
                modulate(ly)
                for t in range(NPROJ):
                    evacuate(f"proj{ly}", t, PLAN[f"proj{ly}"] + t + 1, width(ly, t), proj[:, t, 0:width(ly, t)])
                    if t == HZ + 1:
                        act.activation(proj[:, HQ:HZ + 2, 0:width(ly, HQ)], proj[:, HQ:HZ + 2, 0:width(ly, HQ)],
                                       ACT.Silu).then_inc(gates_ready, 1)
                wl = width(ly, AZ)
                link(act.activation(proj[:, AZ:AZ + 2, 0:wl], proj[:, AZ:AZ + 2, 0:wl], ACT.Silu))
                act.activation(proj[:, FZ:CZ + 2, 0:wl], proj[:, FZ:CZ + 2, 0:wl], ACT.Silu).then_inc(gates_ready, 1)
                act.wait_ge(gates_ready, 2 * ly + 2)
                for j in range(2):
                    act.wait_ge(vt_ps, 3 * ly + j + 1)
                    act.activation(v_tok[:, j], duo_ps[:, 0:TOK].rearrange("p (c f) -> p c f", c=NCH), ACT.Copy).then_inc(vt_ready, 1)
                for u, j, d in hg_units(ly):
                    if d == 0 and j == 1:
                        act.wait_ge(hg_out, 2 * ly + j)
                    hgrn_unit(ly, u, j, d)
                    if d == 1:
                        hgrn_norm(ly, j)
                attention(ly)
                fourier(ly)
                output(ly)
            act.wait_ge(scaled, 16)
            act.dma_start(mem_x, mem).then_inc(mem_landed, 16)
            act.wait_ge(chunk_used, PLAN["out1"] + KT)
            act.dma_start(const2, const2_d).then_inc(const2_landed, 16)
            act.wait_ge(conv_out, 4)
            act.dma_start(pos_i, positions).then_inc(pos_landed, 16)
            norm_root(N_FINAL, lambda k: h[:, k, 0:LAT], LAT, lambda k: act.wait_ge(h_ready, KT + k + 1))
            norm_root(N_MEM, lambda k: mem_x[:, k, :], CTX, lambda k: act.wait_ge(mem_landed, 16))
            norm_root(N_MIX_PRE, lambda k: x_2[:, k, :], LAT, lambda k: act.wait_ge(scaled, 8 * N_FINAL + k + 1))
            for n in range(KT):
                evacuate("ck", n, PLAN["ck"] + n + 1, CTX, key_c[:, n, :])
            for n in range(KT):
                g = EVAC["cv"] + n
                act.wait_ge(chunk_used, PLAN["cv"] + n + 1)
                act.activation(val_c[:, :, n * P:(n + 1) * P], wide_ps[:, g % 2, 0:2 * P].rearrange("p (t n) -> p t n", t=2),
                               ACT.Copy).then_inc(evacuated, 1)
            act.wait_ge(rope_arg, 2)
            link(act.activation(cos_2, sin_2, ACT.Abs))
            link(act.activation(cos_2, cos_2, ACT.Sin, bias=half_pi, scale=-1.0))
            act.activation(sin_2, sin_2, ACT.Sin).then_inc(rope_table, 1)
            for t in range(22):
                evacuate("proj_2", t, PLAN["proj_2"] + t + 1, LAT, tile_2[:, t, :])
                q = t - DQ2 - 2
                if 0 <= q < 12:
                    act.wait_ge(cv_sum, q + 1)
                    act.activation(tile_2[:, DQ2 + q, :], conv_y[:, q % 2, :], ACT.Silu).then_inc(cv_ready, 1)
            evacuate("ab_2", 0, PLAN["ab_2"] + 1, 64, small[:, 240:304])
            act.wait_ge(evacuated, EVAC["ab_2"] + 1)
            act.activation(tile_2[:, DG2:DG2 + 4, :], tile_2[:, DG2:DG2 + 4, :], ACT.Silu).then_inc(dgate_ready, 1)
            act.wait_ge(g_x, 1)
            act.activation(beta, ab[:, :, 8:16], ACT.Sigmoid).then_inc(g_l, 1)
            link(act.activation(g_soft, g_tok, ACT.Abs))
            link(act.activation(g_soft, g_soft, ACT.Exp, scale=-1.0))
            act.activation(g_soft, g_soft, ACT.Ln, bias=1.0).then_inc(g_l, 1)
            act.activation(a_exp, prm["a_log"], ACT.Exp).then_inc(g_l, 1)
            act.wait_ge(g_c, 2)
            act.activation(g_exp, g_cum, ACT.Exp).then_inc(g_e, 1)
            for n in range(8):
                act.wait_ge(cv_ready, n + 1)
                if n >= 2:
                    act.wait_ge(l2_ss, n - 1)
                act.activation(sq[:, n % 2, 0:LAT], tile_2[:, DQ2 + n, :], ACT.Square).then_inc(l2_sq, 1)
                act.wait_ge(l2_ss, n + 1)
                if n >= 2:
                    act.wait_ge(l2_ready, n - 1)
                act.activation(work[:, 2 + n % 2, 0:LAT], pair_ps[:, 512 * (n % 2):512 * (n % 2) + LAT], ACT.Sqrt,
                               bias=eps[:, 0:1]).then_inc(l2_rt, 1)
            act.wait_ge(v2_ps, 1)
            act.activation(v_tok[:, 0, 0:NLAT, :], duo_ps[:, 0:LAT].rearrange("p (c f) -> p c f", c=NLAT), ACT.Copy).then_inc(v2_ready, 1)

            def window_transposed(m):
                a, b, _, _ = window_keys(WIN[m][2])
                act.wait_ge(w_pt_ps, m + 1)
                if m >= 2:
                    act.wait_ge(w_o_ps, m - 1)
                act.activation(probs_t(m)[:, 0:b - a], pair_ps[:, 0:b - a], ACT.Copy).then_inc(w_pt, 1)

            for m, (i, r, c) in enumerate(WIN):
                a, b, _, _ = window_keys(c)
                one = slice(m % 4, m % 4 + 1)
                act.wait_ge(w_max, m + 1)
                p = probs(m)[:, 0:b - a]
                act.activation(p, p, ACT.Exp, bias=neg_max2[:, one], accum_out=row_sum2[:, one]).then_inc(w_exp, 1)
                act.activation(sink_e[:, one], prm["sink"][:, i + 4 * r:i + 4 * r + 1], ACT.Exp,
                               bias=neg_max2[:, one]).then_inc(w_exp, 1)
                if m:
                    window_transposed(m - 1)
            window_transposed(len(WIN) - 1)
            for s in range(NLAT):
                for d in range(2):
                    g = 2 * s + d
                    last = CH - 1 if d == 0 else 0
                    act.wait_ge(dn_diff, g + 1)
                    act.activation(dn(d, XM), dn(d, XM), ACT.Exp).then_inc(dn_exp, 1)
                    act.activation(g_end[:, d], g_end[:, d], ACT.Exp).then_inc(dn_exp, 1)
                    act.activation(dn(d, QG), dn_bank(d, 0), ACT.Exp).then_inc(dn_exp, 1)
                    act.activation(s_decay[:, d], dn_bank(d, 0)[:, :, last], ACT.Exp).then_inc(dn_exp, 1)
                for l in range(1, LEVELS):
                    for d in range(2):
                        at = 2 * (6 * s + l - 1) + d
                        act.wait_ge(dn_y_ps, at + 1)
                        act.activation(dn(d, Y), dn_bank(d, 3), ACT.Copy).then_inc(dn_y, 1)
                for d in range(2):
                    act.wait_ge(dn_w_ps, 2 * s + d + 1)
                    act.activation(dn(d, WT), dn_bank(d, 0), ACT.Copy, scale=-1.0).then_inc(dn_w, 1)
                for d in range(2):
                    act.wait_ge(dn_v_ps, 2 * s + d + 1)
                    act.activation(dn(d, VN), dn_bank(d, 1), ACT.Copy).then_inc(dn_v, 1)
            act.wait_ge(dn_s, 2 * NLAT)
            for n in range(4):
                if n >= 2:
                    act.wait_ge(do_ss, n - 1)
                act.activation(sq[:, n % 2, 0:LAT], o_dn[:, n, :], ACT.Square).then_inc(do_sq, 1)
                act.wait_ge(do_ss, n + 1)
                if n >= 2:
                    act.wait_ge(do_out, n - 1)
                act.activation(work[:, 2 + n % 2, 0:LAT], pair_ps[:, 512 * (n % 2):512 * (n % 2) + LAT], ACT.Sqrt,
                               bias=eps[:, 0:1], scale=1.0 / P).then_inc(do_rt, 1)

            def closed(stage, n, chunks):
                for t in range(KT):
                    evacuate(stage, t, PLAN[stage] + chunks * (t + 1), LAT, y_2[:, t, :])
                norm_root(n, lambda k: y_2[:, k, :], LAT, lambda k: None)

            closed("out_2", N_MIX_POST, 1)
            norm_root(N_CROSS_PRE, lambda k: x_2[:, k, :], LAT, lambda k: act.wait_ge(x_ready, k + 1))
            for t in range(KT):
                evacuate("cq", t, PLAN["cq"] + t + 1, LAT, q_c[:, t, :])
            for m in range(len(CROSS) + 1):
                if m < len(CROSS):
                    one = slice(m % 4, m % 4 + 1)
                    act.wait_ge(c_max, m + 1)
                    act.activation(probs(m)[:, 0:CTX], wide_ps[:, m % 2, 0:CTX], ACT.Exp, bias=neg_max2[:, one],
                                   scale=256 ** -0.5, accum_out=row_sum2[:, one]).then_inc(c_exp, 1)
                if m:
                    act.wait_ge(c_pt_ps, m)
                    if m >= 3:
                        act.wait_ge(c_o_ps, m - 2)
                    act.activation(probs_t(m - 1)[:, 0:CTX], pair_ps[:, 0:CTX], ACT.Copy).then_inc(c_pt, 1)
            closed("co", N_CROSS_POST, 1)
            norm_root(N_FFN_PRE, lambda k: x_2[:, k, :], LAT, lambda k: act.wait_ge(x_ready, KT + k + 1))
            for t in range(44):
                if t % 2 == 0:
                    evacuate("gu", t, PLAN["gu"] + t + 1, LAT, tile_2[:, t // 2, :], ACT.Silu)
                else:
                    if t >= 5:
                        act.wait_ge(ffn_ready, t // 2 - 1)
                    evacuate("gu", t, PLAN["gu"] + t + 1, LAT, resid[:, t // 2 % 2, 0:LAT])
            closed("down", N_FFN_POST, 3)

        @block.vector
        def _(dve):
            dve_count = [0]

            def link(ins):
                dve_count[0] += 1
                ins.then_inc(dve_chain, 1)
                dve.wait_ge(dve_chain, dve_count[0])

            def reciprocal_root(n, w):
                dve.wait_ge(root_ready, n + 1)
                dve.reciprocal(root[:, 0:w], root[:, 0:w]).then_inc(inv_ready, 1)
                dve.wait_ge(inv_ready, n + 1)

            def modulation(ly):
                dve.wait_ge(chunk_used, PLAN[f"mod{ly}"] + N_MOD)
                bias = prm["b_mod"][:, ly * N_MOD:(ly + 1) * N_MOD].unsqueeze(2).broadcast_to([P, N_MOD, 2])
                dve.tensor_tensor(mod[:, ly], duo_ps[:, 512 * (1 - ly):512 * (1 - ly) + 48].rearrange("p (n s) -> p n s", s=2), bias,
                                  ALU.add).then_inc(mod_ready, 1)
                dve.wait_ge(mod_ready, 2 * ly + 1)
                gain = prm["norm_g"][:, ly * KT:(ly + 1) * KT].unsqueeze(2).broadcast_to([P, KT, 2])
                dve.scalar_tensor_tensor(out=mod_scale[:, ly], in0=mod[:, ly, KT:2 * KT], scalar=1.0, in1=gain, op0=ALU.add,
                                         op1=ALU.mult).then_inc(mod_ready, 1)

            def lower_bounds():
                dve.wait_ge(setup_landed, 32)
                dve.tensor_tensor(lb_e, prm["lb"][:, 4:8], prm["lb"][:, 0:4], ALU.subtract).then_inc(lb_ready, 1)
                dve.wait_ge(lb_ready, 2)
                link(dve.scalar_tensor_tensor(out=lb_log1m, in0=lb_e, scalar=0.0, in1=lb_log, op0=ALU.max, op1=ALU.add))
                link(dve.tensor_scalar(lb_log1m, lb_log1m, -1.0, None, ALU.mult))
                link(dve.scalar_tensor_tensor(out=lb_log, in0=lb_e, scalar=0.0, in1=lb_log, op0=ALU.min, op1=ALU.subtract))
                dve.tensor_scalar(lb_neg, lb_log, -1.0, None, ALU.mult).then_inc(lb_ready, 1)
                dve.wait_ge(lb_ready, 3)

            def hgrn_unit(ly, u, j, d):
                z = proj[:, (FF, FB)[d] + j, :]
                q = proj[:, HQ + j, 0:width(ly, HQ)]
                one = 2 * d + j
                dve.wait_ge(hg_soft, u + 1)
                link(dve.scalar_tensor_tensor(out=lf_b, in0=z, scalar=0.0, in1=e_b, op0=ALU.min, op1=ALU.subtract))
                dve.scalar_tensor_tensor(out=m_b, in0=z, scalar=0.0, in1=e_b, op0=ALU.max, op1=ALU.add).then_inc(hg_lf, 1)
                if ly == 1:
                    dve.wait_ge(hg_lf, u + 1)
                    dve.tensor_scalar(lf_b, lf_b, lb_log1m[:, one:one + 1], None, ALU.add).then_inc(hg_lb, 1)
                    dve.wait_ge(hg_abs, u - 3)
                    dve.scalar_tensor_tensor(out=lf_b, in0=lf_b, scalar=lb_log[:, one:one + 1], in1=e_b, op0=ALU.max,
                                             op1=ALU.add).then_inc(hg_lb, 1)
                    dve.wait_ge(hg_lb, 2 * (u - 4) + 2)
                if u:
                    dve.wait_ge(lev_diff, 2 * LEVELS * u)
                for c in range(NCH):
                    run = slice(c * CH, (c + 1) * CH)
                    src, dst = lf_b[:, run], a_b[:, run]
                    if d:
                        src, dst = src[:, ::-1], dst[:, ::-1]
                    ins = dve.tensor_tensor_scan(dst, cst["ones"], src, 0.0, ALU.mult, ALU.add)
                    if c < NCH - 1:
                        link(ins)
                    else:
                        ins.then_inc(hg_a, 1)
                dve.wait_ge(hg_a, u + 1)
                a_c = a_b.rearrange("p (c t) -> p c t", t=CH)
                last = a_c[:, :, CH - 1:CH] if d == 0 else a_c[:, :, 0:1]
                dve.tensor_tensor(e_b.rearrange("p (c t) -> p c t", t=CH), last.broadcast_to([P, NCH, CH]), a_c,
                                  ALU.subtract).then_inc(hg_ed0, 1)
                dve.wait_ge(hg_ea, 2 * u + 2)
                w = width(ly, HQ)
                if u:
                    dve.wait_ge(hg_o_ps, u)
                dve.tensor_tensor(qe_b[:, 0:w], q, m_b[:, 0:w], ALU.mult).then_inc(hg_qe, 1)
                dve.wait_ge(hg_ed, u + 1)
                dve.tensor_tensor(ke_b, z, e_b, ALU.mult).then_inc(hg_ke, 1)
                q_side, k_side = (1, 0) if d == 0 else (0, 1)
                for l in range(LEVELS):
                    b = 1 << l
                    o, kk, qq = halves(decay[:, l, 0:w], b), halves(z[:, 0:w], b), halves(q, b)
                    dve.wait_ge(lev_exp, LEVELS * u + l + 1)
                    link(dve.tensor_tensor(o[:, :, q_side, :], o[:, :, q_side, :], qq[:, :, q_side, :], ALU.mult))
                    dve.tensor_tensor(o[:, :, k_side, :], o[:, :, k_side, :], kk[:, :, k_side, :], ALU.mult).then_inc(lev_ready, 1)
                dve.wait_ge(hg_u, u + 1)
                seq = order(d)
                link(dve.memset(state[:, seq[0], :], 0.0))
                for n in range(1, NCH):
                    was, now = seq[n - 1], seq[n]
                    for r in range(2):
                        rows = slice(64 * r, 64 * r + 64)
                        ins = dve.scalar_tensor_tensor(
                            out=state[rows, now, :], in0=state[rows, was, :], scalar=f_last[rows, was:was + 1],
                            in1=duo_ps[rows, was * CH + 64 * r:was * CH + 64 * r + 64], op0=ALU.mult, op1=ALU.add)
                        if n == NCH - 1 and r == 1:
                            ins.then_inc(hg_s, 1)
                        else:
                            link(ins)
                level = cst[f"level{d}"]
                for n in range(2 * len(chunk_list(ly))):
                    m = SC0[u] + n
                    dve.wait_ge(sc_ps, m + 1)
                    if m >= 4:
                        dve.wait_ge(sc_used, m - 3)
                    dve.tensor_tensor(masked[:, m % 4, :], duo_ps[:, 512 * (m % 2):512 * (m % 2) + 448], level,
                                      ALU.mult).then_inc(sc_ready, 1)

            def hgrn_out(ly, j):
                n = 2 * ly + j
                w = width(ly, HQ)
                dve.wait_ge(hg_diag, n + 1)
                dve.wait_ge(hg_o_ps, 4 * ly + 2 * j + 2)
                link(dve.tensor_tensor(e_b[:, 0:w], duo_ps[:, 0:w], proj[:, HI + j, 0:w], ALU.mult))
                dve.tensor_tensor(ke_b[:, 0:w], pair_ps[:, 0:w], e_b[:, 0:w], ALU.add).then_inc(hg_o, 1)
                dve.wait_ge(hg_rt, n + 1)
                link(dve.reciprocal(e_b[:, 0:w], e_b[:, 0:w]))
                link(dve.tensor_tensor(ke_b[:, 0:w], ke_b[:, 0:w], e_b[:, 0:w], ALU.mult))
                gz = proj[:, HZ + j, 0:w]
                dve.scalar_tensor_tensor(out=gz, in0=ke_b[:, 0:w], scalar=prm["hg_g"][:, n:n + 1], in1=gz, op0=ALU.mult,
                                         op1=ALU.mult).then_inc(hg_out, 1)

            def attention(ly):
                for n, (t, w) in enumerate(qk_tiles(ly)):
                    x = proj[:, t, 0:w]
                    gain = prm["k_g" if t == AK else "q_g"][:, ly:ly + 1]
                    dve.wait_ge(qk_rt, 3 * ly + n + 1)
                    link(dve.reciprocal(m_b[:, 0:w], m_b[:, 0:w]))
                    dve.scalar_tensor_tensor(out=x, in0=x, scalar=gain, in1=m_b[:, 0:w], op0=ALU.mult,
                                             op1=ALU.mult).then_inc(qk_norm, 1)
                    dve.wait_ge(qk_rot, 3 * ly + n + 1)
                    link(dve.tensor_tensor(lf_b[:, 0:LAT], duo_ps[:, 0:LAT], cst["sin"], ALU.mult))
                    link(dve.tensor_tensor(x[:, 0:LAT], x[:, 0:LAT], cst["cos"], ALU.mult))
                    dve.tensor_tensor(x[:, 0:LAT], x[:, 0:LAT], lf_b[:, 0:LAT], ALU.add).then_inc(qk_ready, 1)
                units = att_units(ly)
                for n in range(len(units) + 2):
                    if n < len(units):
                        m = ATT0[ly] + n
                        a, b = keys_of(units[n][2])
                        one = slice(m % 4, m % 4 + 1)
                        dve.wait_ge(at_s, m + 1)
                        link(dve.tensor_reduce(row_max[:, one], wide_ps[:, m % 2, a:b], AX.X, ALU.max))
                        dve.tensor_scalar(neg_max[:, one], row_max[:, one], -HD ** -0.5, None, ALU.mult).then_inc(at_max, 1)
                    if n >= 1 and n <= len(units):
                        m = ATT0[ly] + n - 1
                        a, b = keys_of(units[n - 1][2])
                        one = slice(m % 4, m % 4 + 1)
                        dve.wait_ge(at_exp, m + 1)
                        link(dve.reciprocal(row_inv[:, one], row_sum[:, one]))
                        dve.tensor_scalar(probs(m)[:, a:b], probs(m)[:, a:b], row_inv[:, one], None, ALU.mult).then_inc(at_p, 1)
                    if n >= 2:
                        m = ATT0[ly] + n - 2
                        i, r, c = units[n - 2]
                        rows = slice(64 * r, 64 * r + 64)
                        az = proj[rows, AZ + i, c * CH:(c + 1) * CH]
                        dve.wait_ge(at_o_ps, m + 1)
                        dve.tensor_tensor(az, duo_ps[rows, 512 * (m % 2):512 * (m % 2) + CH], az, ALU.mult).then_inc(at_out, 1)

            def fourier(ly):
                for s in (0, 1)[:2 - ly]:
                    a, b = ((0, LAT), (LAT, TOK))[s]
                    dve.wait_ge(ft_y_ps, 2 * ly + s + 1)
                    for j in range(2):
                        fz = proj[:, FZ + j, a:b]
                        dve.tensor_tensor(fz, duo_ps[:, 512 * j:512 * j + b - a], fz, ALU.mult).then_inc(ft_out, 1)

            def residual(ly):
                w = width(ly, HQ)
                for n in range(KT):
                    dve.wait_ge(evacuated, EVAC[f"out{ly}"] + n + 1)
                    dve.tensor_tensor(h[:, n, 0:w], h[:, n, 0:w], resid[:, n % 2, 0:w], ALU.add).then_inc(h_ready, 1)

            lower_bounds()
            modulation(0)
            for ly in range(DEPTH):
                if ly == 1:
                    pass
                reciprocal_root(ly, TOK)
                for k in range(KT):
                    dve.tensor_tensor(xn_t[:, k, :], h[:, k, :], root[:, :], ALU.mult).then_inc(scaled, 1)
                if ly == 0:
                    modulation(1)
                for u, j, d in hg_units(ly):
                    hgrn_unit(ly, u, j, d)
                    if d == 1:
                        hgrn_out(ly, j)
                attention(ly)
                fourier(ly)
                residual(ly)
            reciprocal_root(N_FINAL, LAT)
            for k in range(KT):
                dve.scalar_tensor_tensor(out=h[:, k, 0:LAT], in0=h[:, k, 0:LAT], scalar=prm["final_g"][:, k:k + 1],
                                         in1=root[:, 0:LAT], op0=ALU.mult, op1=ALU.mult).then_inc(scaled, 1)
            def half_turn():
                dve.memset(half_pi, float(np.pi / 2)).then_inc(rope_arg, 1)
                dve.wait_ge(const2_landed, 16)
                dve.wait_ge(pos_landed, 16)
                turn = 2 * np.pi
                c1 = 6.28125
                c2 = float(np.float32(round((turn - c1) * 2 ** 20) / 2 ** 20))
                link(dve.tensor_copy(sin_2, pos_i))
                link(dve.tensor_scalar(sin_2, sin_2, cst2["inv_freq"], None, ALU.mult))
                link(dve.tensor_scalar(cos_2, sin_2, 1.0 / turn, 12582912.0, ALU.mult, ALU.add))
                link(dve.tensor_scalar(cos_2, cos_2, 12582912.0, None, ALU.subtract))
                for part in (c1, c2, turn - c1 - c2):
                    link(dve.scalar_tensor_tensor(out=sin_2, in0=cos_2, scalar=-part, in1=sin_2, op0=ALU.mult, op1=ALU.add))
                dve.tensor_scalar(sin_2, sin_2, 3.1415925, -3.1415925, ALU.min, ALU.max).then_inc(rope_arg, 1)

            def scale_tiles(n, src, dst, gain):
                for k in range(KT):
                    w = src[:, k, :].shape[1]
                    dve.scalar_tensor_tensor(out=dst[:, k, :], in0=src[:, k, :], scalar=prm[gain][:, k:k + 1],
                                             in1=root[:, 0:w], op0=ALU.mult, op1=ALU.mult).then_inc(scaled, 1)

            reciprocal_root(N_MEM, CTX)
            scale_tiles(N_MEM, mem_x, mem_x, "g_mem")
            reciprocal_root(N_MIX_PRE, LAT)
            scale_tiles(N_MIX_PRE, x_2, y_2, "g_mix_pre")
            half_turn()
            taps = prm["conv2"].rearrange("p (n t) -> p n t", t=5)
            for q in range(12):
                x, y = tile_2[:, DQ2 + q, :], conv_y[:, q % 2, :]
                dve.wait_ge(evacuated, EVAC["proj_2"] + DQ2 + q + 1)
                if q >= 2:
                    dve.wait_ge(cv_ready, q - 1)
                link(dve.tensor_scalar(y, x, taps[:, q, 2:3], None, ALU.mult))
                for t in (0, 1, 3, 4):
                    off = t - 2
                    a, b = max(0, -off), LAT - max(0, off)
                    ins = dve.scalar_tensor_tensor(out=y[:, a:b], in0=x[:, a + off:b + off], scalar=taps[:, q, t:t + 1],
                                                   in1=y[:, a:b], op0=ALU.mult, op1=ALU.add)
                    if t < 4:
                        link(ins)
                    else:
                        ins.then_inc(cv_sum, 1)
            dve.wait_ge(evacuated, EVAC["ab_2"] + 1)
            dve.tensor_tensor(g_tok, ab[:, :, 0:8], prm["dt_bias"].unsqueeze(1).broadcast_to([P, NLAT, 8]), ALU.add).then_inc(g_x, 1)
            dve.wait_ge(g_l, 3)
            link(dve.scalar_tensor_tensor(out=g_tok, in0=g_tok, scalar=0.0, in1=g_soft, op0=ALU.max, op1=ALU.add))
            dve.scalar_tensor_tensor(out=g_tok, in0=g_tok, scalar=-1.0, in1=a_exp.unsqueeze(1).broadcast_to([P, NLAT, 8]),
                                     op0=ALU.mult, op1=ALU.mult).then_inc(g_ready, 1)
            dve.wait_ge(g_ps, 1)
            for d in range(2):
                dve.tensor_copy(g_cum[:, :, 4 * d:4 * d + 4], duo_ps[:, 16 * d:16 * d + 16].rearrange("p (c n) -> p c n", c=NLAT)).then_inc(g_c, 1)
            dve.wait_ge(g_e, 1)
            dve.tensor_tensor(beta_g, beta, g_exp, ALU.mult).then_inc(g_b, 1)
            for n in range(8):
                x, r = tile_2[:, DQ2 + n, :], work[:, 2 + n % 2, 0:LAT]
                dve.wait_ge(l2_rt, n + 1)
                link(dve.reciprocal(r, r))
                dve.scalar_tensor_tensor(out=x, in0=x, scalar=P ** -0.5 if n < 4 else 1.0, in1=r, op0=ALU.mult,
                                         op1=ALU.mult).then_inc(l2_ready, 1)
            dve.wait_ge(rope_table, 1)
            for n in range(5):
                x, t = tile_2[:, n, :], work[:, 4 + n % 2, 0:LAT]
                dve.wait_ge(rp_rot, n + 1)
                link(dve.tensor_tensor(t, pair_ps[:, 512 * (n % 2):512 * (n % 2) + LAT], sin_2, ALU.mult))
                link(dve.tensor_tensor(x, x, cos_2, ALU.mult))
                dve.tensor_tensor(x, x, t, ALU.add).then_inc(rp_ready, 1)
            for m in range(len(WIN) + 2):
                if m < len(WIN):
                    i, r, c = WIN[m]
                    a, b, ma, mb = window_keys(c)
                    one = slice(m % 4, m % 4 + 1)
                    dve.wait_ge(w_s, m + 1)
                    if m >= 2:
                        dve.wait_ge(w_pt_ps, m - 1)
                    head = i + 4 * r
                    link(dve.tensor_tensor_reduce(probs(m)[:, 0:b - a], wide_ps[:, m % 2, 0:b - a], cst2["window"][:, ma:mb],
                                                  HD ** -0.5, prm["sink"][:, head:head + 1], ALU.add, ALU.max,
                                                  row_max2[:, one]))
                    dve.tensor_scalar(neg_max2[:, one], row_max2[:, one], -1.0, None, ALU.mult).then_inc(w_max, 1)
                if 1 <= m <= len(WIN):
                    n = m - 1
                    a, b, _, _ = window_keys(WIN[n][2])
                    one = slice(n % 4, n % 4 + 1)
                    dve.wait_ge(w_exp, 2 * n + 2)
                    link(dve.tensor_tensor(row_sum2[:, one], row_sum2[:, one], sink_e[:, one], ALU.add))
                    link(dve.reciprocal(row_inv2[:, one], row_sum2[:, one]))
                    dve.tensor_scalar(probs(n)[:, 0:b - a], probs(n)[:, 0:b - a], row_inv2[:, one], None, ALU.mult).then_inc(w_p, 1)
                if m >= 2:
                    n = m - 2
                    i, r, c = WIN[n]
                    rows = slice(64 * r, 64 * r + 64)
                    dve.wait_ge(w_o_ps, n + 1)
                    dve.tensor_copy(tile_2[rows, i, c * CH:(c + 1) * CH], duo_ps[rows, 512 * (n % 2):512 * (n % 2) + CH]).then_inc(w_out_s, 1)

            def heads(v):
                return v.unsqueeze(2).broadcast_to([P, 4, CH])

            ident_4 = cst["ident"].unsqueeze(1).broadcast_to([P, 4, CH])
            for s in range(NLAT):
                for d in range(2):
                    g, c = 2 * s + d, chunk_at(d, s)
                    last = CH - 1 if d == 0 else 0
                    mine = slice(4 * d, 4 * d + 4)
                    dve.wait_ge(dn_a, g + 1)
                    link(dve.tensor_tensor(dn(d, XM), dn_bank(d, 0), heads(g_cum[:, c, mine]), ALU.subtract))
                    link(dve.tensor_tensor(g_end[:, d], dn_bank(d, 0)[:, :, last], g_cum[:, c, mine], ALU.subtract))
                    dve.tensor_tensor(dn(d, XM), dn(d, XM), cst2[f"tri{d}"].unsqueeze(1).broadcast_to([P, 4, CH]), ALU.mult).then_inc(dn_diff, 1)
                    dve.wait_ge(dn_exp, 4 * g + 4)
                    link(dve.tensor_tensor(dn(d, XT), dn_bank(d, 1), dn(d, XM), ALU.mult))
                    dve.tensor_tensor(dn(d, QK), dn_bank(d, 3), dn(d, XM), ALU.mult).then_inc(dn_x, 1)
                    dve.tensor_tensor(dn(d, XT), dn(d, XT), dn_bank(d, 2), ALU.mult).then_inc(dn_x, 1)
                    dve.wait_ge(dn_tok_ps, g + 1)
                    dve.tensor_tensor(dn(d, KBG), dn_bank(d, 0), heads(beta_g[:, c, mine]), ALU.mult).then_inc(dn_tok, 1)
                    dve.tensor_tensor(dn(d, KG), dn_bank(d, 0), heads(g_end[:, d]), ALU.mult).then_inc(dn_tok, 1)
                    dve.tensor_tensor(dn(d, VB), dn_bank(d, 1), heads(beta[:, c, mine]), ALU.mult).then_inc(dn_tok, 1)
                for l in range(LEVELS):
                    for d in range(2):
                        at = 2 * (LEVELS * s + l) + d
                        dve.wait_ge(dn_z_ps, at + 1)
                        if l == 0:
                            link(dve.scalar_tensor_tensor(out=dn(d, T), in0=dn_bank(d, 2), scalar=-1.0, in1=ident_4, op0=ALU.mult, op1=ALU.add))
                            dve.scalar_tensor_tensor(out=dn(d, R), in0=dn(d, XM), scalar=-1.0, in1=ident_4, op0=ALU.mult, op1=ALU.add).then_inc(dn_t, 1)
                        else:
                            if l < LEVELS - 1:
                                link(dve.tensor_tensor(dn(d, T), dn(d, T), dn_bank(d, 2), ALU.subtract))
                            dve.tensor_tensor(dn(d, R), dn(d, R), dn_bank(d, 3), ALU.subtract).then_inc(dn_t, 1)
                for d in range(2):
                    c = chunk_at(d, s)
                    o = o_dn[:, :, c * CH:(c + 1) * CH]
                    dve.wait_ge(dn_o_ps, 2 * s + d + 1)
                    if s < NLAT // 2:
                        link(dve.tensor_copy(o, dn_bank(d, 2)))
                        if s == 0:
                            dve.tensor_copy(s_dn[:, d], dn_bank(d, 3)).then_inc(dn_s, 1)
                    if s >= NLAT // 2:
                        ins = dve.tensor_tensor(o, o, dn_bank(d, 2), ALU.add)
                        if s == NLAT - 1:
                            ins.then_inc(dn_s, 1)
                        else:
                            link(ins)
                    if 0 < s < NLAT - 1:
                        link(dve.tensor_tensor(s_dn[:, d], s_dn[:, d], heads(s_decay[:, d]), ALU.mult))
                        dve.tensor_tensor(s_dn[:, d], s_dn[:, d], dn_bank(d, 3), ALU.add).then_inc(dn_s, 1)
            for n in range(4):
                o, r, gate = o_dn[:, n, :], work[:, 2 + n % 2, 0:LAT], tile_2[:, DG2 + n, :]
                dve.wait_ge(do_rt, n + 1)
                link(dve.reciprocal(r, r))
                link(dve.tensor_tensor(o, o, r, ALU.mult))
                dve.scalar_tensor_tensor(out=gate, in0=o, scalar=prm["g_dn"], in1=gate, op0=ALU.mult, op1=ALU.mult).then_inc(do_out, 1)

            def add_closed(n, gain, done):
                reciprocal_root(n, LAT)
                scale_tiles(n, y_2, y_2, gain)
                for k in range(KT):
                    dve.wait_ge(scaled, 8 * n + k + 1)
                    dve.tensor_tensor(x_2[:, k, :], x_2[:, k, :], y_2[:, k, :], ALU.add).then_inc(done, 1)

            add_closed(N_MIX_POST, "g_mix_post", x_ready)
            reciprocal_root(N_CROSS_PRE, LAT)
            scale_tiles(N_CROSS_PRE, x_2, y_2, "g_cross_pre")
            for m in range(len(CROSS) + 2):
                if m < len(CROSS):
                    one = slice(m % 4, m % 4 + 1)
                    dve.wait_ge(c_s, m + 1)
                    link(dve.tensor_reduce(row_max2[:, one], wide_ps[:, m % 2, 0:CTX], AX.X, ALU.max))
                    dve.tensor_scalar(neg_max2[:, one], row_max2[:, one], -256 ** -0.5, None, ALU.mult).then_inc(c_max, 1)
                if 1 <= m <= len(CROSS):
                    n = m - 1
                    one = slice(n % 4, n % 4 + 1)
                    dve.wait_ge(c_exp, n + 1)
                    link(dve.reciprocal(row_inv2[:, one], row_sum2[:, one]))
                    dve.tensor_scalar(probs(n)[:, 0:CTX], probs(n)[:, 0:CTX], row_inv2[:, one], None, ALU.mult).then_inc(c_p, 1)
                if m >= 2:
                    n = m - 2
                    hd, c = CROSS[n]
                    dve.wait_ge(c_o_ps, n + 1)
                    dve.tensor_copy(o_c[:, 2 * hd:2 * hd + 2, c * CH:(c + 1) * CH],
                                    duo_ps[:, 512 * (n % 2):512 * (n % 2) + 256].rearrange("p (e t) -> p e t", e=2)).then_inc(c_out, 1)
            add_closed(N_CROSS_POST, "g_cross_post", x_ready)
            reciprocal_root(N_FFN_PRE, LAT)
            scale_tiles(N_FFN_PRE, x_2, y_2, "g_ffn_pre")
            for t in range(22):
                dve.wait_ge(evacuated, EVAC["gu"] + 2 * t + 2)
                dve.tensor_tensor(tile_2[:, t, :], tile_2[:, t, :], resid[:, t % 2, 0:LAT], ALU.mult).then_inc(ffn_ready, 1)
            add_closed(N_FFN_POST, "g_ffn_post", final_ready)

        @block.tensor
        def _(pe):
            def use_chunk(c):
                pe.wait_ge(landed[c % RING], 16 * (c // RING + 1))
                return ring[:, c % RING, :]

            def project(stage, tile, chunk, k_tiles, rhs, w, rhs_ready=None):
                g = EVAC[stage] + tile
                if g >= 2:
                    pe.wait_ge(evacuated, g - 1)
                for k in range(k_tiles):
                    if k % KT == 0:
                        wt = use_chunk(chunk + k // KT)
                    if rhs_ready:
                        rhs_ready(k)
                    for a, b in pieces(w):
                        last = pe.matmul(wide_ps[:, g % 2, a:b], wt[:, k % KT * P:(k % KT + 1) * P], rhs(k)[:, a:b],
                                         start=k == 0, stop=k == k_tiles - 1)
                    if k % KT == KT - 1 or k == k_tiles - 1:
                        last.then_inc(chunk_used, 1)

            def modulation(ly):
                if ly == 0:
                    pe.wait_ge(c_ready, 1)
                for n in range(N_MOD):
                    wt = use_chunk(PLAN[f"mod{ly}"] + n)
                    at = 512 * (1 - ly) + 2 * n
                    for k in range(KT):
                        last = pe.matmul(duo_ps[:, at:at + 2], wt[:, k * P:(k + 1) * P], c_act[:, 2 * k:2 * k + 2],
                                         start=k == 0, stop=k == KT - 1, skip_group_check=True)
                    last.then_inc(chunk_used, 1)

            def norm_sum(n, w):
                for k in range(KT):
                    pe.wait_ge(sq_ready, 8 * n + k + 1)
                    for a, b in pieces(w):
                        last = pe.matmul(pair_ps[:, a:b], cst["ones"], sq[:, k % 2, a:b], start=k == 0, stop=k == KT - 1)
                    last.then_inc(sq_used, 1)

            def by_token(src, ps, done):
                for c in range(NCH):
                    last = pe.transpose(ps[:, c * CH:(c + 1) * CH], src[:, c * CH:(c + 1) * CH], cst["ident"])
                last.then_inc(done, 1)

            def hgrn_unit(ly, u, j, d):
                ctx_out = ly == 0
                if d == 0:
                    if j:
                        pe.wait_ge(hg_o, 2 * ly + j)
                    for a, b in pieces(width(ly, HQ)):
                        pe.matmul(pair_ps[:, a:b], zero[0:1, :], cst["cos"][0:1, 0:b - a], start=True, stop=False,
                                  skip_group_check=True)
                pe.wait_ge(hg_ke, u + 1)
                if d == 1 or j == 1:
                    pe.wait_ge(sc_ready, SC0[u])
                by_token(ke_b, duo_ps, hg_kt_ps)
                pe.wait_ge(hg_kt, u + 1)
                for c in range(NCH):
                    last = pe.matmul(duo_ps[:, c * CH:(c + 1) * CH], k_tok[:, c, :], v_tok[:, j, c, :], start=True, stop=True)
                last.then_inc(hg_u, 1)
                pe.wait_ge(lev_ready, LEVELS * (u + 1))
                pe.wait_ge(hg_qe, u + 1)
                pe.wait_ge(hg_s, u + 1)
                side = 1 if d == 0 else 0
                tiles = [(c, r) for c in chunk_list(ly) for r in range(2)]

                def scores(n):
                    c, r = tiles[n]
                    m = SC0[u] + n
                    rows = slice(64 * r, 64 * r + 64)
                    if m >= 2:
                        pe.wait_ge(sc_ready, m - 1)
                    for l in range(LEVELS):
                        w = decay[rows, l, c * CH:(c + 1) * CH]
                        last = pe.matmul(duo_ps[:, 512 * (m % 2) + 64 * l:512 * (m % 2) + 64 * l + 64], w,
                                         halves(w, 1 << l)[:, :, side, :], start=True, stop=True, skip_group_check=True)
                    last.then_inc(sc_ps, 1)

                def values(n):
                    c, r = tiles[n]
                    m = SC0[u] + n
                    rows = slice(64 * r, 64 * r + 64)
                    pe.wait_ge(sc_ready, m + 1)
                    o = pair_ps[rows, c * CH:(c + 1) * CH]
                    if c != order(d)[0]:
                        pe.matmul(o, state[rows, c, :], qe_b[rows, c * CH:(c + 1) * CH], start=False, stop=False,
                                  skip_group_check=True)
                    for l in range(LEVELS):
                        last = pe.matmul(halves(o, 1 << l)[:, :, side, :], v_tok[:, j, c, rows],
                                         masked[:, m % 4, 64 * l:64 * l + 64], start=False, stop=l == LEVELS - 1,
                                         skip_group_check=True)
                    last.then_inc(sc_used, 1)
                    if n == len(tiles) - 1:
                        pe.matmul(pair_ps[:, c * CH:c * CH + 64], zero[0:1, :], cst["cos"][0:1, 0:64], start=False, stop=True,
                                  skip_group_check=True).then_inc(hg_o_ps, 1)

                for n in range(len(tiles) + 1):
                    if n < len(tiles):
                        scores(n)
                    if n:
                        values(n - 1)

            def hgrn_norm(ly, j):
                w = width(ly, HQ)
                n = 2 * ly + j
                pe.wait_ge(hg_qk, n + 1)
                pe.wait_ge(sc_ready, SC0[4 * ly + 2 * j + 2])
                for a, b in pieces(w):
                    last = pe.matmul(duo_ps[:, a:b], cst["ones_head"], proj[:, FF + j, a:b], start=True, stop=True)
                last.then_inc(hg_diag, 1)
                pe.wait_ge(hg_sq, n + 1)
                for a, b in pieces(w):
                    last = pe.matmul(duo_ps[:, a:b], cst["ones_head"], m_b[:, a:b], start=True, stop=True)
                last.then_inc(hg_ms, 1)

            def attention(ly):
                for n, (t, w) in enumerate(qk_tiles(ly)):
                    m = 3 * ly + n
                    pe.wait_ge(qk_sq, m + 1)
                    for a, b in pieces(w):
                        last = pe.matmul(pair_ps[:, a:b], cst["ones_head"], e_b[:, a:b], start=True, stop=True)
                    last.then_inc(qk_ms, 1)
                    pe.wait_ge(qk_norm, m + 1)
                    if n:
                        pe.wait_ge(qk_ready, m)
                    pe.matmul(duo_ps[:, 0:LAT], cst["rot_pair"], proj[:, t, 0:LAT], start=True, stop=True).then_inc(qk_rot, 1)
                by_token(proj[:, AV, :], pair_ps, vt_ps)
                pe.wait_ge(vt_ready, 3 * ly + 3)
                pe.wait_ge(qk_ready, 3 * ly + 3)
                units = att_units(ly)
                for n in range(len(units) + 2):
                    if n < len(units):
                        i, r, c = units[n]
                        m = ATT0[ly] + n
                        rows = slice(64 * r, 64 * r + 64)
                        if n >= 2:
                            pe.wait_ge(at_exp, m - 1)
                        for a, b in ([(0, LAT)] if c < NLAT else []) + [(LAT, TOK)]:
                            last = pe.matmul(wide_ps[:, m % 2, a:b], proj[rows, AQ + i, c * CH:(c + 1) * CH],
                                             proj[rows, AK, a:b], start=True, stop=True)
                        last.then_inc(at_s, 1)
                    if 1 <= n <= len(units):
                        m = ATT0[ly] + n - 1
                        a, b = keys_of(units[n - 1][2])
                        pe.wait_ge(at_p, m + 1)
                        if n >= 2:
                            pe.wait_ge(at_pt, m)
                        for t in range(a // P, b // P):
                            last = pe.transpose(pair_ps[:, t * P:(t + 1) * P], probs(m)[:, t * P:(t + 1) * P], cst["ident"])
                        last.then_inc(at_pt_ps, 1)
                    if n >= 2:
                        m = ATT0[ly] + n - 2
                        i, r, c = units[n - 2]
                        a, b = keys_of(c)
                        pe.wait_ge(at_pt, m + 1)
                        if n >= 4:
                            pe.wait_ge(at_out, m - 1)
                        for t in range(a // P, b // P):
                            last = pe.matmul(duo_ps[64 * r:64 * r + 64, 512 * (m % 2):512 * (m % 2) + CH],
                                             v_tok[:, 0, t, 64 * r:64 * r + 64], probs_t(m)[:, t * P:(t + 1) * P],
                                             start=t == a // P, stop=t == b // P - 1)
                        last.then_inc(at_o_ps, 1)

            def fourier(ly):
                pe.wait_ge(at_pt, ATT0[ly] + len(att_units(ly)))
                pe.wait_ge(at_out, ATT0[ly] + len(att_units(ly)))
                m = FT0[ly]
                chunk = PLAN[f"dft{ly}"]
                for s in (0, 1)[:2 - ly]:
                    lo, n_t = ((0, NLAT), (LAT, 2))[s]
                    size = n_t * P
                    for tt in range(n_t):
                        for j in range(2):
                            if m - FT0[ly] >= 2:
                                pe.wait_ge(ft_a, m - 1)
                            pe.matmul(pair_ps[:, 512 * (m % 2):512 * (m % 2) + 256],
                                      proj[:, FU + j, lo + tt * P:lo + (tt + 1) * P], cst["dft_ch"], start=True,
                                      stop=True).then_inc(ft_a_ps, 1)
                            m += 1
                    pe.wait_ge(ft_a, m)
                    if s:
                        pe.wait_ge(ft_out, 4 * ly + 2)
                    for tt in range(n_t):
                        if s == 0 or tt == 0:
                            wt = use_chunk(chunk)
                            chunk += 1
                        base = 0 if s == 0 else tt * 2 * size
                        for j in range(2):
                            for part in range(2):
                                last = pe.matmul(duo_ps[:, 512 * j:512 * j + size], ft_buf[:, tt, j, part * P:(part + 1) * P],
                                                 wt[:, base + part * size:base + (part + 1) * size],
                                                 start=tt == 0 and part == 0, stop=tt == n_t - 1 and part == 1,
                                                 skip_group_check=True)
                        if s == 0 or tt == n_t - 1:
                            last.then_inc(chunk_used, 1)
                    pe.matmul(duo_ps[:, 512:512 + 64], zero[0:1, :], cst["cos"][0:1, 0:64], start=False, stop=True,
                              skip_group_check=True).then_inc(ft_y_ps, 1)

            pe.wait_ge(setup_landed, 32)
            pe.wait_ge(ready, 2)
            norm_sum(0, TOK)
            modulation(0)
            modulation(1)
            for ly in range(DEPTH):
                if ly:
                    norm_sum(ly, TOK)
                for t in range(NPROJ):
                    project(f"proj{ly}", t, PLAN[f"proj{ly}"] + t, KT, lambda k: xn_t[:, k, :], width(ly, t),
                            (lambda k: pe.wait_ge(xn_ready, 16 * ly + 2 * k + 2)) if t == 0 else None)
                for j in range(2):
                    pe.wait_ge(evacuated, EVAC[f"proj{ly}"] + NPROJ)
                    if ly == 0 and j == 0:
                        pe.wait_ge(mod_ready, 4)
                    if j:
                        pe.wait_ge(vt_ready, 3 * ly + 1)
                    by_token(proj[:, HI + j, :], duo_ps, vt_ps)
                pe.wait_ge(vt_ready, 3 * ly + 2)
                for u, j, d in hg_units(ly):
                    hgrn_unit(ly, u, j, d)
                    if d == 1:
                        hgrn_norm(ly, j)
                attention(ly)
                fourier(ly)
                pe.wait_ge(ft_out, (4, 6)[ly])
                pe.wait_ge(conv_out, 2 * ly + 2)
                for n in range(KT):
                    project(f"out{ly}", n, PLAN[f"out{ly}"] + n, KT, lambda k: proj[:, MIX[k], :], width(ly, HQ))
            norm_sum(N_FINAL, LAT)
            def scaled_by(n):
                return lambda k: pe.wait_ge(scaled, 8 * n + k + 1)

            def ck(n):
                project("ck", n, PLAN["ck"] + n, KT, lambda k: mem_x[:, k, :], CTX, scaled_by(N_MEM) if n == 0 else None)

            norm_sum(N_MEM, CTX)
            ck(0)
            ck(1)
            norm_sum(N_MIX_PRE, LAT)
            for n in range(2, KT):
                ck(n)
            for n in range(KT):
                g = EVAC["cv"] + n
                pe.wait_ge(evacuated, g - 1)
                wt = use_chunk(PLAN["cv"] + n)
                for t in range(2):
                    for k in range(KT):
                        last = pe.matmul(wide_ps[:, g % 2, t * P:(t + 1) * P], mem_x[:, k, t * P:(t + 1) * P],
                                         wt[:, k * P:(k + 1) * P], start=k == 0, stop=k == KT - 1)
                last.then_inc(chunk_used, 1)
            for t in range(22):
                project("proj_2", t, PLAN["proj_2"] + t, KT, lambda k: y_2[:, k, :], LAT, scaled_by(N_MIX_PRE) if t == 0 else None)
            wt = use_chunk(PLAN["ab_2"])
            g = EVAC["ab_2"]
            pe.wait_ge(evacuated, g - 1)
            for c in range(NLAT):
                for k in range(KT):
                    last = pe.matmul(wide_ps[:, g % 2, 16 * c:16 * c + 16], y_2[:, k, c * CH:(c + 1) * CH],
                                     wt[:, k * P:k * P + 16], start=k == 0, stop=k == KT - 1)
            last.then_inc(chunk_used, 1)
            pe.wait_ge(g_ready, 1)
            pe.wait_ge(const2_landed, 16)
            for d in range(2):
                last = pe.matmul(duo_ps[:, 16 * d:16 * d + 16], cst2[f"tri{d}"], g_tok[:, :, 4 * d:4 * d + 4], start=True, stop=True)
            last.then_inc(g_ps, 1)
            for n in range(8):
                pe.wait_ge(l2_sq, n + 1)
                if n >= 2:
                    pe.wait_ge(l2_rt, n - 1)
                pe.matmul(pair_ps[:, 512 * (n % 2):512 * (n % 2) + LAT], cst["ones"], sq[:, n % 2, 0:LAT], start=True,
                          stop=True).then_inc(l2_ss, 1)
            pe.wait_ge(l2_rt, 8)
            for n in range(5):
                if n >= 2:
                    pe.wait_ge(rp_ready, n - 1)
                pe.matmul(pair_ps[:, 512 * (n % 2):512 * (n % 2) + LAT], cst2["rot_half"], tile_2[:, n, :], start=True,
                          stop=True).then_inc(rp_rot, 1)
            pe.wait_ge(g_c, 2)
            for c in range(NLAT):
                last = pe.transpose(duo_ps[:, c * CH:(c + 1) * CH], tile_2[:, AV2, c * CH:(c + 1) * CH], cst["ident"])
            last.then_inc(v2_ps, 1)
            pe.wait_ge(v2_ready, 1)
            pe.wait_ge(rp_ready, 5)
            for m in range(len(WIN) + 2):
                if m < len(WIN):
                    i, r, c = WIN[m]
                    rows = slice(64 * r, 64 * r + 64)
                    a, b, _, _ = window_keys(c)
                    if m >= 2:
                        pe.wait_ge(w_max, m - 1)
                    pe.matmul(wide_ps[:, m % 2, 0:b - a], tile_2[rows, i, c * CH:(c + 1) * CH], tile_2[rows, AK2, a:b],
                              start=True, stop=True).then_inc(w_s, 1)
                if 1 <= m <= len(WIN):
                    n = m - 1
                    a, b, _, _ = window_keys(WIN[n][2])
                    pe.wait_ge(w_p, n + 1)
                    if n:
                        pe.wait_ge(w_pt, n)
                    for t in range((b - a) // P):
                        last = pe.transpose(pair_ps[:, t * P:(t + 1) * P], probs(n)[:, t * P:(t + 1) * P], cst["ident"])
                    last.then_inc(w_pt_ps, 1)
                if m >= 2:
                    n = m - 2
                    i, r, c = WIN[n]
                    a, b, _, _ = window_keys(c)
                    pe.wait_ge(w_pt, n + 1)
                    if n >= 2:
                        pe.wait_ge(w_out_s, n - 1)
                    for t in range((b - a) // P):
                        last = pe.matmul(duo_ps[64 * r:64 * r + 64, 512 * (n % 2):512 * (n % 2) + CH],
                                         v_tok[:, 0, a // P + t, 64 * r:64 * r + 64], probs_t(n)[:, t * P:(t + 1) * P],
                                         start=t == 0, stop=t == (b - a) // P - 1)
                    last.then_inc(w_o_ps, 1)

            def four(out_ap, lhs, rhs, **flags):
                for hd in range(4):
                    last = pe.matmul(out_ap[:, hd, :], lhs(hd), rhs(hd), start=True, stop=True, **flags)
                return last

            pe.wait_ge(w_out_s, len(WIN))
            pe.wait_ge(l2_ready, 8)
            pe.wait_ge(g_b, 1)
            for s in range(NLAT):
                for d in range(2):
                    g, c = 2 * s + d, chunk_at(d, s)
                    run = slice(c * CH, (c + 1) * CH)
                    if s:
                        pe.wait_ge(dn_s, g - 1)
                    wide = lambda v: v.broadcast_to([P, P])
                    four(dn_bank(d, 0), lambda hd: wide(g_tok[:, c, 4 * d + hd:4 * d + hd + 1]), lambda hd: cst2[f"tri{d}"])
                    four(dn_bank(d, 1), lambda hd: tile_2[:, DK2 + hd, run], lambda hd: tile_2[:, DK2 + hd, run])
                    four(dn_bank(d, 2), lambda hd: wide(beta[:, c, 4 * d + hd:4 * d + hd + 1]), lambda hd: cst["ident"])
                    four(dn_bank(d, 3), lambda hd: tile_2[:, DK2 + hd, run], lambda hd: tile_2[:, DQ2 + hd, run]).then_inc(dn_a, 1)
                for d in range(2):
                    g, c = 2 * s + d, chunk_at(d, s)
                    pe.wait_ge(dn_x, 2 * g + 2)
                    for hd in range(4):
                        pe.transpose(dn_bank(d, 0)[:, hd, :], tile_2[:, DK2 + hd, c * CH:(c + 1) * CH], cst["ident"])
                    for hd in range(4):
                        last = pe.transpose(dn_bank(d, 1)[:, hd, :], tile_2[:, DV2 + hd, c * CH:(c + 1) * CH], cst["ident"])
                    last.then_inc(dn_tok_ps, 1)
                for d in range(2):
                    pe.wait_ge(dn_xm, 2 * (LEVELS * s) + d + 1)
                    four(dn_bank(d, 2), lambda hd: dn(d, XM)[:, hd, :], lambda hd: cst["ident"]).then_inc(dn_z_ps, 1)
                for l in range(1, LEVELS):
                    for d in range(2):
                        pe.wait_ge(dn_xm, 2 * (LEVELS * s + l) + d + 1)
                        pe.wait_ge(dn_t, 2 * (LEVELS * s + l - 1) + d + 1)
                        four(dn_bank(d, 3), lambda hd: dn(d, XM)[:, hd, :], lambda hd: dn(d, T)[:, hd, :]).then_inc(dn_y_ps, 1)
                    for d in range(2):
                        pe.wait_ge(dn_y, 2 * (6 * s + l - 1) + d + 1)
                        if l < LEVELS - 1:
                            four(dn_bank(d, 2), lambda hd: dn(d, R)[:, hd, :], lambda hd: dn(d, Y)[:, hd, :])
                        four(dn_bank(d, 3), lambda hd: dn(d, Y)[:, hd, :], lambda hd: dn(d, R)[:, hd, :]).then_inc(dn_z_ps, 1)
                for d in range(2):
                    pe.wait_ge(dn_t, 2 * (LEVELS * s + LEVELS - 1) + d + 1)
                    pe.wait_ge(dn_tok, 3 * (2 * s + d) + 3)
                    four(dn_bank(d, 0), lambda hd: dn(d, KBG)[:, hd, :], lambda hd: dn(d, R)[:, hd, :]).then_inc(dn_w_ps, 1)
                for d in range(2):
                    pe.wait_ge(dn_w, 2 * s + d + 1)
                    for hd in range(4):
                        last = pe.matmul(dn_bank(d, 1)[:, hd, :], dn(d, R)[:, hd, :], dn(d, VB)[:, hd, :], start=True, stop=s == 0)
                        if s:
                            last = pe.matmul(dn_bank(d, 1)[:, hd, :], dn(d, WT)[:, hd, :], s_dn[:, d, hd, :], start=False, stop=True)
                    last.then_inc(dn_v_ps, 1)
                for d in range(2):
                    pe.wait_ge(dn_v, 2 * s + d + 1)
                    pe.wait_ge(dn_qg, 2 * (2 * s + d) + 2)
                    four(dn_bank(d, 3), lambda hd: dn(d, KG)[:, hd, :], lambda hd: dn(d, VN)[:, hd, :])
                    for hd in range(4):
                        if s:
                            pe.matmul(dn_bank(d, 2)[:, hd, :], s_dn[:, d, hd, :], dn(d, QG)[:, hd, :], start=True, stop=False)
                        last = pe.matmul(dn_bank(d, 2)[:, hd, :], dn(d, VN)[:, hd, :], dn(d, QK)[:, hd, :], start=s == 0, stop=True)
                    last.then_inc(dn_o_ps, 1)
            for n in range(4):
                pe.wait_ge(do_sq, n + 1)
                if n >= 2:
                    pe.wait_ge(do_rt, n - 1)
                pe.matmul(pair_ps[:, 512 * (n % 2):512 * (n % 2) + LAT], cst["ones"], sq[:, n % 2, 0:LAT], start=True,
                          stop=True).then_inc(do_ss, 1)
            pe.wait_ge(do_out, 4)
            for n in range(KT):
                project("out_2", n, PLAN["out_2"] + n, KT, lambda k: tile_2[:, MIX2[k], :], LAT)
            norm_sum(N_MIX_POST, LAT)
            norm_sum(N_CROSS_PRE, LAT)
            for n in range(KT):
                project("cq", n, PLAN["cq"] + n, KT, lambda k: y_2[:, k, :], LAT, scaled_by(N_CROSS_PRE) if n == 0 else None)
            pe.wait_ge(evacuated, EVAC["cq"] + KT)
            for m in range(len(CROSS) + 2):
                if m < len(CROSS):
                    hd, c = CROSS[m]
                    if m >= 2:
                        pe.wait_ge(c_exp, m - 1)
                    for e in range(2):
                        last = pe.matmul(wide_ps[:, m % 2, 0:CTX], q_c[:, 2 * hd + e, c * CH:(c + 1) * CH], key_c[:, 2 * hd + e, :],
                                         start=e == 0, stop=e == 1)
                    last.then_inc(c_s, 1)
                if 1 <= m <= len(CROSS):
                    n = m - 1
                    pe.wait_ge(c_p, n + 1)
                    if n:
                        pe.wait_ge(c_pt, n)
                    for t in range(2):
                        last = pe.transpose(pair_ps[:, t * P:(t + 1) * P], probs(n)[:, t * P:(t + 1) * P], cst["ident"])
                    last.then_inc(c_pt_ps, 1)
                if m >= 2:
                    n = m - 2
                    hd, c = CROSS[n]
                    pe.wait_ge(c_pt, n + 1)
                    if n >= 2:
                        pe.wait_ge(c_out, n - 1)
                    for e in range(2):
                        for t in range(2):
                            last = pe.matmul(duo_ps[:, 512 * (n % 2) + e * P:512 * (n % 2) + (e + 1) * P],
                                             val_c[:, t, (2 * hd + e) * P:(2 * hd + e + 1) * P], probs_t(n)[:, t * P:(t + 1) * P],
                                             start=t == 0, stop=t == 1)
                    last.then_inc(c_o_ps, 1)
            pe.wait_ge(c_out, len(CROSS))
            for n in range(KT):
                project("co", n, PLAN["co"] + n, KT, lambda k: o_c[:, k, :], LAT)
            norm_sum(N_CROSS_POST, LAT)
            norm_sum(N_FFN_PRE, LAT)
            for n in range(44):
                project("gu", n, PLAN["gu"] + n, KT, lambda k: y_2[:, k, :], LAT, scaled_by(N_FFN_PRE) if n == 0 else None)
            pe.wait_ge(ffn_ready, 22)
            for n in range(KT):
                project("down", n, PLAN["down"] + 3 * n, 22, lambda k: tile_2[:, k, :], LAT)
            norm_sum(N_FFN_POST, LAT)


def tiles_of_rows(v):
    return np.ascontiguousarray(np.moveaxis(np.asarray(v).reshape(-1, P), 1, 0))


def feature_major(x):
    t, f = x.shape
    return x.T.reshape(f // P, P, t).transpose(1, 0, 2)


def chunks_of(w):
    k, n = w.shape
    return w.reshape(k // P, P, n // P, P).transpose(2, 1, 0, 3).reshape(n // P, P, k)


def head_pairs(heads, width=HD):
    return np.concatenate([np.arange(h * width, (h + 1) * width) for h in heads])


def in_order():
    start = dict(zip(("cb", "cc", "cv", "cz", "aq", "ak", "av", "az", "hq", "ff", "fb", "hi", "hz", "fu", "fz"),
                     np.cumsum([0, 256, 256, 256, 256, 256, 128, 128, 256, 256, 256, 256, 256, 256, 256])))
    whole = lambda name, n=256: start[name] + np.arange(n)
    heads = head_pairs((0, 2, 1, 3))
    return np.concatenate([whole("hq"), whole("hz"), whole("ff"), whole("fb"), whole("hi"), start["aq"] + heads,
                           whole("ak", 128), whole("av", 128), start["az"] + heads, whole("fu"), whole("fz"),
                           whole("cz"), whole("cb"), whole("cc"), whole("cv")])


def dft(n):
    k = np.outer(np.arange(n), np.arange(n)) % n
    return np.cos(2 * np.pi * k / n) / np.sqrt(n), np.sin(2 * np.pi * k / n) / np.sqrt(n)


def dft_chunks():
    c, s = dft(LAT)
    lat = np.concatenate([c.reshape(NLAT, P, LAT), -s.reshape(NLAT, P, LAT)], axis=2)
    c, s = dft(CTX)
    ctx = np.concatenate([c.reshape(2, P, CTX), -s.reshape(2, P, CTX)], axis=2).transpose(1, 0, 2).reshape(1, P, CHUNK)
    return lat, ctx


def half_mask(b, back):
    s, t = np.arange(P)[:, None], np.arange(P)[None, :]
    read, written = (t % (2 * b) >= b, s % (2 * b) < b) if not back else (t % (2 * b) < b, s % (2 * b) >= b)
    return (s // (2 * b) == t // (2 * b)) & read & written


def level_masks(back):
    t = np.arange(P)
    return np.concatenate([half_mask(1 << l, back)[:, ((t >> l) & 1) == (0 if back else 1)] for l in range(LEVELS)], 1)


def rotation(pairs):
    r = np.zeros((P, P))
    for a, b in pairs:
        r[b, a] = -1.0
        r[a, b] = 1.0
    return r


def constants():
    n = HD // 4
    rows, cols = np.divmod(np.arange(LAT), 64)
    freqs = (10000.0 ** (-np.arange(n, dtype=np.float32) / n)).astype(np.float32)
    ang = np.concatenate([rows[:, None].astype(np.float32) * freqs, cols[:, None].astype(np.float32) * freqs], 1)
    wide = lambda f: np.tile(np.repeat(f(ang.astype(np.float64)), 2, axis=1), (1, 2)).T
    head = np.kron(np.eye(2), np.ones((HD, HD)))
    c, s = dft(HD)
    ch = np.concatenate([np.kron(np.eye(2), c), np.kron(np.eye(2), s)], 1)
    pairs = [(64 * h + 2 * i, 64 * h + 2 * i + 1) for h in range(2) for i in range(32)]
    c1 = np.concatenate([np.eye(P), np.ones((P, P)), head, rotation(pairs), wide(np.cos), wide(np.sin), ch,
                         level_masks(False), level_masks(True)], 1)
    s, t = np.arange(P)[:, None], np.arange(P)[None, :]
    halves = [(64 * h + i, 64 * h + 32 + i) for h in range(2) for i in range(32)]
    inv_freq = (10000.0 ** (-np.arange(32, dtype=np.float32) / 32)).astype(np.float32)
    c2 = np.concatenate([(s <= t), (s >= t)] + [half_mask(1 << l, back) for back in (False, True) for l in range(LEVELS)]
                        + [np.where(t >= s, 0, NEG), np.zeros((P, P)), np.where(t <= s, 0, NEG), rotation(halves),
                           np.tile(inv_freq, 4)[:, None]], 1)
    assert c1.shape[1] == N_CONST and c2.shape[1] == N_CONST2
    return c1.astype(np.float32), c2.astype(np.float32)


def in_2_order():
    return np.concatenate([head_pairs([h for i in range(4) for h in (i, i + 4)]), np.arange(512, 2816)])


def lay_out(i):
    a = {k: np.asarray(v) for k, v in i.items()}
    lat, ctx = dft_chunks()
    heads = head_pairs((0, 2, 1, 3))
    out_rows = np.concatenate([np.arange(256), 256 + heads, np.arange(512, 1024)])
    dn_rows = np.concatenate([head_pairs([h for k in range(4) for h in (k, k + 4)]), np.arange(512, 1024)])
    stream = [chunks_of(a["w_mod"][0]), chunks_of(a["w_mod"][1])]
    for ly in range(DEPTH):
        stream += [chunks_of(a["w_in"][ly][:, in_order()]), lat.astype(np.float32)]
        stream += [ctx.astype(np.float32)] if ly == 0 else []
        stream += [chunks_of(a["w_out"][ly][out_rows])]
    w_in_2 = a["w_in_2"][0]
    ab = np.zeros((D, P), np.float32)
    ab[:, 0:16] = w_in_2[:, 2816:2832]
    down = np.zeros((24 * P, D), np.float32)
    down[0:2816] = a["w_down_2"][0]
    ckv = a["w_ckv_2"][0]
    gu = a["w_gate_up_2"][0].reshape(D, 2, 22, P).transpose(0, 2, 1, 3).reshape(D, 44 * P)
    stream += [chunks_of(ckv[:, 0:D]), chunks_of(ckv[:, D:]), chunks_of(w_in_2[:, in_2_order()]), chunks_of(ab),
               chunks_of(a["w_out_2"][0][dn_rows]), chunks_of(a["w_cq_2"][0]), chunks_of(a["w_co_2"][0]),
               chunks_of(gu), chunks_of_down(down)]
    weights = np.concatenate(stream, 0)
    assert weights.shape == (PLAN["end"], P, CHUNK)
    wide = lambda v: np.broadcast_to(v.reshape(1, -1), (P, v.size))
    par = {
        "c": np.stack([a["c"][0].reshape(KT, P), a["c_ctx"].reshape(KT, P)], 2).transpose(1, 0, 2).reshape(P, 2 * KT),
        "norm_g": tiles_of_rows(a["norm_g"]), "b_mod": tiles_of_rows(a["b_mod"]), "conv_w": tiles_of_rows(a["conv_w"]),
        "q_g": np.tile(a["q_norm_g"], (1, 2)).T, "k_g": np.tile(a["k_norm_g"], (1, 2)).T,
        "lb": tiles_of_rows(a["hgrn_lb"].transpose(1, 0, 2)), "hg_g": tiles_of_rows(a["hgrn_norm_g"]),
        "final_g": tiles_of_rows(a["final_g"]), "g_mix_pre": tiles_of_rows(a["g_mix_pre_2"]),
        "conv2": a["conv_w_2"][0].reshape(5, 12, P).transpose(2, 1, 0).reshape(P, 60), "a_log": wide(a["a_log_2"]),
        "dt_bias": wide(a["dt_bias_2"]), "g_dn": a["g_dn_out_2"].T, "sink": wide(a["attn_sink_2"]),
        "g_mix_post": tiles_of_rows(a["g_mix_post_2"]), "g_cross_pre": tiles_of_rows(a["g_cross_pre_2"]),
        "g_mem": tiles_of_rows(a["g_mem_2"]), "g_cross_post": tiles_of_rows(a["g_cross_post_2"]),
        "g_ffn_pre": tiles_of_rows(a["g_ffn_pre_2"]), "g_ffn_post": tiles_of_rows(a["g_ffn_post_2"]),
    }
    const, const2 = constants()
    return {
        "tokens": np.concatenate([feature_major(a["x"][0]), feature_major(a["ctx"][0])], 2),
        "mem": feature_major(a["mem_2"][0]), "positions": np.broadcast_to(a["positions_2"], (P, LAT)),
        "weights": weights, "const": const, "const2": const2,
        "par": np.concatenate([par[n] for n in PAR_COLS], 1),
    }


def chunks_of_down(w):
    return w.reshape(3, KT, P, KT, P).transpose(3, 0, 2, 1, 4).reshape(3 * KT, P, CHUNK)


def kernel(**inputs):
    import concourse.bacc as bacc
    from concourse.bass_utils import run_bass_kernel_spmd

    nc = bacc.Bacc("TRN2", target_bir_lowering=False, num_devices=1)
    arrays = {n: np.ascontiguousarray(v) for n, v in lay_out(inputs).items()}
    args = [nc.dram_tensor(n, v.shape, mybir.dt.from_np(v.dtype), kind="ExternalInput").ap() for n, v in arrays.items()]
    out = nc.dram_tensor("out", (P, KT, LAT), F32, kind="ExternalOutput").ap()
    build(nc, *args, out)
    got = run_bass_kernel_spmd(nc, [arrays], core_ids=[0]).results[0]["out"]
    return np.ascontiguousarray(got.transpose(2, 1, 0).reshape(1, LAT, D))
```

```python
from contextlib import ExitStack

import numpy as np

import concourse.bass as bass
from concourse import mybir

F32 = mybir.dt.float32
F32R = mybir.dt.float32r
I32 = mybir.dt.int32
ALU = mybir.AluOpType
ACT = mybir.ActivationFunctionType
AX = mybir.AxisListType

P = 128
D = 1024
KT = D // P
LAT, CTX = 512, 256
TOK = LAT + CTX
CH = 128
NCH, NLAT = TOK // CH, LAT // CH
EPS = 1e-6
DEPTH = 2
HD = 64
RING = 5
CHUNK = KT * P
LEVELS = 7
NEG = -1e30

HQ, HZ, FF, FB, HI, AQ, AK, AV, AZ, FU, FZ, CB, CZ, CC, CV = 0, 2, 4, 6, 8, 10, 12, 13, 14, 16, 18, 20, 22, 24, 26
NPROJ = 28
MIX = [CB, CB + 1, AZ, AZ + 1, HZ, HZ + 1, FZ, FZ + 1]
CTX_TILES_LAST = (FF, FF + 1, FB, FB + 1, HI, HI + 1, AK, AV)

N_MOD = 3 * KT
FOURIER_CHUNKS = {0: NLAT + 1, 1: NLAT}


def chunk_plan():
    at, plan = 0, {}
    for name, n in ([("mod0", N_MOD), ("proj0", NPROJ), ("dft0", FOURIER_CHUNKS[0]), ("mod1", N_MOD), ("out0", KT),
                     ("proj1", NPROJ), ("dft1", FOURIER_CHUNKS[1]), ("out1", KT)]
                    + [("ck", KT), ("cv", KT), ("proj_2", 22), ("ab_2", 1), ("out_2", KT), ("cq", KT), ("co", KT),
                       ("gu", 44), ("down", 3 * KT)]):
        plan[name] = at
        at += n
    plan["end"] = at
    return plan


PLAN = chunk_plan()


def split_plan():
    stages = [("proj0", NPROJ, KT), ("out0", KT, KT), ("proj1", NPROJ, KT), ("out1", KT, KT), ("proj_2", 22, KT),
              ("out_2", KT, KT), ("cq", KT, KT), ("co", KT, KT), ("gu", 44, KT), ("down", 3 * KT, 22)]
    chunks, chunk_at, tile_at, c, t = {}, {}, {}, 0, 0
    for name, n, tiles in stages:
        chunks[name], chunk_at[name], tile_at[name] = n, c, t
        c, t = c + n, t + tiles
    return chunks, chunk_at, tile_at


SPLIT_CHUNKS, SPLIT_AT, TILE_AT = split_plan()


def table(entries):
    at, out = 0, {}
    for name, n in entries:
        out[name] = (at, at + n)
        at += n
    return out, at


CONST_COLS, N_CONST = table([("ident", P), ("ones", P), ("ones_head", P), ("rot_pair", P), ("cos", LAT), ("sin", LAT),
                             ("dft_ch", 2 * P), ("level0", LEVELS * 64), ("level1", LEVELS * 64)])
CONST2_COLS, N_CONST2 = table([("tri0", P), ("tri1", P), ("inv0", LEVELS * P), ("inv1", LEVELS * P),
                               ("window", 3 * P), ("rot_half", P), ("inv_freq", 1)])
PAR_COLS, N_PAR = table([("c", 2 * KT), ("norm_g", DEPTH * KT), ("b_mod", DEPTH * N_MOD), ("conv_w", DEPTH * 6),
                         ("q_g", DEPTH), ("k_g", DEPTH), ("lb", 8), ("hg_g", DEPTH * 2), ("final_g", KT),
                         ("g_mix_pre", KT), ("conv2", 60), ("a_log", 8), ("dt_bias", 8), ("g_dn", 1), ("sink", 8),
                         ("g_mix_post", KT), ("g_cross_pre", KT), ("g_mem", KT), ("g_cross_post", KT),
                         ("g_ffn_pre", KT), ("g_ffn_post", KT)])

SPLIT_STREAM = [PLAN[name] + n for name in SPLIT_CHUNKS for n in range(SPLIT_CHUNKS[name])]


def evacuation_plan():
    at, plan = 0, {}
    for name, n in [("proj0", NPROJ), ("out0", KT), ("proj1", NPROJ), ("out1", KT), ("ck", KT), ("cv", KT),
                    ("proj_2", 22), ("ab_2", 1), ("out_2", KT), ("cq", KT), ("co", KT), ("gu", 44), ("down", KT)]:
        plan[name] = at
        at += n
    return plan


EVAC = evacuation_plan()
N_LAYER0, N_LAYER1, N_FINAL, N_MEM, N_MIX_PRE, N_MIX_POST, N_CROSS_PRE, N_CROSS_POST, N_FFN_PRE, N_FFN_POST = range(10)


def order(back, with_latent=True):
    return [5, 4, 3, 2, 1, 0] if back else [4, 5, 0, 1, 2, 3]


def halves(ap, b):
    return ap.rearrange("p (n two b) -> p n two b", two=2, b=b)


def build(nc, tokens, mem, positions, weights, const_d, const2_d, par_d, out):
    with ExitStack() as ctx:
        def sb(name, shape, dt=F32):
            return ctx.enter_context(nc.sbuf_tensor(name, shape, dt))

        def sem(name):
            return ctx.enter_context(nc.semaphore(name))

        h = sb("h", [P, KT, TOK])
        shapes = {"xn": [P, KT * TOK],
                  "proj": [P, NPROJ, TOK],
                  "ring": [P, RING, CHUNK],
                  "const_sb": [P, N_CONST],
                  "work": [P, 8, TOK],
                  "scratch": [P, 2 * CHUNK],
                  "state": [P, 2, NCH, HD],
                  "qe_2": [P, TOK],
                  "conv_tmp": [P, TOK]}
        with ExitStack() as same_place:
            bufs = {n: same_place.enter_context(nc.sbuf_tensor(n, shape, F32)) for n, shape in shapes.items()}
        rounded_bufs = {n: sb(n + "_r", shape, F32R) for n, shape in shapes.items()}
        xn, proj, ring, const, work, scratch, state, qe_2, conv_tmp = bufs.values()

        def as_r(ap):
            return bass.AP(tensor=rounded_bufs[ap.tensor.name], offset=ap.offset, ap=ap.ap)

        par = sb("par_sb", [P, N_PAR])
        zero = sb("zero", [P, P])
        eps = sb("eps", [P, 1])
        small = sb("small", [P, 520])
        wide_ps = ctx.enter_context(nc.psum_tensor("wide_ps", [P, 2, 1024], F32))
        pair_ps = ctx.enter_context(nc.psum_tensor("pair_ps", [P, 1024], F32))
        duo_ps = ctx.enter_context(nc.psum_tensor("duo_ps", [P, 1024], F32))

        xn_t = xn[:, :].rearrange("p (k t) -> p k t", k=KT)
        cst = {n: const[:, a:b] for n, (a, b) in CONST_COLS.items()}
        prm = {n: par[:, a:b] for n, (a, b) in PAR_COLS.items()}
        c_act = small[:, 0:16]
        mod = small[:, 16:112].rearrange("p (l n s) -> p l n s", l=DEPTH, n=N_MOD)
        mod_scale = small[:, 112:144].rearrange("p (l n s) -> p l n s", l=DEPTH, n=KT)
        lb_e, lb_log, lb_log1m, lb_neg = (small[:, 144 + 4 * n:148 + 4 * n] for n in range(4))
        f_last = small[:, 160:166]
        row_max, neg_max, row_sum, row_inv = (small[:, 168 + 8 * n:176 + 8 * n] for n in range(4))
        masked = scratch[:, 0:4 * LEVELS * 64].rearrange("p (n t) -> p n t", n=4)
        w_lead = scratch[:, :].rearrange("p (n t) -> p n t", n=2)
        state_flat = state[:, :, :, :].rearrange("p d c f -> p (d c f)")
        sq = work[:, 0:2]
        root = work[:, 2]
        resid = work[:, 3:5]
        lf_b, a_b, e_b, m_b, ke_b, kt_b = (work[:, n] for n in range(6))
        v_tok = work[:, 6:8].rearrange("p j t -> p (j t)").rearrange("p (j c f) -> p j c f", j=2, c=NCH)
        k_tok = kt_b.rearrange("p (c f) -> p c f", c=NCH)

        def decay(u, l):
            if u % 2 == 0:
                return xn_t[:, l, :]
            return proj[:, CZ + l, :] if l < LEVELS - 1 else conv_tmp[:, :]

        def q_decayed(u):
            return qe_2[:, :] if u % 2 else xn_t[:, LEVELS, :]


        setup_landed = sem("setup_landed")
        tokens_landed = [sem(f"tokens_landed{n}") for n in range(KT // 2)]
        landed = [sem(f"chunk_landed{n}") for n in range(RING)]
        chunk_used = sem("chunk_used")
        evacuated = sem("evacuated")
        dve_chain, act_chain, pool_chain = sem("dve_chain"), sem("act_chain"), sem("pool_chain")
        ready = sem("fixed_ready")
        c_ready = sem("c_ready")
        mod_ready = sem("mod_ready")
        lb_ready = sem("lb_ready")
        sq_ready, sq_used = sem("sq_ready"), sem("sq_used")
        root_ready, inv_ready = sem("root_ready"), sem("inv_ready")
        scaled = sem("scaled")
        xn_ready = sem("xn_ready")
        h_ready = sem("h_ready")
        gates_ready = sem("gates_ready")
        vt_ps, vt_ready = sem("vt_ps"), sem("vt_ready")
        hg_soft, hg_lf, hg_k, hg_lb, hg_a = sem("hg_soft"), sem("hg_lf"), sem("hg_k"), sem("hg_lb"), sem("hg_a")
        hg_abs = sem("hg_abs")
        hg_ea, hg_qe, hg_ed0, hg_ed, hg_ke = sem("hg_ea"), sem("hg_qe"), sem("hg_ed0"), sem("hg_ed"), sem("hg_ke")
        hg_kt_ps, hg_kt, hg_u, hg_s = sem("hg_kt_ps"), sem("hg_kt"), sem("hg_u"), sem("hg_s")
        lev_diff, lev_exp, lev_ready = sem("lev_diff"), sem("lev_exp"), sem("lev_ready")
        sc_ps, sc_ready, sc_used = sem("sc_ps"), sem("sc_ready"), sem("sc_used")
        hg_o_ps, hg_qk, hg_diag, hg_o, hg_sq, hg_ms, hg_rt, hg_out = (
            sem(n) for n in ("hg_o_ps", "hg_qk", "hg_diag", "hg_o", "hg_sq", "hg_ms", "hg_rt", "hg_out"))
        qk_sq, qk_ms, qk_rt, qk_norm, qk_rot, qk_ready = (
            sem(n) for n in ("qk_sq", "qk_ms", "qk_rt", "qk_norm", "qk_rot", "qk_ready"))
        at_s, at_max, at_exp, at_p, at_pt_ps, at_pt, at_o_ps, at_out = (
            sem(n) for n in ("at_s", "at_max", "at_exp", "at_p", "at_pt_ps", "at_pt", "at_o_ps", "at_out"))
        ft_a_ps, ft_a, ft_y_ps, ft_out = (sem(n) for n in ("ft_a_ps", "ft_a", "ft_y_ps", "ft_out"))
        conv_out = sem("conv_out")
        w_lead_ready, w_split = sem("w_lead_ready"), sem("w_split")
        lead_ready = sem("lead_ready")
        x_lead, x_split = sem("x_lead"), sem("x_split")
        mix_split_lead, mix_split = sem("mix_split_lead"), sem("mix_split")
        final_ready = sem("final_ready")
        stored = sem("stored")

        def width(ly, tile):
            return TOK if ly == 0 or tile in CTX_TILES_LAST else LAT

        def pieces(w):
            return [(0, w)] if w <= LAT else [(0, LAT), (LAT, TOK)]

        def chunk_list(ly):
            return range(NCH) if ly == 0 else range(NLAT)

        def att_units(ly):
            return [(i, r, c) for i in range(2) for r in range(2) for c in chunk_list(ly)]

        def keys_of(c):
            return (0, TOK) if c < NLAT else (LAT, TOK)

        ATT0 = {0: 0, 1: len(att_units(0))}
        SC0 = {u: sum(2 * len(chunk_list(v // 4)) for v in range(u)) for u in range(9)}
        def qk_tiles(ly):
            return [(AQ, width(ly, AQ)), (AQ + 1, width(ly, AQ)), (AK, TOK)]

        def hg_units(ly):
            return [(ly * 4 + 2 * j + d, j, d) for j in range(2) for d in range(2)]

        probs = lambda m: xn[:, TOK * (m % 3):TOK * (m % 3) + TOK]
        probs_t = lambda m: xn[:, TOK * (3 + m % 2):TOK * (4 + m % 2)]
        ft_buf = scratch[:, 0:1024].rearrange("p (t f) -> p t f", t=NLAT)

        def ft_steps(ly):
            return [(s, j, tt) for s in (0, 1)[:2 - ly] for j in range(2) for tt in range((NLAT, 2)[s])]

        FT0 = {0: 0, 1: 12}
        mod_ps = duo_ps[:, 64 * LEVELS:64 * LEVELS + 2 * N_MOD]
        ft_bank = lambda s, j: wide_ps[:, j, :] if s else duo_ps[:, 512 * j:512 * j + 512]


        def lead_tile(k):
            return conv_tmp[:, :] if k == 2 else work[:, k, :]

        def mix_lead(k):
            return (xn_t[:, 5, :], xn_t[:, 6, :], state_flat, xn_t[:, 0, :], xn_t[:, 7, :], work[:, 5, :],
                    conv_tmp[:, :], qe_2[:, :])[k]

        X_SPLITS = {"proj0": 0, "out0": KT, "proj1": KT + 1, "out1": 2 * KT + 1, "proj_2": 2 * KT + 2,
                    "out_2": 3 * KT + 2, "cq": 3 * KT + 6, "gu": 4 * KT + 6, "down": 5 * KT + 6}
        MIX_ORDER = [0, 1, 4, 5, 6, 7, 2, 3]
        flat = proj[:, :, :].rearrange("p n t -> p (n t)")
        spot = [0]

        def place(n):
            spot[0] += n
            return flat[:, spot[0] - n:spot[0]]

        x_2 = h[:, :, 0:LAT]
        mem_x = h[:, :, LAT:TOK]
        tile_2 = place(22 * LAT).rearrange("p (n t) -> p n t", t=LAT)
        const2 = place(N_CONST2)
        cst2 = {n: const2[:, a:b] for n, (a, b) in CONST2_COLS.items()}
        key_c = place(KT * CTX).rearrange("p (k t) -> p k t", k=KT)
        val_c = place(2 * D).rearrange("p (t n) -> p t n", t=2)
        cos_2, sin_2 = place(LAT), place(LAT)
        o_dn = place(4 * LAT).rearrange("p (h t) -> p h t", h=4)
        q_c, o_c = tile_2[:, 0:KT, :], tile_2[:, KT:2 * KT, :]
        y_2 = xn_t[:, :, 0:LAT]
        pos_i = state_flat[:, 0:LAT].bitcast(I32)
        conv_y = [state_flat[:, 0:LAT], qe_2[:, 0:LAT]]
        up_2 = conv_y

        def mix2_lead(k):
            return tile_2[:, DQ2 + k, :]

        def hidden_lead(t):
            return flat[:, (22 + t) * LAT:(23 + t) * LAT] if t < 20 else cst[("cos", "sin")[t - 20]]

        quad = lambda m: wide_ps[:, m // 2 % 2, 512 * (m % 2):512 * (m % 2) + 512]
        twin = lambda m: pair_ps[:, 512 * (m % 2):512 * (m % 2) + 512]
        half_pi = small[:, 210:211]
        row_max2, neg_max2, row_sum2, row_inv2, sink_e = (small[:, 212 + 4 * n:216 + 4 * n] for n in range(5))
        ab = small[:, 240:304].rearrange("p (c n) -> p c n", c=NLAT)
        g_tok, g_soft, beta, g_cum, g_exp, beta_g = (
            small[:, 304 + 32 * n:336 + 32 * n].rearrange("p (c n) -> p c n", c=NLAT) for n in range(6))
        a_exp = small[:, 496:504]
        g_end = small[:, 504:512].rearrange("p (d n) -> p d n", d=2)
        s_decay = small[:, 512:520].rearrange("p (d n) -> p d n", d=2)
        dn_store = [xn[:, :].rearrange("p (n h t) -> p n h t", n=12, h=4),
                    work[:, :, :].rearrange("p n t -> p (n t)").rearrange("p (n h t) -> p n h t", n=12, h=4)]
        XT, T, R, Y, XM, QK, KBG, VB, KG, WT, VN, QG = range(12)
        s_dn = scratch[:, 0:1024].rearrange("p (d h v) -> p d h v", d=2, h=4)

        def dn(d, name):
            return dn_store[d][:, name]

        def dn_bank(d, n):
            ps = (wide_ps[:, n // 2, 512 * (n % 2):512 * (n % 2) + 512] if d == 0
                  else (pair_ps, duo_ps)[n // 2][:, 512 * (n % 2):512 * (n % 2) + 512])
            return ps.rearrange("p (h t) -> p h t", h=4)

        def chunk_at(d, s):
            return s if d == 0 else NLAT - 1 - s

        AQ2, AK2, AV2, DQ2, DK2, DV2, DG2 = 0, 4, 5, 6, 10, 14, 18
        MIX2 = [0, 1, 2, 3, DG2, DG2 + 1, DG2 + 2, DG2 + 3]
        WIN = [(i, r, c) for i in range(4) for r in range(2) for c in range(NLAT)]
        CROSS = [(hd, c) for hd in range(4) for c in range(NLAT)]

        def window_keys(c):
            a, b = max(c - 1, 0), min(c + 2, NLAT)
            return a * P, b * P, (a - c + 1) * P, (b - c + 1) * P

        const2_landed, mem_landed, pos_landed = sem("const2_landed"), sem("mem_landed"), sem("pos_landed")
        x_ready = sem("x_ready")
        rope_arg, rope_table = sem("rope_arg"), sem("rope_table")
        cv_sum, cv_ready, dgate_ready = sem("cv_sum"), sem("cv_ready"), sem("dgate_ready")
        l2_sq, l2_ss, l2_rt, l2_ready = sem("l2_sq"), sem("l2_ss"), sem("l2_rt"), sem("l2_ready")
        rp_rot, rp_ready = sem("rp_rot"), sem("rp_ready")
        v2_ps, v2_ready = sem("v2_ps"), sem("v2_ready")
        w_s, w_max, w_exp, w_p, w_pt_ps, w_pt, w_o_ps, w_out_s = (
            sem(n) for n in ("w_s", "w_max", "w_exp", "w_p", "w_pt_ps", "w_pt", "w_o_ps", "w_out"))
        g_x, g_l, g_ready, g_ps, g_c, g_e, g_b = (sem(n) for n in ("g_x", "g_l", "g_ready", "g_ps", "g_c", "g_e", "g_b"))
        dn_a, dn_diff, dn_exp, dn_x, dn_row, dn_tok_ps, dn_tok = (
            sem(n) for n in ("dn_a", "dn_diff", "dn_exp", "dn_x", "dn_row", "dn_tok_ps", "dn_tok"))
        dn_qg, dn_xm, dn_y_ps, dn_y, dn_z_ps, dn_t = (sem(n) for n in ("dn_qg", "dn_xm", "dn_y_ps", "dn_y", "dn_z_ps", "dn_t"))
        dn_w_ps, dn_w, dn_v_ps, dn_v, dn_o_ps, dn_s = (sem(n) for n in ("dn_w_ps", "dn_w", "dn_v_ps", "dn_v", "dn_o_ps", "dn_s"))
        do_sq, do_ss, do_rt, do_out = (sem(n) for n in ("do_sq", "do_ss", "do_rt", "do_out"))
        c_s, c_max, c_exp, c_p, c_pt_ps, c_pt, c_o_ps, c_out = (
            sem(n) for n in ("c_s", "c_max", "c_exp", "c_p", "c_pt_ps", "c_pt", "c_o_ps", "c_out"))
        ffn_ready = sem("ffn_ready")

        block = ctx.enter_context(nc.Block())

        @block.sync
        def _(sp):
            sp.dma_start(par[:, :], par_d).then_inc(setup_landed, 16)
            sp.dma_start(const[:, :], const_d).then_inc(setup_landed, 16)
            lead = -(-(N_MOD + 1) // RING) * RING
            for c in range(lead):
                if c >= RING:
                    sp.wait_ge(chunk_used, c - RING + 1)
                sp.dma_start(ring[:, c % RING, :], weights[c]).then_inc(landed[c % RING], 16)
                if c < KT // 2:
                    part = slice(2 * c, 2 * c + 2)
                    sp.dma_start(h[:, part, :], tokens[:, part, :]).then_inc(tokens_landed[c], 16)
            turns = (PLAN["end"] - lead) // RING
            with sp.Fori(0, turns) as turn:
                for s in range(RING):
                    sp.wait_ge(chunk_used, turn * RING + (lead - RING + s + 1))
                    sp.dma_start(ring[:, s, :], weights[turn * RING + (lead + s)]).then_inc(landed[s], 16)
            for c in range(lead + turns * RING, PLAN["end"]):
                sp.wait_ge(chunk_used, c - RING + 1)
                sp.dma_start(ring[:, c % RING, :], weights[c]).then_inc(landed[c % RING], 16)
            sp.wait_ge(final_ready, KT)
            sp.dma_start(out, h[:, :, 0:LAT]).then_inc(stored, 16)
            sp.wait_ge(stored, 16)

        @block.gpsimd
        def _(pool):
            def link(ins):
                pool_count[0] += 1
                ins.then_inc(pool_chain, 1)
                pool.wait_ge(pool_chain, pool_count[0])

            pool_count = [0]
            pool.memset(zero[:, :], 0.0).then_inc(ready, 1)
            pool.memset(eps[:, :], EPS).then_inc(ready, 1)

            lead_count = [0]

            def split(src, lead, done):
                lead_count[0] += 1
                pool.tensor_copy(as_r(lead), src).then_inc(lead_ready, 1)
                pool.wait_ge(lead_ready, lead_count[0])
                pool.tensor_tensor(as_r(src), src, as_r(lead).bitcast(F32), ALU.subtract).then_inc(done, 1)

            def split_weights(stage, chunks=None):
                for n in chunks or range(SPLIT_CHUNKS[stage]):
                    c, m = PLAN[stage] + n, SPLIT_AT[stage] + n
                    pool.wait_ge(w_lead_ready, m + 1)
                    wt = ring[:, c % RING, :]
                    pool.tensor_tensor(as_r(wt), wt, as_r(w_lead[:, m % 2, :]).bitcast(F32), ALU.subtract).then_inc(w_split, 1)

            def split_mix(ly):
                w = width(ly, HQ)
                split_weights(f"out{ly}", range(2))
                pool.wait_ge(hg_out, 2 * ly + 2)
                for k in MIX_ORDER[0:6]:
                    split(proj[:, MIX[k], 0:w], mix_lead(k)[:, 0:w], mix_split)
                pool.wait_ge(at_out, ATT0[ly] + len(att_units(ly)) // 2)
                split(proj[:, AZ, 0:w], mix_lead(2)[:, 0:w], mix_split)
                split_weights(f"out{ly}", range(2, KT))

            def conv(ly):
                w = width(ly, CB)
                taps = prm["conv_w"].rearrange("p (l t j) -> p l t j", l=DEPTH, t=3)
                for j in range(2):
                    cb, cc, cv, cz, tmp = proj[:, CB + j, 0:w], proj[:, CC + j, 0:w], proj[:, CV + j, 0:w], proj[:, CZ + j, 0:w], conv_tmp[:, 0:w]
                    pool.wait_ge(evacuated, EVAC[f"proj{ly}"] + NPROJ)
                    pool.wait_ge(gates_ready, 2 * ly + 2)
                    link(pool.tensor_tensor(cc, cc, cv, ALU.mult))
                    link(pool.tensor_scalar(cv, cc, taps[:, ly, 1, j:j + 1], None, ALU.mult))
                    for tap, to, frm in ((0, 1, 0), (2, 0, 1)):
                        link(pool.tensor_scalar(tmp, cc, taps[:, ly, tap, j:j + 1], None, ALU.mult))
                        for a, b in pieces(w):
                            n = b - a - 1
                            link(pool.tensor_tensor(cv[:, a + to:a + to + n], cv[:, a + to:a + to + n],
                                                    tmp[:, a + frm:a + frm + n], ALU.add))
                    link(pool.tensor_tensor(cv, cv, cb, ALU.mult))
                    pool.tensor_tensor(cb, cv, cz, ALU.mult).then_inc(conv_out, 1)
                    pool.wait_ge(conv_out, 2 * ly + j + 1)

            def level_differences(u, d, ly):
                w = TOK if ly == 0 else LAT
                pool.wait_ge(hg_a, u + 1)
                if u >= 2:
                    pool.wait_ge(sc_ps, SC0[u - 1])
                for l in range(LEVELS):
                    b = 1 << l
                    a, o = halves(a_b[:, 0:w], b), halves(decay(u, l)[:, 0:w], b)
                    q, k = (1, 0) if d == 0 else (0, 1)
                    ref = a[:, :, 0, b - 1:b] if d == 0 else a[:, :, 1, 0:1]
                    ref = ref.broadcast_to([P, w // (2 * b), b])
                    pool.tensor_tensor(o[:, :, q, :], a[:, :, q, :], ref, ALU.subtract).then_inc(lev_diff, 1)
                    pool.tensor_tensor(o[:, :, k, :], ref, a[:, :, k, :], ALU.subtract).then_inc(lev_diff, 1)

            def diagonal(ly, j):
                w = width(ly, HQ)
                u = ly * 4 + 2 * j + 1
                pool.wait_ge(lev_ready, LEVELS * (u + 1))
                pool.wait_ge(hg_ke, u + 1)
                link(pool.tensor_tensor(proj[:, FF + j, 0:w], proj[:, FF + j, 0:w], proj[:, FB + j, 0:w], ALU.add))
                pool.tensor_tensor(proj[:, FF + j, 0:w], proj[:, FF + j, 0:w], proj[:, HQ + j, 0:w], ALU.mult).then_inc(hg_qk, 1)

            for ly in range(DEPTH):
                split_weights(f"proj{ly}")
                for u, j, d in hg_units(ly):
                    level_differences(u, d, ly)
                    if d == 1:
                        diagonal(ly, j)
                    if u % 4 == 0:
                        conv(ly)
                        pool.wait_ge(conv_out, 2 * ly + 2)
                split_mix(ly)
            split_weights("proj_2")
            for s in range(NLAT):
                for l in range(LEVELS):
                    for d in range(2):
                        g, c = 2 * s + d, chunk_at(d, s)
                        if l == 0:
                            pool.wait_ge(dn_x, 2 * g + 2)
                        elif l == 1:
                            pool.wait_ge(dn_t, 2 * (LEVELS * s) + d + 1)
                        else:
                            pool.wait_ge(dn_y_ps, 2 * (6 * s + l - 2) + d + 1)
                        mask = cst2[f"inv{d}"][:, l * P:(l + 1) * P].unsqueeze(1).broadcast_to([P, 4, CH])
                        pool.tensor_tensor(dn(d, XM), dn(d, XT), mask, ALU.mult).then_inc(dn_xm, 1)
                        if l == 0:
                            q = tile_2[:, DQ2:DQ2 + 4, c * CH:(c + 1) * CH]
                            pool.tensor_tensor(dn(d, QG), dn(d, QG), q, ALU.mult).then_inc(dn_qg, 1)
                            pool.tensor_tensor(dn(d, QK), dn(d, QK), cst2[f"tri{d}"].unsqueeze(1).broadcast_to([P, 4, CH]),
                                               ALU.mult).then_inc(dn_qg, 1)
            pool.wait_ge(dn_s, 2 * NLAT)
            split_weights("out_2", range(2))
            for k in range(4):
                split(tile_2[:, MIX2[k], :], mix2_lead(k), mix_split)
            split_weights("out_2", range(2, KT))
            split_weights("cq")
            split_weights("co", range(2))
            for k in range(KT):
                pool.wait_ge(c_out, NLAT * (k // 2 + 1))
                split(o_c[:, k, :], lead_tile(k)[:, 0:LAT], mix_split)
            split_weights("co", range(2, KT))
            for stage in ("gu", "down"):
                split_weights(stage)

        @block.scalar
        def _(act):
            act_count = [0]

            def link(ins):
                act_count[0] += 1
                ins.then_inc(act_chain, 1)
                act.wait_ge(act_chain, act_count[0])

            def norm_root(n, src, w, source_ready):
                for k in range(KT):
                    source_ready(k)
                    if 8 * n + k >= 2:
                        act.wait_ge(sq_used, 8 * n + k - 1)
                    act.activation(sq[:, k % 2, 0:w], src(k), ACT.Square).then_inc(sq_ready, 1)
                act.wait_ge(sq_used, 8 * (n + 1))
                if n:
                    act.wait_ge(scaled, 8 * n)
                act.activation(root[:, 0:w], pair_ps[:, 0:w], ACT.Sqrt, bias=eps[:, 0:1],
                               scale=1.0 / D).then_inc(root_ready, 1)

            def evacuate(stage, tile, chunks, w, dst, func=ACT.Copy):
                g = EVAC[stage] + tile
                act.wait_ge(chunk_used, chunks)
                act.activation(dst, wide_ps[:, g % 2, 0:w], func).then_inc(evacuated, 1)
                act.wait_ge(evacuated, g + 1)

            def weight_leads(stage, n, count=1):
                for i in range(n, n + count):
                    c, m = PLAN[stage] + i, SPLIT_AT[stage] + i
                    act.wait_ge(landed[c % RING], 16 * (c // RING + 1))
                    if m >= 2:
                        act.wait_ge(chunk_used, SPLIT_STREAM[m - 2] + 1)
                    act.activation(as_r(w_lead[:, m % 2, :]), ring[:, c % RING, :], ACT.Copy).then_inc(w_lead_ready, 1)

            def leads_after(stage, tile, following=None):
                n = SPLIT_CHUNKS[stage]
                step = 3 if stage == "down" else 1
                for i in range(step * tile + 2, step * tile + 2 + step):
                    if i < n:
                        weight_leads(stage, i)
                    elif following:
                        weight_leads(following, i - n)

            def modulate(ly):
                act.wait_ge(mod_ready, 2 * (ly + 1))
                for k in range(KT):
                    act.wait_ge(scaled, 8 * ly + k + 1)
                    for s, (a, b) in enumerate(pieces(TOK)):
                        act.activation(xn_t[:, k, a:b], xn_t[:, k, a:b], ACT.Identity, bias=mod[:, ly, k, s:s + 1],
                                       scale=mod_scale[:, ly, k, s:s + 1]).then_inc(xn_ready, 1)

            def lower_bounds():
                act.wait_ge(lb_ready, 1)
                link(act.activation(lb_log, lb_e, ACT.Abs))
                link(act.activation(lb_log, lb_log, ACT.Exp, scale=-1.0))
                act.activation(lb_log, lb_log, ACT.Ln, bias=1.0).then_inc(lb_ready, 1)

            def softplus(u, j, d):
                z = proj[:, (FF, FB)[d] + j, :]
                if u % 4:
                    act.wait_ge(hg_ke, u)
                link(act.activation(e_b, z, ACT.Abs))
                link(act.activation(e_b, e_b, ACT.Exp, scale=-1.0))
                act.activation(e_b, e_b, ACT.Ln, bias=1.0).then_inc(hg_soft, 1)

            def hgrn_unit(ly, u, j, d):
                z = proj[:, (FF, FB)[d] + j, :]
                if u % 4:
                    softplus(u, j, d)
                act.wait_ge(hg_lf, u + 1)
                bias = 0.0 if ly == 0 else lb_log1m[:, 2 * d + j:2 * d + j + 1]
                act.activation(z, m_b, ACT.Exp, bias=bias, scale=-1.0).then_inc(hg_k, 1)
                if ly == 1:
                    act.wait_ge(hg_lb, 2 * (u - 4) + 1)
                    link(act.activation(e_b, lf_b, ACT.Abs, bias=lb_neg[:, 2 * d + j:2 * d + j + 1]))
                    link(act.activation(e_b, e_b, ACT.Exp, scale=-1.0))
                    act.activation(e_b, e_b, ACT.Ln, bias=1.0).then_inc(hg_abs, 1)
                act.wait_ge(hg_a, u + 1)
                act.wait_ge(hg_k, u + 1)
                act.activation(m_b, a_b, ACT.Exp).then_inc(hg_ea, 1)
                last = a_b.rearrange("p (c t) -> p c t", t=CH)[:, :, CH - 1 if d == 0 else 0]
                act.activation(f_last, last, ACT.Exp).then_inc(hg_ea, 1)
                act.wait_ge(hg_ed0, u + 1)
                act.activation(e_b, e_b, ACT.Exp).then_inc(hg_ed, 1)
                w = TOK if ly == 0 else LAT
                for l in range(LEVELS):
                    act.wait_ge(lev_diff, 2 * (LEVELS * u + l + 1))
                    act.activation(decay(u, l)[:, 0:w], decay(u, l)[:, 0:w], ACT.Exp).then_inc(lev_exp, 1)
                    if l == 1 and u % 4 == 3:
                        head_root(ly, 0)
                    if l == 2:
                        act.wait_ge(hg_kt_ps, u + 1)
                        act.activation(kt_b, wide_ps[:, 0, 0:TOK], ACT.Copy).then_inc(hg_kt, 1)

            def head_square(ly, j):
                n = 2 * ly + j
                w = width(ly, HQ)
                act.wait_ge(hg_o, n + 1)
                act.activation(proj[:, HI + j, 0:w], proj[:, FF + j, 0:w], ACT.Square).then_inc(hg_sq, 1)

            def head_root(ly, j):
                n = 2 * ly + j
                w = width(ly, HQ)
                act.wait_ge(hg_ms, n + 1)
                act.activation(proj[:, FB + j, 0:w], wide_ps[:, 1, 0:w], ACT.Sqrt, bias=eps[:, 0:1], scale=1.0 / HD).then_inc(hg_rt, 1)

            def attention(ly):
                for n, (t, w) in enumerate(qk_tiles(ly)):
                    m = 3 * ly + n
                    if n:
                        act.wait_ge(qk_norm, m)
                    else:
                        act.wait_ge(hg_out, 2 * ly + 2)
                    act.activation(e_b[:, 0:w], proj[:, t, 0:w], ACT.Square).then_inc(qk_sq, 1)
                    act.wait_ge(qk_ms, m + 1)
                    act.activation(m_b[:, 0:w], pair_ps[:, 0:w], ACT.Sqrt, bias=eps[:, 0:1], scale=1.0 / HD).then_inc(qk_rt, 1)
                act.wait_ge(vt_ps, 3 * ly + 3)
                act.activation(v_tok[:, 0], pair_ps[:, 0:TOK].rearrange("p (c f) -> p c f", c=NCH), ACT.Copy).then_inc(vt_ready, 1)
                units = att_units(ly)
                for n in range(len(units) + 2):
                    if n >= 2:
                        probs_transposed(ATT0[ly] + n - 2, keys_of(units[n - 2][2]))
                    if n >= len(units):
                        continue
                    m = ATT0[ly] + n
                    a, b = keys_of(units[n][2])
                    act.wait_ge(at_max, m + 1)
                    if n >= 3:
                        act.wait_ge(at_pt_ps, m - 2)
                    act.activation(probs(m)[:, a:b], wide_ps[:, m % 2, a:b], ACT.Exp, bias=neg_max[:, m % 4:m % 4 + 1],
                                   scale=HD ** -0.5, accum_out=row_sum[:, m % 4:m % 4 + 1]).then_inc(at_exp, 1)

            def probs_transposed(m, keys):
                a, b = keys
                act.wait_ge(at_pt_ps, m + 1)
                if m >= 2:
                    act.wait_ge(at_o_ps, m - 1)
                act.activation(probs_t(m)[:, a:b], pair_ps[:, a:b], ACT.Copy).then_inc(at_pt, 1)

            def fourier(ly):
                for n, (s, j, tt) in enumerate(ft_steps(ly)):
                    m = FT0[ly] + n
                    act.wait_ge(ft_a_ps, m + 1)
                    if tt == 0:
                        act.wait_ge(ft_y_ps, 4 * ly + 2 * s + j) if ly or s or j else None
                    act.activation(ft_buf[:, tt, :], pair_ps[:, 512 * (m % 2):512 * (m % 2) + 256], ACT.Copy).then_inc(ft_a, 1)

            def output(ly):
                for n in range(KT):
                    leads_after(f"out{ly}", n, "proj1" if ly == 0 else None)
                    g = EVAC[f"out{ly}"] + n
                    act.wait_ge(chunk_used, PLAN[f"out{ly}"] + n + 1)
                    if 8 * ly + n >= 2:
                        act.wait_ge(h_ready, 8 * ly + n - 1)
                    w = width(ly, HQ)
                    for s, (a, b) in enumerate(pieces(w)):
                        ins = act.activation(resid[:, n % 2, a:b], wide_ps[:, g % 2, a:b], ACT.Copy,
                                             scale=mod[:, ly, 2 * KT + n, s:s + 1])
                        if b == w:
                            ins.then_inc(evacuated, 1)

            act.wait_ge(setup_landed, 32)
            act.wait_ge(ready, 2)
            act.activation(c_act, prm["c"], ACT.Silu).then_inc(c_ready, 1)
            lower_bounds()
            for ly in range(DEPTH):
                w = TOK
                norm_root(ly, lambda k: h[:, k, :], TOK,
                          (lambda k: act.wait_ge(tokens_landed[k // 2], 16)) if ly == 0 else (lambda k: act.wait_ge(h_ready, k + 1)))
                if ly == 0:
                    weight_leads("proj0", 0, 2)
                modulate(ly)
                for t in range(NPROJ):
                    leads_after(f"proj{ly}", t)
                    evacuate(f"proj{ly}", t, PLAN[f"proj{ly}"] + t + 1, width(ly, t), proj[:, t, 0:width(ly, t)])
                    if t == HZ + 1:
                        act.activation(proj[:, HQ:HZ + 2, 0:width(ly, HQ)], proj[:, HQ:HZ + 2, 0:width(ly, HQ)],
                                       ACT.Silu).then_inc(gates_ready, 1)
                wl = width(ly, AZ)
                link(act.activation(proj[:, AZ:AZ + 2, 0:wl], proj[:, AZ:AZ + 2, 0:wl], ACT.Silu))
                link(act.activation(proj[:, FZ:FZ + 2, 0:wl], proj[:, FZ:FZ + 2, 0:wl], ACT.Silu))
                act.activation(proj[:, CZ:CZ + 2, 0:wl], proj[:, CZ:CZ + 2, 0:wl], ACT.Silu).then_inc(gates_ready, 1)
                act.wait_ge(gates_ready, 2 * ly + 2)
                for j in range(2):
                    act.wait_ge(vt_ps, 3 * ly + j + 1)
                    act.activation(v_tok[:, j], duo_ps[:, 0:TOK].rearrange("p (c f) -> p c f", c=NCH), ACT.Copy).then_inc(vt_ready, 1)
                softplus(4 * ly, 0, 0)
                fourier(ly)
                for u, j, d in hg_units(ly):
                    if u % 4 == 3:
                        head_square(ly, 0)
                    hgrn_unit(ly, u, j, d)
                head_square(ly, 1)
                head_root(ly, 1)
                act.wait_ge(sc_used, SC0[4 * ly + 4])
                weight_leads(f"out{ly}", 0, 2)
                attention(ly)
                output(ly)
            act.wait_ge(scaled, 16)
            act.dma_start(mem_x, mem).then_inc(mem_landed, 16)
            act.wait_ge(chunk_used, PLAN["out1"] + KT)
            act.dma_start(const2, const2_d).then_inc(const2_landed, 16)
            act.wait_ge(hg_out, 4)
            act.wait_ge(chunk_used, PLAN["out1"] + KT)
            act.dma_start(pos_i, positions).then_inc(pos_landed, 16)
            norm_root(N_FINAL, lambda k: h[:, k, 0:LAT], LAT, lambda k: act.wait_ge(h_ready, KT + k + 1))
            norm_root(N_MEM, lambda k: mem_x[:, k, :], CTX, lambda k: act.wait_ge(mem_landed, 16))
            norm_root(N_MIX_PRE, lambda k: x_2[:, k, :], LAT, lambda k: act.wait_ge(scaled, 8 * N_FINAL + k + 1))
            for n in range(KT):
                evacuate("ck", n, PLAN["ck"] + n + 1, CTX, key_c[:, n, :])
            for n in range(KT):
                g = EVAC["cv"] + n
                act.wait_ge(chunk_used, PLAN["cv"] + n + 1)
                act.activation(val_c[:, :, n * P:(n + 1) * P], wide_ps[:, g % 2, 0:2 * P].rearrange("p (t n) -> p t n", t=2),
                               ACT.Copy).then_inc(evacuated, 1)
                if n == KT - 3:
                    weight_leads("proj_2", 0, 2)
            act.wait_ge(rope_arg, 2)
            link(act.activation(cos_2, sin_2, ACT.Abs))
            link(act.activation(cos_2, cos_2, ACT.Sin, bias=half_pi, scale=-1.0))
            act.activation(sin_2, sin_2, ACT.Sin).then_inc(rope_table, 1)
            for t in range(22):
                leads_after("proj_2", t)
                evacuate("proj_2", t, PLAN["proj_2"] + t + 1, LAT, tile_2[:, t, :])
                q = t - DQ2 - 2
                if 0 <= q < 12:
                    act.wait_ge(cv_sum, q + 1)
                    act.activation(tile_2[:, DQ2 + q, :], conv_y[q % 2], ACT.Silu).then_inc(cv_ready, 1)
            evacuate("ab_2", 0, PLAN["ab_2"] + 1, 64, small[:, 240:304])
            act.wait_ge(evacuated, EVAC["ab_2"] + 1)
            act.activation(tile_2[:, DG2:DG2 + 4, :], tile_2[:, DG2:DG2 + 4, :], ACT.Silu).then_inc(dgate_ready, 1)
            act.wait_ge(g_x, 1)
            act.activation(beta, ab[:, :, 8:16], ACT.Sigmoid).then_inc(g_l, 1)
            link(act.activation(g_soft, g_tok, ACT.Abs))
            link(act.activation(g_soft, g_soft, ACT.Exp, scale=-1.0))
            act.activation(g_soft, g_soft, ACT.Ln, bias=1.0).then_inc(g_l, 1)
            act.activation(a_exp, prm["a_log"], ACT.Exp).then_inc(g_l, 1)
            act.wait_ge(g_c, 2)
            act.activation(g_exp, g_cum, ACT.Exp).then_inc(g_e, 1)
            for n in range(8):
                act.wait_ge(cv_ready, n + 1)
                if n >= 2:
                    act.wait_ge(l2_ss, n - 1)
                act.activation(sq[:, n % 2, 0:LAT], tile_2[:, DQ2 + n, :], ACT.Square).then_inc(l2_sq, 1)
                act.wait_ge(l2_ss, n + 1)
                if n >= 2:
                    act.wait_ge(l2_ready, n - 1)
                act.activation(work[:, 2 + n % 2, 0:LAT], pair_ps[:, 512 * (n % 2):512 * (n % 2) + LAT], ACT.Sqrt,
                               bias=eps[:, 0:1]).then_inc(l2_rt, 1)
            act.wait_ge(v2_ps, 1)
            act.activation(v_tok[:, 0, 0:NLAT, :], duo_ps[:, 0:LAT].rearrange("p (c f) -> p c f", c=NLAT), ACT.Copy).then_inc(v2_ready, 1)

            def window_transposed(m):
                a, b, _, _ = window_keys(WIN[m][2])
                act.wait_ge(w_pt_ps, m + 1)
                if m >= 2:
                    act.wait_ge(w_o_ps, m - 1)
                act.activation(probs_t(m)[:, 0:b - a], twin(m)[:, 0:b - a], ACT.Copy).then_inc(w_pt, 1)

            for m in range(len(WIN) + 2):
                if m >= 2:
                    window_transposed(m - 2)
                if m >= len(WIN):
                    continue
                i, r, c = WIN[m]
                a, b, _, _ = window_keys(c)
                one = slice(m % 4, m % 4 + 1)
                act.wait_ge(w_max, m + 1)
                p = probs(m)[:, 0:b - a]
                act.activation(p, p, ACT.Exp, bias=neg_max2[:, one], accum_out=row_sum2[:, one]).then_inc(w_exp, 1)
                act.activation(sink_e[:, one], prm["sink"][:, i + 4 * r:i + 4 * r + 1], ACT.Exp,
                               bias=neg_max2[:, one]).then_inc(w_exp, 1)
            for s in range(NLAT):
                for d in range(2):
                    g = 2 * s + d
                    last = CH - 1 if d == 0 else 0
                    act.wait_ge(dn_diff, g + 1)
                    act.activation(dn(d, XM), dn(d, XM), ACT.Exp).then_inc(dn_exp, 1)
                    act.activation(g_end[:, d], g_end[:, d], ACT.Exp).then_inc(dn_exp, 1)
                    act.activation(dn(d, QG), dn_bank(d, 0), ACT.Exp).then_inc(dn_exp, 1)
                    act.activation(s_decay[:, d], dn_bank(d, 0)[:, :, last], ACT.Exp).then_inc(dn_exp, 1)
                for l in range(1, LEVELS):
                    for d in range(2):
                        at = 2 * (6 * s + l - 1) + d
                        act.wait_ge(dn_y_ps, at + 1)
                        act.activation(dn(d, Y), dn_bank(d, 3), ACT.Copy).then_inc(dn_y, 1)
                for d in range(2):
                    act.wait_ge(dn_w_ps, 2 * s + d + 1)
                    act.activation(dn(d, WT), dn_bank(d, 0), ACT.Copy, scale=-1.0).then_inc(dn_w, 1)
                for d in range(2):
                    act.wait_ge(dn_v_ps, 2 * s + d + 1)
                    act.activation(dn(d, VN), dn_bank(d, 1), ACT.Copy).then_inc(dn_v, 1)
            act.wait_ge(dn_s, 2 * NLAT)
            for n in range(4):
                if n >= 2:
                    act.wait_ge(do_ss, n - 1)
                act.activation(sq[:, n % 2, 0:LAT], o_dn[:, n, :], ACT.Square).then_inc(do_sq, 1)
                act.wait_ge(do_ss, n + 1)
                if n >= 2:
                    act.wait_ge(do_out, n - 1)
                act.activation(work[:, 2 + n % 2, 0:LAT], pair_ps[:, 512 * (n % 2):512 * (n % 2) + LAT], ACT.Sqrt,
                               bias=eps[:, 0:1], scale=1.0 / P).then_inc(do_rt, 1)

            weight_leads("out_2", 0, 2)

            def closed(stage, n, chunks, following=None):
                for t in range(KT):
                    leads_after(stage, t, following)
                    evacuate(stage, t, PLAN[stage] + chunks * (t + 1), LAT, y_2[:, t, :])
                norm_root(n, lambda k: y_2[:, k, :], LAT, lambda k: None)

            closed("out_2", N_MIX_POST, 1, "cq")
            norm_root(N_CROSS_PRE, lambda k: x_2[:, k, :], LAT, lambda k: act.wait_ge(x_ready, k + 1))
            for t in range(KT):
                leads_after("cq", t, "co")
                evacuate("cq", t, PLAN["cq"] + t + 1, LAT, q_c[:, t, :])
            for m in range(len(CROSS) + 2):
                if m >= 2:
                    act.wait_ge(c_pt_ps, m - 1)
                    if m >= 4:
                        act.wait_ge(c_o_ps, m - 3)
                    act.activation(probs_t(m - 2)[:, 0:CTX], twin(m - 2)[:, 0:CTX], ACT.Copy).then_inc(c_pt, 1)
                if m < len(CROSS):
                    one = slice(m % 4, m % 4 + 1)
                    act.wait_ge(c_max, m + 1)
                    if m >= 3:
                        act.wait_ge(c_pt_ps, m - 2)
                    act.activation(probs(m)[:, 0:CTX], quad(m)[:, 0:CTX], ACT.Exp, bias=neg_max2[:, one],
                                   scale=256 ** -0.5, accum_out=row_sum2[:, one]).then_inc(c_exp, 1)
            closed("co", N_CROSS_POST, 1, "gu")
            norm_root(N_FFN_PRE, lambda k: x_2[:, k, :], LAT, lambda k: act.wait_ge(x_ready, KT + k + 1))
            for t in range(44):
                leads_after("gu", t, "down")
                if t % 2 == 0:
                    evacuate("gu", t, PLAN["gu"] + t + 1, LAT, tile_2[:, t // 2, :], ACT.Silu)
                else:
                    if t >= 5:
                        act.wait_ge(ffn_ready, t // 2 - 1)
                    evacuate("gu", t, PLAN["gu"] + t + 1, LAT, up_2[t // 2 % 2])
            closed("down", N_FFN_POST, 3)

        @block.vector
        def _(dve):
            dve_count = [0]

            def link(ins):
                dve_count[0] += 1
                ins.then_inc(dve_chain, 1)
                dve.wait_ge(dve_chain, dve_count[0])

            def reciprocal_root(n, w):
                dve.wait_ge(root_ready, n + 1)
                dve.reciprocal(root[:, 0:w], root[:, 0:w]).then_inc(inv_ready, 1)
                dve.wait_ge(inv_ready, n + 1)

            def modulation(ly):
                dve.wait_ge(chunk_used, PLAN[f"mod{ly}"] + N_MOD)
                bias = prm["b_mod"][:, ly * N_MOD:(ly + 1) * N_MOD].unsqueeze(2).broadcast_to([P, N_MOD, 2])
                dve.tensor_tensor(mod[:, ly], mod_ps.rearrange("p (n s) -> p n s", s=2), bias,
                                  ALU.add).then_inc(mod_ready, 1)
                dve.wait_ge(mod_ready, 2 * ly + 1)
                gain = prm["norm_g"][:, ly * KT:(ly + 1) * KT].unsqueeze(2).broadcast_to([P, KT, 2])
                dve.scalar_tensor_tensor(out=mod_scale[:, ly], in0=mod[:, ly, KT:2 * KT], scalar=1.0, in1=gain, op0=ALU.add,
                                         op1=ALU.mult).then_inc(mod_ready, 1)

            x_count = [0]

            def split(src, lead):
                x_count[0] += 1
                dve.tensor_copy(as_r(lead), src).then_inc(x_lead, 1)
                dve.wait_ge(x_lead, x_count[0])
                dve.tensor_tensor(as_r(src), src, as_r(lead).bitcast(F32), ALU.subtract).then_inc(x_split, 1)

            def lower_bounds():
                dve.wait_ge(setup_landed, 32)
                dve.tensor_tensor(lb_e, prm["lb"][:, 4:8], prm["lb"][:, 0:4], ALU.subtract).then_inc(lb_ready, 1)
                dve.wait_ge(lb_ready, 2)
                link(dve.scalar_tensor_tensor(out=lb_log1m, in0=lb_e, scalar=0.0, in1=lb_log, op0=ALU.max, op1=ALU.add))
                link(dve.tensor_scalar(lb_log1m, lb_log1m, -1.0, None, ALU.mult))
                link(dve.scalar_tensor_tensor(out=lb_log, in0=lb_e, scalar=0.0, in1=lb_log, op0=ALU.min, op1=ALU.subtract))
                dve.tensor_scalar(lb_neg, lb_log, -1.0, None, ALU.mult).then_inc(lb_ready, 1)
                dve.wait_ge(lb_ready, 3)

            PARTS = 13

            def hgrn_part(ly, u, j, d, part):
                z = proj[:, (FF, FB)[d] + j, :]
                w = width(ly, HQ)
                q = proj[:, HQ + j, 0:w]
                one = 2 * d + j
                if part == 0:
                    dve.wait_ge(hg_soft, u + 1)
                    link(dve.scalar_tensor_tensor(out=lf_b, in0=z, scalar=0.0, in1=e_b, op0=ALU.min, op1=ALU.subtract))
                    dve.scalar_tensor_tensor(out=m_b, in0=z, scalar=0.0, in1=e_b, op0=ALU.max, op1=ALU.add).then_inc(hg_lf, 1)
                    if ly == 1:
                        dve.wait_ge(hg_lf, u + 1)
                        dve.tensor_scalar(lf_b, lf_b, lb_log1m[:, one:one + 1], None, ALU.add).then_inc(hg_lb, 1)
                if part == 1 and ly == 1:
                    dve.wait_ge(hg_abs, u - 3)
                    dve.scalar_tensor_tensor(out=lf_b, in0=lf_b, scalar=lb_log[:, one:one + 1], in1=e_b, op0=ALU.max,
                                             op1=ALU.add).then_inc(hg_lb, 1)
                    dve.wait_ge(hg_lb, 2 * (u - 4) + 2)
                if part in (1, 2):
                    if u:
                        dve.wait_ge(lev_diff, 2 * LEVELS * u)
                    for c in ((0, 1, 2), (3, 4, 5))[part - 1]:
                        run = slice(c * CH, (c + 1) * CH)
                        src, dst = lf_b[:, run], a_b[:, run]
                        if d:
                            src, dst = src[:, ::-1], dst[:, ::-1]
                        ins = dve.tensor_tensor_scan(dst, cst["ones"], src, 0.0, ALU.mult, ALU.add)
                        if c < NCH - 1:
                            link(ins)
                        else:
                            ins.then_inc(hg_a, 1)
                if part == 3:
                    dve.wait_ge(hg_a, u + 1)
                    a_c = a_b.rearrange("p (c t) -> p c t", t=CH)
                    last = a_c[:, :, CH - 1:CH] if d == 0 else a_c[:, :, 0:1]
                    dve.tensor_tensor(e_b.rearrange("p (c t) -> p c t", t=CH), last.broadcast_to([P, NCH, CH]), a_c,
                                      ALU.subtract).then_inc(hg_ed0, 1)
                if part == 4:
                    if u >= 2:
                        dve.wait_ge(hg_o_ps, u - 1)
                    dve.wait_ge(hg_ea, 2 * u + 2)
                    dve.tensor_tensor(q_decayed(u)[:, 0:w], q, m_b[:, 0:w], ALU.mult).then_inc(hg_qe, 1)
                    dve.wait_ge(hg_ed, u + 1)
                    dve.tensor_tensor(ke_b, z, e_b, ALU.mult).then_inc(hg_ke, 1)
                q_side, k_side = (1, 0) if d == 0 else (0, 1)
                if 5 <= part < 5 + LEVELS:
                    l = part - 5
                    b = 1 << l
                    o, kk, qq = halves(decay(u, l)[:, 0:w], b), halves(z[:, 0:w], b), halves(q, b)
                    dve.wait_ge(lev_exp, LEVELS * u + l + 1)
                    link(dve.tensor_tensor(o[:, :, q_side, :], o[:, :, q_side, :], qq[:, :, q_side, :], ALU.mult))
                    dve.tensor_tensor(o[:, :, k_side, :], o[:, :, k_side, :], kk[:, :, k_side, :], ALU.mult).then_inc(lev_ready, 1)
                if part == PARTS - 1:
                    dve.wait_ge(hg_u, u + 1)
                    seq = order(d)
                    st = state[:, u % 2]
                    link(dve.memset(st[:, seq[0], :], 0.0))
                    for n in range(1, NCH):
                        was, now = seq[n - 1], seq[n]
                        for r in range(2):
                            rows = slice(64 * r, 64 * r + 64)
                            ins = dve.scalar_tensor_tensor(
                                out=st[rows, now, :], in0=st[rows, was, :], scalar=f_last[rows, was:was + 1],
                                in1=wide_ps[rows, 1, was * CH + 64 * r:was * CH + 64 * r + 64], op0=ALU.mult, op1=ALU.add)
                            if n == NCH - 1 and r == 1:
                                ins.then_inc(hg_s, 1)
                            else:
                                link(ins)

            def hgrn_masks(ly, u, d, following):
                level = cst[f"level{d}"]
                n_tiles = 2 * len(chunk_list(ly))
                for n in range(n_tiles):
                    m = SC0[u] + n
                    dve.wait_ge(sc_ps, m + 1)
                    if m >= 4:
                        dve.wait_ge(sc_used, m - 3)
                    dve.tensor_tensor(masked[:, m % 4, :], duo_ps[:, 512 * (m % 2):512 * (m % 2) + 448], level,
                                      ALU.mult).then_inc(sc_ready, 1)
                    for part in range(PARTS):
                        if following and part * n_tiles // PARTS == n:
                            hgrn_part(ly, *following, part)

            def hgrn_out(ly, j):
                n = 2 * ly + j
                w = width(ly, HQ)
                dve.wait_ge(hg_diag, n + 1)
                dve.wait_ge(hg_o_ps, 4 * ly + 2 * j + 2)
                o, t = proj[:, FF + j, 0:w], proj[:, FB + j, 0:w]
                link(dve.tensor_tensor(t, wide_ps[:, 0, 0:w], proj[:, HI + j, 0:w], ALU.mult))
                dve.tensor_tensor(o, pair_ps[:, 0:w], t, ALU.add).then_inc(hg_o, 1)

            def hgrn_close(ly, j):
                n = 2 * ly + j
                w = width(ly, HQ)
                o, t = proj[:, FF + j, 0:w], proj[:, FB + j, 0:w]
                dve.wait_ge(hg_rt, n + 1)
                link(dve.reciprocal(t, t))
                link(dve.tensor_tensor(o, o, t, ALU.mult))
                gz = proj[:, HZ + j, 0:w]
                dve.scalar_tensor_tensor(out=gz, in0=o, scalar=prm["hg_g"][:, n:n + 1], in1=gz, op0=ALU.mult,
                                         op1=ALU.mult).then_inc(hg_out, 1)

            def attention(ly):
                for n, (t, w) in enumerate(qk_tiles(ly)):
                    x = proj[:, t, 0:w]
                    gain = prm["k_g" if t == AK else "q_g"][:, ly:ly + 1]
                    dve.wait_ge(qk_rt, 3 * ly + n + 1)
                    link(dve.reciprocal(m_b[:, 0:w], m_b[:, 0:w]))
                    dve.scalar_tensor_tensor(out=x, in0=x, scalar=gain, in1=m_b[:, 0:w], op0=ALU.mult,
                                             op1=ALU.mult).then_inc(qk_norm, 1)
                    dve.wait_ge(qk_rot, 3 * ly + n + 1)
                    link(dve.tensor_tensor(lf_b[:, 0:LAT], duo_ps[:, 0:LAT], cst["sin"], ALU.mult))
                    link(dve.tensor_tensor(x[:, 0:LAT], x[:, 0:LAT], cst["cos"], ALU.mult))
                    dve.tensor_tensor(x[:, 0:LAT], x[:, 0:LAT], lf_b[:, 0:LAT], ALU.add).then_inc(qk_ready, 1)
                units = att_units(ly)
                for n in range(len(units) + 4):
                    if n < len(units):
                        m = ATT0[ly] + n
                        a, b = keys_of(units[n][2])
                        one = slice(m % 4, m % 4 + 1)
                        dve.wait_ge(at_s, m + 1)
                        link(dve.tensor_reduce(row_max[:, one], wide_ps[:, m % 2, a:b], AX.X, ALU.max))
                        dve.tensor_scalar(neg_max[:, one], row_max[:, one], -HD ** -0.5, None, ALU.mult).then_inc(at_max, 1)
                    if n >= 1 and n <= len(units):
                        m = ATT0[ly] + n - 1
                        a, b = keys_of(units[n - 1][2])
                        one = slice(m % 4, m % 4 + 1)
                        dve.wait_ge(at_exp, m + 1)
                        link(dve.reciprocal(row_inv[:, one], row_sum[:, one]))
                        dve.tensor_scalar(probs(m)[:, a:b], probs(m)[:, a:b], row_inv[:, one], None, ALU.mult).then_inc(at_p, 1)
                    if n >= 4:
                        m = ATT0[ly] + n - 4
                        i, r, c = units[n - 4]
                        rows = slice(64 * r, 64 * r + 64)
                        az = proj[rows, AZ + i, c * CH:(c + 1) * CH]
                        dve.wait_ge(at_o_ps, m + 1)
                        dve.tensor_tensor(az, duo_ps[rows, 512 * (m % 2):512 * (m % 2) + CH], az, ALU.mult).then_inc(at_out, 1)

            def fourier(ly):
                for s in (0, 1)[:2 - ly]:
                    a, b = ((0, LAT), (LAT, TOK))[s]
                    for j in range(2):
                        fz = proj[:, FZ + j, a:b]
                        dve.wait_ge(ft_y_ps, 4 * ly + 2 * s + j + 1)
                        dve.tensor_tensor(fz, ft_bank(s, j)[:, 0:b - a], fz, ALU.mult).then_inc(ft_out, 1)

            def residual(ly):
                w = width(ly, HQ)
                for n in range(KT):
                    dve.wait_ge(evacuated, EVAC[f"out{ly}"] + n + 1)
                    dve.tensor_tensor(h[:, n, 0:w], h[:, n, 0:w], resid[:, n % 2, 0:w], ALU.add).then_inc(h_ready, 1)

            lower_bounds()
            modulation(0)
            for ly in range(DEPTH):
                reciprocal_root(ly, TOK)
                for k in range(KT):
                    dve.tensor_tensor(xn_t[:, k, :], h[:, k, :], root[:, :], ALU.mult).then_inc(scaled, 1)
                for k in range(KT):
                    dve.wait_ge(xn_ready, 16 * ly + 2 * k + 2)
                    split(xn_t[:, k, :], lead_tile(k))
                units = hg_units(ly)
                for part in range(PARTS):
                    if part == 5:
                        fourier(ly)
                    hgrn_part(ly, *units[0], part)
                for n, (u, j, d) in enumerate(units):
                    hgrn_masks(ly, u, d, units[n + 1] if n < 3 else None)
                    if d == 1:
                        hgrn_out(ly, j)
                    if n == 2:
                        hgrn_close(ly, 0)
                if ly == 0:
                    modulation(1)
                hgrn_close(ly, 1)
                attention(ly)
                dve.wait_ge(at_out, ATT0[ly] + len(att_units(ly)))
                w = width(ly, HQ)
                split(proj[:, AZ + 1, 0:w], mix_lead(3)[:, 0:w])
                residual(ly)
            reciprocal_root(N_FINAL, LAT)
            for k in range(KT):
                dve.scalar_tensor_tensor(out=h[:, k, 0:LAT], in0=h[:, k, 0:LAT], scalar=prm["final_g"][:, k:k + 1],
                                         in1=root[:, 0:LAT], op0=ALU.mult, op1=ALU.mult).then_inc(scaled, 1)
            def half_turn():
                dve.memset(half_pi, float(np.pi / 2)).then_inc(rope_arg, 1)
                dve.wait_ge(const2_landed, 16)
                dve.wait_ge(pos_landed, 16)
                turn = 2 * np.pi
                c1 = 6.28125
                c2 = float(np.float32(round((turn - c1) * 2 ** 20) / 2 ** 20))
                link(dve.tensor_copy(sin_2, pos_i))
                link(dve.tensor_scalar(sin_2, sin_2, cst2["inv_freq"], None, ALU.mult))
                link(dve.tensor_scalar(cos_2, sin_2, 1.0 / turn, 12582912.0, ALU.mult, ALU.add))
                link(dve.tensor_scalar(cos_2, cos_2, 12582912.0, None, ALU.subtract))
                for part in (c1, c2, turn - c1 - c2):
                    link(dve.scalar_tensor_tensor(out=sin_2, in0=cos_2, scalar=-part, in1=sin_2, op0=ALU.mult, op1=ALU.add))
                dve.tensor_scalar(sin_2, sin_2, 3.1415925, -3.1415925, ALU.min, ALU.max).then_inc(rope_arg, 1)

            def scale_tiles(n, src, dst, gain):
                for k in range(KT):
                    w = src[:, k, :].shape[1]
                    dve.scalar_tensor_tensor(out=dst[:, k, :], in0=src[:, k, :], scalar=prm[gain][:, k:k + 1],
                                             in1=root[:, 0:w], op0=ALU.mult, op1=ALU.mult).then_inc(scaled, 1)

            def split_tiles(n):
                for k in range(KT):
                    dve.wait_ge(scaled, 8 * n + k + 1)
                    split(y_2[:, k, :], lead_tile(k)[:, 0:LAT])

            reciprocal_root(N_MEM, CTX)
            scale_tiles(N_MEM, mem_x, mem_x, "g_mem")
            reciprocal_root(N_MIX_PRE, LAT)
            scale_tiles(N_MIX_PRE, x_2, y_2, "g_mix_pre")
            split_tiles(N_MIX_PRE)
            half_turn()
            taps = prm["conv2"].rearrange("p (n t) -> p n t", t=5)
            for q in range(12):
                x, y = tile_2[:, DQ2 + q, :], conv_y[q % 2]
                dve.wait_ge(evacuated, EVAC["proj_2"] + DQ2 + q + 1)
                if q >= 2:
                    dve.wait_ge(cv_ready, q - 1)
                link(dve.tensor_scalar(y, x, taps[:, q, 2:3], None, ALU.mult))
                for t in (0, 1, 3, 4):
                    off = t - 2
                    a, b = max(0, -off), LAT - max(0, off)
                    ins = dve.scalar_tensor_tensor(out=y[:, a:b], in0=x[:, a + off:b + off], scalar=taps[:, q, t:t + 1],
                                                   in1=y[:, a:b], op0=ALU.mult, op1=ALU.add)
                    if t < 4:
                        link(ins)
                    else:
                        ins.then_inc(cv_sum, 1)
            dve.wait_ge(evacuated, EVAC["ab_2"] + 1)
            dve.tensor_tensor(g_tok, ab[:, :, 0:8], prm["dt_bias"].unsqueeze(1).broadcast_to([P, NLAT, 8]), ALU.add).then_inc(g_x, 1)
            dve.wait_ge(g_l, 3)
            link(dve.scalar_tensor_tensor(out=g_tok, in0=g_tok, scalar=0.0, in1=g_soft, op0=ALU.max, op1=ALU.add))
            dve.scalar_tensor_tensor(out=g_tok, in0=g_tok, scalar=-1.0, in1=a_exp.unsqueeze(1).broadcast_to([P, NLAT, 8]),
                                     op0=ALU.mult, op1=ALU.mult).then_inc(g_ready, 1)
            dve.wait_ge(g_ps, 1)
            for d in range(2):
                dve.tensor_copy(g_cum[:, :, 4 * d:4 * d + 4], duo_ps[:, 16 * d:16 * d + 16].rearrange("p (c n) -> p c n", c=NLAT)).then_inc(g_c, 1)
            dve.wait_ge(g_e, 1)
            dve.tensor_tensor(beta_g, beta, g_exp, ALU.mult).then_inc(g_b, 1)
            for n in range(8):
                x, r = tile_2[:, DQ2 + n, :], work[:, 2 + n % 2, 0:LAT]
                dve.wait_ge(l2_rt, n + 1)
                link(dve.reciprocal(r, r))
                dve.scalar_tensor_tensor(out=x, in0=x, scalar=P ** -0.5 if n < 4 else 1.0, in1=r, op0=ALU.mult,
                                         op1=ALU.mult).then_inc(l2_ready, 1)
            dve.wait_ge(rope_table, 1)
            for n in range(5):
                x, t = tile_2[:, n, :], work[:, 4 + n % 2, 0:LAT]
                dve.wait_ge(rp_rot, n + 1)
                link(dve.tensor_tensor(t, pair_ps[:, 512 * (n % 2):512 * (n % 2) + LAT], sin_2, ALU.mult))
                link(dve.tensor_tensor(x, x, cos_2, ALU.mult))
                dve.tensor_tensor(x, x, t, ALU.add).then_inc(rp_ready, 1)
            for m in range(len(WIN) + 4):
                if m < len(WIN):
                    i, r, c = WIN[m]
                    a, b, ma, mb = window_keys(c)
                    one = slice(m % 4, m % 4 + 1)
                    dve.wait_ge(w_s, m + 1)
                    if m >= 3:
                        dve.wait_ge(w_pt_ps, m - 2)
                    head = i + 4 * r
                    link(dve.tensor_tensor_reduce(probs(m)[:, 0:b - a], quad(m)[:, 0:b - a], cst2["window"][:, ma:mb],
                                                  HD ** -0.5, prm["sink"][:, head:head + 1], ALU.add, ALU.max,
                                                  row_max2[:, one]))
                    dve.tensor_scalar(neg_max2[:, one], row_max2[:, one], -1.0, None, ALU.mult).then_inc(w_max, 1)
                if 1 <= m <= len(WIN):
                    n = m - 1
                    a, b, _, _ = window_keys(WIN[n][2])
                    one = slice(n % 4, n % 4 + 1)
                    dve.wait_ge(w_exp, 2 * n + 2)
                    link(dve.tensor_tensor(row_sum2[:, one], row_sum2[:, one], sink_e[:, one], ALU.add))
                    link(dve.reciprocal(row_inv2[:, one], row_sum2[:, one]))
                    dve.tensor_scalar(probs(n)[:, 0:b - a], probs(n)[:, 0:b - a], row_inv2[:, one], None, ALU.mult).then_inc(w_p, 1)
                if m >= 4:
                    n = m - 4
                    i, r, c = WIN[n]
                    rows = slice(64 * r, 64 * r + 64)
                    dve.wait_ge(w_o_ps, n + 1)
                    dve.tensor_copy(tile_2[rows, i, c * CH:(c + 1) * CH], duo_ps[rows, 512 * (n % 2):512 * (n % 2) + CH]).then_inc(w_out_s, 1)

            def heads(v):
                return v.unsqueeze(2).broadcast_to([P, 4, CH])

            ident_4 = cst["ident"].unsqueeze(1).broadcast_to([P, 4, CH])
            for s in range(NLAT):
                for d in range(2):
                    g, c = 2 * s + d, chunk_at(d, s)
                    last = CH - 1 if d == 0 else 0
                    mine = slice(4 * d, 4 * d + 4)
                    dve.wait_ge(dn_a, g + 1)
                    link(dve.tensor_tensor(dn(d, XM), dn_bank(d, 0), heads(g_cum[:, c, mine]), ALU.subtract))
                    link(dve.tensor_tensor(g_end[:, d], dn_bank(d, 0)[:, :, last], g_cum[:, c, mine], ALU.subtract))
                    dve.tensor_tensor(dn(d, XM), dn(d, XM), cst2[f"tri{d}"].unsqueeze(1).broadcast_to([P, 4, CH]), ALU.mult).then_inc(dn_diff, 1)
                    dve.wait_ge(dn_exp, 4 * g + 4)
                    link(dve.tensor_tensor(dn(d, XT), dn_bank(d, 1), dn(d, XM), ALU.mult))
                    dve.tensor_tensor(dn(d, QK), dn_bank(d, 3), dn(d, XM), ALU.mult).then_inc(dn_x, 1)
                    dve.tensor_tensor(dn(d, XT), dn(d, XT), dn_bank(d, 2), ALU.mult).then_inc(dn_x, 1)
                    dve.wait_ge(dn_tok_ps, g + 1)
                    dve.tensor_tensor(dn(d, KBG), dn_bank(d, 0), heads(beta_g[:, c, mine]), ALU.mult).then_inc(dn_tok, 1)
                    dve.tensor_tensor(dn(d, KG), dn_bank(d, 0), heads(g_end[:, d]), ALU.mult).then_inc(dn_tok, 1)
                    dve.tensor_tensor(dn(d, VB), dn_bank(d, 1), heads(beta[:, c, mine]), ALU.mult).then_inc(dn_tok, 1)
                for l in range(LEVELS):
                    for d in range(2):
                        at = 2 * (LEVELS * s + l) + d
                        dve.wait_ge(dn_z_ps, at + 1)
                        if l == 0:
                            link(dve.scalar_tensor_tensor(out=dn(d, T), in0=dn_bank(d, 2), scalar=-1.0, in1=ident_4, op0=ALU.mult, op1=ALU.add))
                            dve.scalar_tensor_tensor(out=dn(d, R), in0=dn(d, XM), scalar=-1.0, in1=ident_4, op0=ALU.mult, op1=ALU.add).then_inc(dn_t, 1)
                        else:
                            if l < LEVELS - 1:
                                link(dve.tensor_tensor(dn(d, T), dn(d, T), dn_bank(d, 2), ALU.subtract))
                            dve.tensor_tensor(dn(d, R), dn(d, R), dn_bank(d, 3), ALU.subtract).then_inc(dn_t, 1)
                for d in range(2):
                    c = chunk_at(d, s)
                    o = o_dn[:, :, c * CH:(c + 1) * CH]
                    dve.wait_ge(dn_o_ps, 2 * s + d + 1)
                    if s < NLAT // 2:
                        link(dve.tensor_copy(o, dn_bank(d, 2)))
                        if s == 0:
                            dve.tensor_copy(s_dn[:, d], dn_bank(d, 3)).then_inc(dn_s, 1)
                    if s >= NLAT // 2:
                        ins = dve.tensor_tensor(o, o, dn_bank(d, 2), ALU.add)
                        if s == NLAT - 1:
                            ins.then_inc(dn_s, 1)
                        else:
                            link(ins)
                    if 0 < s < NLAT - 1:
                        link(dve.tensor_tensor(s_dn[:, d], s_dn[:, d], heads(s_decay[:, d]), ALU.mult))
                        dve.tensor_tensor(s_dn[:, d], s_dn[:, d], dn_bank(d, 3), ALU.add).then_inc(dn_s, 1)
            for n in range(4):
                o, r, gate = o_dn[:, n, :], work[:, 2 + n % 2, 0:LAT], tile_2[:, DG2 + n, :]
                dve.wait_ge(do_rt, n + 1)
                link(dve.reciprocal(r, r))
                link(dve.tensor_tensor(o, o, r, ALU.mult))
                dve.scalar_tensor_tensor(out=gate, in0=o, scalar=prm["g_dn"], in1=gate, op0=ALU.mult, op1=ALU.mult).then_inc(do_out, 1)
                dve.wait_ge(do_out, n + 1)
                split(gate, mix2_lead(4 + n))

            def add_closed(n, gain, done):
                reciprocal_root(n, LAT)
                scale_tiles(n, y_2, y_2, gain)
                for k in range(KT):
                    dve.wait_ge(scaled, 8 * n + k + 1)
                    dve.tensor_tensor(x_2[:, k, :], x_2[:, k, :], y_2[:, k, :], ALU.add).then_inc(done, 1)

            add_closed(N_MIX_POST, "g_mix_post", x_ready)
            reciprocal_root(N_CROSS_PRE, LAT)
            scale_tiles(N_CROSS_PRE, x_2, y_2, "g_cross_pre")
            split_tiles(N_CROSS_PRE)
            for m in range(len(CROSS) + 4):
                if m < len(CROSS):
                    one = slice(m % 4, m % 4 + 1)
                    dve.wait_ge(c_s, m + 1)
                    link(dve.tensor_reduce(row_max2[:, one], quad(m)[:, 0:CTX], AX.X, ALU.max))
                    dve.tensor_scalar(neg_max2[:, one], row_max2[:, one], -256 ** -0.5, None, ALU.mult).then_inc(c_max, 1)
                if 1 <= m <= len(CROSS):
                    n = m - 1
                    one = slice(n % 4, n % 4 + 1)
                    dve.wait_ge(c_exp, n + 1)
                    link(dve.reciprocal(row_inv2[:, one], row_sum2[:, one]))
                    dve.tensor_scalar(probs(n)[:, 0:CTX], probs(n)[:, 0:CTX], row_inv2[:, one], None, ALU.mult).then_inc(c_p, 1)
                if m >= 4:
                    n = m - 4
                    hd, c = CROSS[n]
                    dve.wait_ge(c_o_ps, n + 1)
                    dve.tensor_copy(o_c[:, 2 * hd:2 * hd + 2, c * CH:(c + 1) * CH],
                                    duo_ps[:, 512 * (n % 2):512 * (n % 2) + 256].rearrange("p (e t) -> p e t", e=2)).then_inc(c_out, 1)
            add_closed(N_CROSS_POST, "g_cross_post", x_ready)
            reciprocal_root(N_FFN_PRE, LAT)
            scale_tiles(N_FFN_PRE, x_2, y_2, "g_ffn_pre")
            split_tiles(N_FFN_PRE)
            for t in range(22):
                dve.wait_ge(evacuated, EVAC["gu"] + 2 * t + 2)
                dve.tensor_tensor(tile_2[:, t, :], tile_2[:, t, :], up_2[t % 2], ALU.mult).then_inc(ffn_ready, 1)
                dve.wait_ge(ffn_ready, t + 1)
                split(tile_2[:, t, :], hidden_lead(t))
            add_closed(N_FFN_POST, "g_ffn_post", final_ready)

        @block.tensor
        def _(pe):
            def use_chunk(c):
                pe.wait_ge(landed[c % RING], 16 * (c // RING + 1))
                return ring[:, c % RING, :]

            def project(stage, tile, chunk, k_tiles, rhs, w, rhs_ready=None):
                g = EVAC[stage] + tile
                if g >= 2:
                    pe.wait_ge(evacuated, g - 1)
                for k in range(k_tiles):
                    if k % KT == 0:
                        wt = use_chunk(chunk + k // KT)
                    if rhs_ready:
                        rhs_ready(k)
                    for a, b in pieces(w):
                        last = pe.matmul(wide_ps[:, g % 2, a:b], wt[:, k % KT * P:(k % KT + 1) * P], rhs(k)[:, a:b],
                                         start=k == 0, stop=k == k_tiles - 1)
                    if k % KT == KT - 1 or k == k_tiles - 1:
                        last.then_inc(chunk_used, 1)

            def project_split(stage, tile, k_order, lead, rest, w, input_ready=None):
                g = EVAC[stage] + tile
                if g >= 2:
                    pe.wait_ge(evacuated, g - 1)
                for n, k in enumerate(k_order):
                    if n % KT == 0:
                        at = tile * -(-len(k_order) // KT) + n // KT
                        m = SPLIT_AT[stage] + at
                        pe.wait_ge(w_split, m + 1)
                        w_rest = as_r(ring[:, (PLAN[stage] + at) % RING, :])
                        w_first = as_r(w_lead[:, m % 2, :])
                    if input_ready:
                        input_ready(n)
                    cols = slice(k % KT * P, (k % KT + 1) * P)
                    for a, b in pieces(w):
                        for p, (wt, x) in enumerate(((w_first, lead(k)), (w_first, rest(k)), (w_rest, lead(k)))):
                            last = pe.matmul(wide_ps[:, g % 2, a:b], wt[:, cols], as_r(x[:, a:b]),
                                             start=n == 0 and p == 0, stop=n == len(k_order) - 1 and p == 2)
                    if n % KT == KT - 1 or n == len(k_order) - 1:
                        last.then_inc(chunk_used, 1)

            def after(before):
                return lambda n: pe.wait_ge(x_split, before + n + 1)

            def mix_ready(ly):
                return lambda n: (pe.wait_ge(mix_split, 7 * ly + n + 1) if n < KT - 1 else
                                  pe.wait_ge(x_split, X_SPLITS[f"out{ly}"] + 1))

            def modulation_tile(ly, n):
                wt = use_chunk(PLAN[f"mod{ly}"] + n)
                for k in range(KT):
                    last = pe.matmul(mod_ps[:, 2 * n:2 * n + 2], wt[:, k * P:(k + 1) * P], c_act[:, 2 * k:2 * k + 2],
                                     start=k == 0, stop=k == KT - 1, skip_group_check=True)
                last.then_inc(chunk_used, 1)

            def modulation(ly):
                pe.wait_ge(c_ready, 1)
                for n in range(N_MOD):
                    modulation_tile(ly, n)

            def norm_sum(n, w):
                for k in range(KT):
                    pe.wait_ge(sq_ready, 8 * n + k + 1)
                    for a, b in pieces(w):
                        last = pe.matmul(pair_ps[:, a:b], cst["ones"], sq[:, k % 2, a:b], start=k == 0, stop=k == KT - 1)
                    last.then_inc(sq_used, 1)

            def by_token(src, ps, done):
                for c in range(NCH):
                    last = pe.transpose(ps[:, c * CH:(c + 1) * CH], src[:, c * CH:(c + 1) * CH], cst["ident"])
                last.then_inc(done, 1)

            def keys_by_token(u):
                pe.wait_ge(hg_ke, u + 1)
                by_token(ke_b, wide_ps[:, 0], hg_kt_ps)

            def updates(u, j):
                pe.wait_ge(hg_kt, u + 1)
                if u:
                    pe.wait_ge(hg_s, u)
                if u % 4 == 3:
                    pe.wait_ge(hg_rt, u // 2)
                for c in range(NCH):
                    last = pe.matmul(wide_ps[:, 1, c * CH:(c + 1) * CH], k_tok[:, c, :], v_tok[:, j, c, :], start=True, stop=True)
                last.then_inc(hg_u, 1)

            def hgrn_unit(ly, u, j, d, following):
                if d == 0:
                    if j:
                        pe.wait_ge(hg_o, 2 * ly + j)
                    for a, b in pieces(width(ly, HQ)):
                        pe.matmul(pair_ps[:, a:b], zero[0:1, :], cst["cos"][0:1, 0:b - a], start=True, stop=False,
                                  skip_group_check=True)
                pe.wait_ge(lev_ready, LEVELS * (u + 1))
                pe.wait_ge(hg_qe, u + 1)
                pe.wait_ge(hg_s, u + 1)
                side = 1 if d == 0 else 0
                tiles = [(c, r) for c in chunk_list(ly) for r in range(2)]

                def scores(n):
                    c, r = tiles[n]
                    m = SC0[u] + n
                    rows = slice(64 * r, 64 * r + 64)
                    if m >= 2:
                        pe.wait_ge(sc_ready, m - 1)
                    for l in range(LEVELS):
                        w = decay(u, l)[rows, c * CH:(c + 1) * CH]
                        last = pe.matmul(duo_ps[:, 512 * (m % 2) + 64 * l:512 * (m % 2) + 64 * l + 64], w,
                                         halves(w, 1 << l)[:, :, side, :], start=True, stop=True, skip_group_check=True)
                    last.then_inc(sc_ps, 1)

                def values(n):
                    c, r = tiles[n]
                    m = SC0[u] + n
                    rows = slice(64 * r, 64 * r + 64)
                    pe.wait_ge(sc_ready, m + 1)
                    o = pair_ps[rows, c * CH:(c + 1) * CH]
                    if c != order(d)[0]:
                        pe.matmul(o, state[rows, u % 2, c, :], q_decayed(u)[rows, c * CH:(c + 1) * CH], start=False,
                                  stop=False, skip_group_check=True)
                    for l in range(LEVELS):
                        last = pe.matmul(halves(o, 1 << l)[:, :, side, :], v_tok[:, j, c, rows],
                                         masked[:, m % 4, 64 * l:64 * l + 64], start=False, stop=l == LEVELS - 1,
                                         skip_group_check=True)
                    last.then_inc(sc_used, 1)
                    if n == len(tiles) - 1:
                        pe.matmul(pair_ps[:, c * CH:c * CH + 64], zero[0:1, :], cst["cos"][0:1, 0:64], start=False, stop=True,
                                  skip_group_check=True).then_inc(hg_o_ps, 1)

                for n in range(len(tiles) + 1):
                    if n < len(tiles):
                        scores(n)
                    if n:
                        values(n - 1)
                    if j == 1 and d == 0 and n == 2:
                        head_mean(ly, 0)
                    if ly == 0 and n % 2 == 1:
                        modulation_tile(1, (u * len(tiles) + n) // 2)
                    if following and n == len(tiles) * 7 // 12:
                        keys_by_token(following[0])
                    if following and n == len(tiles) * 10 // 12:
                        updates(following[0], following[1])

            def diagonal(ly, j):
                w = width(ly, HQ)
                n = 2 * ly + j
                pe.wait_ge(hg_qk, n + 1)
                if j == 0:
                    pe.wait_ge(hg_kt, 4 * ly + 3)
                for a, b in pieces(w):
                    last = pe.matmul(wide_ps[:, 0, a:b], cst["ones_head"], proj[:, FF + j, a:b], start=True, stop=True)
                last.then_inc(hg_diag, 1)

            def head_mean(ly, j):
                w = width(ly, HQ)
                n = 2 * ly + j
                pe.wait_ge(hg_sq, n + 1)
                pe.wait_ge(hg_s, 4 * ly + 3 + j)
                for a, b in pieces(w):
                    last = pe.matmul(wide_ps[:, 1, a:b], cst["ones_head"], proj[:, HI + j, a:b], start=True, stop=True)
                last.then_inc(hg_ms, 1)

            def attention(ly):
                for n, (t, w) in enumerate(qk_tiles(ly)):
                    m = 3 * ly + n
                    pe.wait_ge(qk_sq, m + 1)
                    for a, b in pieces(w):
                        last = pe.matmul(pair_ps[:, a:b], cst["ones_head"], e_b[:, a:b], start=True, stop=True)
                    last.then_inc(qk_ms, 1)
                    pe.wait_ge(qk_norm, m + 1)
                    if n:
                        pe.wait_ge(qk_ready, m)
                    pe.matmul(duo_ps[:, 0:LAT], cst["rot_pair"], proj[:, t, 0:LAT], start=True, stop=True).then_inc(qk_rot, 1)
                by_token(proj[:, AV, :], pair_ps, vt_ps)
                pe.wait_ge(vt_ready, 3 * ly + 3)
                pe.wait_ge(qk_ready, 3 * ly + 3)
                units = att_units(ly)
                for n in range(len(units) + 3):
                    if n < len(units):
                        i, r, c = units[n]
                        m = ATT0[ly] + n
                        rows = slice(64 * r, 64 * r + 64)
                        if n >= 2:
                            pe.wait_ge(at_exp, m - 1)
                        for a, b in ([(0, LAT)] if c < NLAT else []) + [(LAT, TOK)]:
                            last = pe.matmul(wide_ps[:, m % 2, a:b], proj[rows, AQ + i, c * CH:(c + 1) * CH],
                                             proj[rows, AK, a:b], start=True, stop=True)
                        last.then_inc(at_s, 1)
                    if 2 <= n <= len(units) + 1:
                        m = ATT0[ly] + n - 2
                        a, b = keys_of(units[n - 2][2])
                        pe.wait_ge(at_p, m + 1)
                        if n >= 3:
                            pe.wait_ge(at_pt, m)
                        for t in range(a // P, b // P):
                            last = pe.transpose(pair_ps[:, t * P:(t + 1) * P], probs(m)[:, t * P:(t + 1) * P], cst["ident"])
                        last.then_inc(at_pt_ps, 1)
                    if n >= 3:
                        m = ATT0[ly] + n - 3
                        i, r, c = units[n - 3]
                        a, b = keys_of(c)
                        pe.wait_ge(at_pt, m + 1)
                        if n >= 5:
                            pe.wait_ge(at_out, m - 1)
                        for t in range(a // P, b // P):
                            last = pe.matmul(duo_ps[64 * r:64 * r + 64, 512 * (m % 2):512 * (m % 2) + CH],
                                             v_tok[:, 0, t, 64 * r:64 * r + 64], probs_t(m)[:, t * P:(t + 1) * P],
                                             start=t == a // P, stop=t == b // P - 1)
                        last.then_inc(at_o_ps, 1)

            def fourier(ly):
                chunk = PLAN[f"dft{ly}"]
                m = FT0[ly]
                for s in (0, 1)[:2 - ly]:
                    lo, n_t = ((0, NLAT), (LAT, 2))[s]
                    size = n_t * P
                    chunks = NLAT if s == 0 else 1
                    for j in range(2):
                        for tt in range(n_t):
                            if m - FT0[ly] >= 2:
                                pe.wait_ge(ft_a, m - 1)
                            pe.matmul(pair_ps[:, 512 * (m % 2):512 * (m % 2) + 256],
                                      proj[:, FU + j, lo + tt * P:lo + (tt + 1) * P], cst["dft_ch"], start=True,
                                      stop=True).then_inc(ft_a_ps, 1)
                            m += 1
                        pe.wait_ge(ft_a, m)
                        for tt in range(n_t):
                            at = chunk + (tt if s == 0 else 0)
                            wt = use_chunk(at)
                            base = 0 if s == 0 else tt * 2 * size
                            for part in range(2):
                                last = pe.matmul(ft_bank(s, j)[:, 0:size], ft_buf[:, tt, part * P:(part + 1) * P],
                                                 wt[:, base + part * size:base + (part + 1) * size],
                                                 start=tt == 0 and part == 0, stop=tt == n_t - 1 and part == 1,
                                                 skip_group_check=True)
                            if j and (s == 0 or tt == n_t - 1):
                                last.then_inc(chunk_used, 1)
                        pe.matmul(ft_bank(s, j)[:, 0:64], zero[0:1, :], cst["cos"][0:1, 0:64], start=False, stop=True,
                                  skip_group_check=True).then_inc(ft_y_ps, 1)
                    chunk += chunks

            pe.wait_ge(setup_landed, 32)
            pe.wait_ge(ready, 2)
            modulation(0)
            norm_sum(0, TOK)
            for ly in range(DEPTH):
                if ly:
                    norm_sum(ly, TOK)
                for t in range(NPROJ):
                    project_split(f"proj{ly}", t, range(KT), lead_tile, lambda k: xn_t[:, k, :], width(ly, t),
                                  after(X_SPLITS[f"proj{ly}"]) if t == 0 else None)
                for j in range(2):
                    pe.wait_ge(evacuated, EVAC[f"proj{ly}"] + NPROJ)
                    if ly == 0 and j == 0:
                        pe.wait_ge(mod_ready, 2)
                    if j:
                        pe.wait_ge(vt_ready, 3 * ly + 1)
                    by_token(proj[:, HI + j, :], duo_ps, vt_ps)
                pe.wait_ge(vt_ready, 3 * ly + 2)
                fourier(ly)
                units = hg_units(ly)
                pe.wait_ge(ft_out, (4, 6)[ly])
                keys_by_token(units[0][0])
                updates(units[0][0], 0)
                for n, (u, j, d) in enumerate(units):
                    hgrn_unit(ly, u, j, d, units[n + 1] if n < 3 else None)
                    if d == 1:
                        diagonal(ly, j)
                head_mean(ly, 1)
                if ly == 0:
                    pe.wait_ge(mod_ready, 4)
                attention(ly)
                for n in range(KT):
                    project_split(f"out{ly}", n, MIX_ORDER, mix_lead, lambda k: proj[:, MIX[k], :], width(ly, HQ),
                                  mix_ready(ly) if n == 0 else None)
            norm_sum(N_FINAL, LAT)
            def scaled_by(n):
                return lambda k: pe.wait_ge(scaled, 8 * n + k + 1)

            def mix2_ready(k):
                if k < 4:
                    pe.wait_ge(mix_split, 14 + k + 1)
                else:
                    pe.wait_ge(x_split, X_SPLITS["out_2"] + k - 3)

            def ck(n):
                project("ck", n, PLAN["ck"] + n, KT, lambda k: mem_x[:, k, :], CTX, scaled_by(N_MEM) if n == 0 else None)

            norm_sum(N_MEM, CTX)
            ck(0)
            ck(1)
            norm_sum(N_MIX_PRE, LAT)
            for n in range(2, KT):
                ck(n)
            for n in range(KT):
                g = EVAC["cv"] + n
                pe.wait_ge(evacuated, g - 1)
                wt = use_chunk(PLAN["cv"] + n)
                for t in range(2):
                    for k in range(KT):
                        last = pe.matmul(wide_ps[:, g % 2, t * P:(t + 1) * P], mem_x[:, k, t * P:(t + 1) * P],
                                         wt[:, k * P:(k + 1) * P], start=k == 0, stop=k == KT - 1)
                last.then_inc(chunk_used, 1)
            for t in range(22):
                project_split("proj_2", t, range(KT), lead_tile, lambda k: y_2[:, k, :], LAT,
                              after(X_SPLITS["proj_2"]) if t == 0 else None)
            wt = use_chunk(PLAN["ab_2"])
            g = EVAC["ab_2"]
            pe.wait_ge(evacuated, g - 1)
            for c in range(NLAT):
                for k in range(KT):
                    for p, x in enumerate((as_r(lead_tile(k)).bitcast(F32), as_r(y_2[:, k, :]).bitcast(F32))):
                        last = pe.matmul(wide_ps[:, g % 2, 16 * c:16 * c + 16], x[:, c * CH:(c + 1) * CH],
                                         wt[:, k * P:k * P + 16], start=k == 0 and p == 0, stop=k == KT - 1 and p == 1)
            last.then_inc(chunk_used, 1)
            pe.wait_ge(g_ready, 1)
            pe.wait_ge(const2_landed, 16)
            for d in range(2):
                last = pe.matmul(duo_ps[:, 16 * d:16 * d + 16], cst2[f"tri{d}"], g_tok[:, :, 4 * d:4 * d + 4], start=True, stop=True)
            last.then_inc(g_ps, 1)
            for n in range(8):
                pe.wait_ge(l2_sq, n + 1)
                if n >= 2:
                    pe.wait_ge(l2_rt, n - 1)
                pe.matmul(pair_ps[:, 512 * (n % 2):512 * (n % 2) + LAT], cst["ones"], sq[:, n % 2, 0:LAT], start=True,
                          stop=True).then_inc(l2_ss, 1)
            pe.wait_ge(l2_rt, 8)
            for n in range(5):
                if n >= 2:
                    pe.wait_ge(rp_ready, n - 1)
                pe.matmul(pair_ps[:, 512 * (n % 2):512 * (n % 2) + LAT], cst2["rot_half"], tile_2[:, n, :], start=True,
                          stop=True).then_inc(rp_rot, 1)
            pe.wait_ge(g_c, 2)
            for c in range(NLAT):
                last = pe.transpose(duo_ps[:, c * CH:(c + 1) * CH], tile_2[:, AV2, c * CH:(c + 1) * CH], cst["ident"])
            last.then_inc(v2_ps, 1)
            pe.wait_ge(v2_ready, 1)
            pe.wait_ge(rp_ready, 5)
            for m in range(len(WIN) + 3):
                if m < len(WIN):
                    i, r, c = WIN[m]
                    rows = slice(64 * r, 64 * r + 64)
                    a, b, _, _ = window_keys(c)
                    if m >= 4:
                        pe.wait_ge(w_max, m - 3)
                    pe.matmul(quad(m)[:, 0:b - a], tile_2[rows, i, c * CH:(c + 1) * CH], tile_2[rows, AK2, a:b],
                              start=True, stop=True).then_inc(w_s, 1)
                if 2 <= m <= len(WIN) + 1:
                    n = m - 2
                    a, b, _, _ = window_keys(WIN[n][2])
                    pe.wait_ge(w_p, n + 1)
                    if n >= 2:
                        pe.wait_ge(w_pt, n - 1)
                    for t in range((b - a) // P):
                        last = pe.transpose(twin(n)[:, t * P:(t + 1) * P], probs(n)[:, t * P:(t + 1) * P], cst["ident"])
                    last.then_inc(w_pt_ps, 1)
                if m >= 3:
                    n = m - 3
                    i, r, c = WIN[n]
                    a, b, _, _ = window_keys(c)
                    pe.wait_ge(w_pt, n + 1)
                    if n >= 2:
                        pe.wait_ge(w_out_s, n - 1)
                    for t in range((b - a) // P):
                        last = pe.matmul(duo_ps[64 * r:64 * r + 64, 512 * (n % 2):512 * (n % 2) + CH],
                                         v_tok[:, 0, a // P + t, 64 * r:64 * r + 64], probs_t(n)[:, t * P:(t + 1) * P],
                                         start=t == 0, stop=t == (b - a) // P - 1)
                    last.then_inc(w_o_ps, 1)

            def four(out_ap, lhs, rhs, **flags):
                for hd in range(4):
                    last = pe.matmul(out_ap[:, hd, :], lhs(hd), rhs(hd), start=True, stop=True, **flags)
                return last

            pe.wait_ge(w_out_s, len(WIN))
            pe.wait_ge(l2_ready, 8)
            pe.wait_ge(g_b, 1)
            for s in range(NLAT):
                for d in range(2):
                    g, c = 2 * s + d, chunk_at(d, s)
                    run = slice(c * CH, (c + 1) * CH)
                    if s:
                        pe.wait_ge(dn_s, g - 1)
                    wide = lambda v: v.broadcast_to([P, P])
                    four(dn_bank(d, 0), lambda hd: wide(g_tok[:, c, 4 * d + hd:4 * d + hd + 1]), lambda hd: cst2[f"tri{d}"])
                    four(dn_bank(d, 1), lambda hd: tile_2[:, DK2 + hd, run], lambda hd: tile_2[:, DK2 + hd, run])
                    four(dn_bank(d, 2), lambda hd: wide(beta[:, c, 4 * d + hd:4 * d + hd + 1]), lambda hd: cst["ident"])
                    four(dn_bank(d, 3), lambda hd: tile_2[:, DK2 + hd, run], lambda hd: tile_2[:, DQ2 + hd, run]).then_inc(dn_a, 1)
                for d in range(2):
                    g, c = 2 * s + d, chunk_at(d, s)
                    pe.wait_ge(dn_x, 2 * g + 2)
                    for hd in range(4):
                        pe.transpose(dn_bank(d, 0)[:, hd, :], tile_2[:, DK2 + hd, c * CH:(c + 1) * CH], cst["ident"])
                    for hd in range(4):
                        last = pe.transpose(dn_bank(d, 1)[:, hd, :], tile_2[:, DV2 + hd, c * CH:(c + 1) * CH], cst["ident"])
                    last.then_inc(dn_tok_ps, 1)
                for d in range(2):
                    pe.wait_ge(dn_xm, 2 * (LEVELS * s) + d + 1)
                    four(dn_bank(d, 2), lambda hd: dn(d, XM)[:, hd, :], lambda hd: cst["ident"]).then_inc(dn_z_ps, 1)
                for l in range(1, LEVELS):
                    for d in range(2):
                        pe.wait_ge(dn_xm, 2 * (LEVELS * s + l) + d + 1)
                        pe.wait_ge(dn_t, 2 * (LEVELS * s + l - 1) + d + 1)
                        four(dn_bank(d, 3), lambda hd: dn(d, XM)[:, hd, :], lambda hd: dn(d, T)[:, hd, :]).then_inc(dn_y_ps, 1)
                    for d in range(2):
                        pe.wait_ge(dn_y, 2 * (6 * s + l - 1) + d + 1)
                        if l < LEVELS - 1:
                            four(dn_bank(d, 2), lambda hd: dn(d, R)[:, hd, :], lambda hd: dn(d, Y)[:, hd, :])
                        four(dn_bank(d, 3), lambda hd: dn(d, Y)[:, hd, :], lambda hd: dn(d, R)[:, hd, :]).then_inc(dn_z_ps, 1)
                for d in range(2):
                    pe.wait_ge(dn_t, 2 * (LEVELS * s + LEVELS - 1) + d + 1)
                    pe.wait_ge(dn_tok, 3 * (2 * s + d) + 3)
                    four(dn_bank(d, 0), lambda hd: dn(d, KBG)[:, hd, :], lambda hd: dn(d, R)[:, hd, :]).then_inc(dn_w_ps, 1)
                for d in range(2):
                    pe.wait_ge(dn_w, 2 * s + d + 1)
                    for hd in range(4):
                        last = pe.matmul(dn_bank(d, 1)[:, hd, :], dn(d, R)[:, hd, :], dn(d, VB)[:, hd, :], start=True, stop=s == 0)
                        if s:
                            last = pe.matmul(dn_bank(d, 1)[:, hd, :], dn(d, WT)[:, hd, :], s_dn[:, d, hd, :], start=False, stop=True)
                    last.then_inc(dn_v_ps, 1)
                for d in range(2):
                    pe.wait_ge(dn_v, 2 * s + d + 1)
                    pe.wait_ge(dn_qg, 2 * (2 * s + d) + 2)
                    four(dn_bank(d, 3), lambda hd: dn(d, KG)[:, hd, :], lambda hd: dn(d, VN)[:, hd, :])
                    for hd in range(4):
                        if s:
                            pe.matmul(dn_bank(d, 2)[:, hd, :], s_dn[:, d, hd, :], dn(d, QG)[:, hd, :], start=True, stop=False)
                        last = pe.matmul(dn_bank(d, 2)[:, hd, :], dn(d, VN)[:, hd, :], dn(d, QK)[:, hd, :], start=s == 0, stop=True)
                    last.then_inc(dn_o_ps, 1)
            for n in range(4):
                pe.wait_ge(do_sq, n + 1)
                if n >= 2:
                    pe.wait_ge(do_rt, n - 1)
                pe.matmul(pair_ps[:, 512 * (n % 2):512 * (n % 2) + LAT], cst["ones"], sq[:, n % 2, 0:LAT], start=True,
                          stop=True).then_inc(do_ss, 1)
            for n in range(KT):
                project_split("out_2", n, range(KT), mix2_lead, lambda k: tile_2[:, MIX2[k], :], LAT, mix2_ready if n == 0 else None)
            norm_sum(N_MIX_POST, LAT)
            norm_sum(N_CROSS_PRE, LAT)
            for n in range(KT):
                project_split("cq", n, range(KT), lead_tile, lambda k: y_2[:, k, :], LAT, after(X_SPLITS["cq"]) if n == 0 else None)
            pe.wait_ge(evacuated, EVAC["cq"] + KT)
            for m in range(len(CROSS) + 3):
                if m < len(CROSS):
                    hd, c = CROSS[m]
                    if m >= 4:
                        pe.wait_ge(c_exp, m - 3)
                    for e in range(2):
                        last = pe.matmul(quad(m)[:, 0:CTX], q_c[:, 2 * hd + e, c * CH:(c + 1) * CH], key_c[:, 2 * hd + e, :],
                                         start=e == 0, stop=e == 1)
                    last.then_inc(c_s, 1)
                if 2 <= m <= len(CROSS) + 1:
                    n = m - 2
                    pe.wait_ge(c_p, n + 1)
                    if n >= 2:
                        pe.wait_ge(c_pt, n - 1)
                    for t in range(2):
                        last = pe.transpose(twin(n)[:, t * P:(t + 1) * P], probs(n)[:, t * P:(t + 1) * P], cst["ident"])
                    last.then_inc(c_pt_ps, 1)
                if m >= 3:
                    n = m - 3
                    hd, c = CROSS[n]
                    pe.wait_ge(c_pt, n + 1)
                    if n >= 2:
                        pe.wait_ge(c_out, n - 1)
                    for e in range(2):
                        for t in range(2):
                            last = pe.matmul(duo_ps[:, 512 * (n % 2) + e * P:512 * (n % 2) + (e + 1) * P],
                                             val_c[:, t, (2 * hd + e) * P:(2 * hd + e + 1) * P], probs_t(n)[:, t * P:(t + 1) * P],
                                             start=t == 0, stop=t == 1)
                    last.then_inc(c_o_ps, 1)
            for n in range(KT):
                project_split("co", n, range(KT), lead_tile, lambda k: o_c[:, k, :], LAT,
                              (lambda k: pe.wait_ge(mix_split, 18 + k + 1)) if n == 0 else None)
            norm_sum(N_CROSS_POST, LAT)
            norm_sum(N_FFN_PRE, LAT)
            for n in range(44):
                project_split("gu", n, range(KT), lead_tile, lambda k: y_2[:, k, :], LAT, after(X_SPLITS["gu"]) if n == 0 else None)
            for n in range(KT):
                project_split("down", n, range(22), hidden_lead, lambda k: tile_2[:, k, :], LAT,
                              after(X_SPLITS["down"]) if n == 0 else None)
            norm_sum(N_FFN_POST, LAT)


def tiles_of_rows(v):
    return np.ascontiguousarray(np.moveaxis(np.asarray(v).reshape(-1, P), 1, 0))


def feature_major(x):
    t, f = x.shape
    return x.T.reshape(f // P, P, t).transpose(1, 0, 2)


def chunks_of(w):
    k, n = w.shape
    return w.reshape(k // P, P, n // P, P).transpose(2, 1, 0, 3).reshape(n // P, P, k)


def head_pairs(heads, width=HD):
    return np.concatenate([np.arange(h * width, (h + 1) * width) for h in heads])


def in_order():
    start = dict(zip(("cb", "cc", "cv", "cz", "aq", "ak", "av", "az", "hq", "ff", "fb", "hi", "hz", "fu", "fz"),
                     np.cumsum([0, 256, 256, 256, 256, 256, 128, 128, 256, 256, 256, 256, 256, 256, 256])))
    whole = lambda name, n=256: start[name] + np.arange(n)
    heads = head_pairs((0, 2, 1, 3))
    return np.concatenate([whole("hq"), whole("hz"), whole("ff"), whole("fb"), whole("hi"), start["aq"] + heads,
                           whole("ak", 128), whole("av", 128), start["az"] + heads, whole("fu"), whole("fz"),
                           whole("cb"), whole("cz"), whole("cc"), whole("cv")])


def dft(n):
    k = np.outer(np.arange(n), np.arange(n)) % n
    return np.cos(2 * np.pi * k / n) / np.sqrt(n), np.sin(2 * np.pi * k / n) / np.sqrt(n)


def dft_chunks():
    c, s = dft(LAT)
    lat = np.concatenate([c.reshape(NLAT, P, LAT), -s.reshape(NLAT, P, LAT)], axis=2)
    c, s = dft(CTX)
    ctx = np.concatenate([c.reshape(2, P, CTX), -s.reshape(2, P, CTX)], axis=2).transpose(1, 0, 2).reshape(1, P, CHUNK)
    return lat, ctx


def half_mask(b, back):
    s, t = np.arange(P)[:, None], np.arange(P)[None, :]
    read, written = (t % (2 * b) >= b, s % (2 * b) < b) if not back else (t % (2 * b) < b, s % (2 * b) >= b)
    return (s // (2 * b) == t // (2 * b)) & read & written


def level_masks(back):
    t = np.arange(P)
    return np.concatenate([half_mask(1 << l, back)[:, ((t >> l) & 1) == (0 if back else 1)] for l in range(LEVELS)], 1)


def rotation(pairs):
    r = np.zeros((P, P))
    for a, b in pairs:
        r[b, a] = -1.0
        r[a, b] = 1.0
    return r


def constants():
    n = HD // 4
    rows, cols = np.divmod(np.arange(LAT), 64)
    freqs = (10000.0 ** (-np.arange(n, dtype=np.float32) / n)).astype(np.float32)
    ang = np.concatenate([rows[:, None].astype(np.float32) * freqs, cols[:, None].astype(np.float32) * freqs], 1)
    wide = lambda f: np.tile(np.repeat(f(ang.astype(np.float64)), 2, axis=1), (1, 2)).T
    head = np.kron(np.eye(2), np.ones((HD, HD)))
    c, s = dft(HD)
    ch = np.concatenate([np.kron(np.eye(2), c), np.kron(np.eye(2), s)], 1)
    pairs = [(64 * h + 2 * i, 64 * h + 2 * i + 1) for h in range(2) for i in range(32)]
    c1 = np.concatenate([np.eye(P), np.ones((P, P)), head, rotation(pairs), wide(np.cos), wide(np.sin), ch,
                         level_masks(False), level_masks(True)], 1)
    s, t = np.arange(P)[:, None], np.arange(P)[None, :]
    halves = [(64 * h + i, 64 * h + 32 + i) for h in range(2) for i in range(32)]
    inv_freq = (10000.0 ** (-np.arange(32, dtype=np.float32) / 32)).astype(np.float32)
    c2 = np.concatenate([(s <= t), (s >= t)] + [half_mask(1 << l, back) for back in (False, True) for l in range(LEVELS)]
                        + [np.where(t >= s, 0, NEG), np.zeros((P, P)), np.where(t <= s, 0, NEG), rotation(halves),
                           np.tile(inv_freq, 4)[:, None]], 1)
    assert c1.shape[1] == N_CONST and c2.shape[1] == N_CONST2
    return c1.astype(np.float32), c2.astype(np.float32)


def in_2_order():
    return np.concatenate([head_pairs([h for i in range(4) for h in (i, i + 4)]), np.arange(512, 2816)])


def lay_out(i):
    a = {k: np.asarray(v) for k, v in i.items()}
    lat, ctx = dft_chunks()
    heads = head_pairs((0, 2, 1, 3))
    out_rows = np.concatenate([np.arange(256), 256 + heads, np.arange(512, 1024)])
    dn_rows = np.concatenate([head_pairs([h for k in range(4) for h in (k, k + 4)]), np.arange(512, 1024)])
    stream = [chunks_of(a["w_mod"][0])]
    for ly in range(DEPTH):
        stream += [chunks_of(a["w_in"][ly][:, in_order()]), lat.astype(np.float32)]
        stream += [ctx.astype(np.float32), chunks_of(a["w_mod"][1])] if ly == 0 else []
        stream += [chunks_of(a["w_out"][ly][out_rows])]
    w_in_2 = a["w_in_2"][0]
    ab = np.zeros((D, P), np.float32)
    ab[:, 0:16] = w_in_2[:, 2816:2832]
    down = np.zeros((24 * P, D), np.float32)
    down[0:2816] = a["w_down_2"][0]
    ckv = a["w_ckv_2"][0]
    gu = a["w_gate_up_2"][0].reshape(D, 2, 22, P).transpose(0, 2, 1, 3).reshape(D, 44 * P)
    stream += [chunks_of(ckv[:, 0:D]), chunks_of(ckv[:, D:]), chunks_of(w_in_2[:, in_2_order()]), chunks_of(ab),
               chunks_of(a["w_out_2"][0][dn_rows]), chunks_of(a["w_cq_2"][0]), chunks_of(a["w_co_2"][0]),
               chunks_of(gu), chunks_of_down(down)]
    weights = np.concatenate(stream, 0)
    assert weights.shape == (PLAN["end"], P, CHUNK)
    wide = lambda v: np.broadcast_to(v.reshape(1, -1), (P, v.size))
    par = {
        "c": np.stack([a["c"][0].reshape(KT, P), a["c_ctx"].reshape(KT, P)], 2).transpose(1, 0, 2).reshape(P, 2 * KT),
        "norm_g": tiles_of_rows(a["norm_g"]), "b_mod": tiles_of_rows(a["b_mod"]), "conv_w": tiles_of_rows(a["conv_w"]),
        "q_g": np.tile(a["q_norm_g"], (1, 2)).T, "k_g": np.tile(a["k_norm_g"], (1, 2)).T,
        "lb": tiles_of_rows(a["hgrn_lb"].transpose(1, 0, 2)), "hg_g": tiles_of_rows(a["hgrn_norm_g"]),
        "final_g": tiles_of_rows(a["final_g"]), "g_mix_pre": tiles_of_rows(a["g_mix_pre_2"]),
        "conv2": a["conv_w_2"][0].reshape(5, 12, P).transpose(2, 1, 0).reshape(P, 60), "a_log": wide(a["a_log_2"]),
        "dt_bias": wide(a["dt_bias_2"]), "g_dn": a["g_dn_out_2"].T, "sink": wide(a["attn_sink_2"]),
        "g_mix_post": tiles_of_rows(a["g_mix_post_2"]), "g_cross_pre": tiles_of_rows(a["g_cross_pre_2"]),
        "g_mem": tiles_of_rows(a["g_mem_2"]), "g_cross_post": tiles_of_rows(a["g_cross_post_2"]),
        "g_ffn_pre": tiles_of_rows(a["g_ffn_pre_2"]), "g_ffn_post": tiles_of_rows(a["g_ffn_post_2"]),
    }
    const, const2 = constants()
    return {
        "tokens": np.concatenate([feature_major(a["x"][0]), feature_major(a["ctx"][0])], 2),
        "mem": feature_major(a["mem_2"][0]), "positions": np.broadcast_to(a["positions_2"], (P, LAT)),
        "weights": weights, "const": const, "const2": const2,
        "par": np.concatenate([par[n] for n in PAR_COLS], 1),
    }


def chunks_of_down(w):
    return w.reshape(3, KT, P, KT, P).transpose(3, 0, 2, 1, 4).reshape(3 * KT, P, CHUNK)


def kernel(**inputs):
    import concourse.bacc as bacc
    from concourse.bass_utils import run_bass_kernel_spmd

    nc = bacc.Bacc("TRN2", target_bir_lowering=False, num_devices=1)
    arrays = {n: np.ascontiguousarray(v) for n, v in lay_out(inputs).items()}
    args = [nc.dram_tensor(n, v.shape, mybir.dt.from_np(v.dtype), kind="ExternalInput").ap() for n, v in arrays.items()]
    out = nc.dram_tensor("out", (P, KT, LAT), F32, kind="ExternalOutput").ap()
    build(nc, *args, out)
    got = run_bass_kernel_spmd(nc, [arrays], core_ids=[0]).results[0]["out"]
    return np.ascontiguousarray(got.transpose(2, 1, 0).reshape(1, LAT, D))
```

```python
from contextlib import ExitStack

import numpy as np

import concourse.bass as bass
from concourse import mybir

F32 = mybir.dt.float32
F32R = mybir.dt.float32r
I32 = mybir.dt.int32
ALU = mybir.AluOpType
ACT = mybir.ActivationFunctionType
AX = mybir.AxisListType

P = 128
D = 1024
KT = D // P
LAT, CTX = 512, 256
TOK = LAT + CTX
CH = 128
NCH, NLAT = TOK // CH, LAT // CH
EPS = 1e-6
DEPTH = 2
HD = 64
RING = 5
CHUNK = KT * P
LEVELS = 7
NEG = -1e30

HQ, HZ, FF, FB, HI, AQ, AK, AV, AZ, FU, FZ, CB, CZ, CC, CV = 0, 2, 4, 6, 8, 10, 12, 13, 14, 16, 18, 20, 22, 24, 26
NPROJ = 28
MIX = [CB, CB + 1, AZ, AZ + 1, HZ, HZ + 1, FZ, FZ + 1]
CTX_TILES_LAST = (FF, FF + 1, FB, FB + 1, HI, HI + 1, AK, AV)

N_MOD = 3 * KT
FOURIER_CHUNKS = {0: NLAT + 1, 1: NLAT}


def chunk_plan():
    at, plan = 0, {}
    for name, n in ([("mod0", N_MOD), ("proj0", NPROJ + N_MOD), ("dft0", FOURIER_CHUNKS[0]), ("out0", KT),
                     ("proj1", NPROJ), ("dft1", FOURIER_CHUNKS[1]), ("out1", KT)]
                    + [("ck", KT), ("cv", KT), ("proj_2", 22), ("ab_2", 1), ("out_2", KT), ("cq", KT), ("co", KT),
                       ("gu", 44), ("down", 3 * KT)]):
        plan[name] = at
        at += n
    plan["end"] = at
    return plan


PLAN = chunk_plan()


def where(stage, n):
    if stage == "mod1":
        return PLAN["proj0"] + 2 * n
    if stage == "proj0":
        return PLAN["proj0"] + n + min(n + 1, N_MOD)
    return PLAN[stage] + n


def split_plan():
    stages = [("proj0", NPROJ, KT), ("out0", KT, KT), ("proj1", NPROJ, KT), ("out1", KT, KT), ("proj_2", 22, KT),
              ("out_2", KT, KT), ("cq", KT, KT), ("co", KT, KT), ("gu", 44, KT), ("down", 3 * KT, 22)]
    chunks, chunk_at, tile_at, c, t = {}, {}, {}, 0, 0
    for name, n, tiles in stages:
        chunks[name], chunk_at[name], tile_at[name] = n, c, t
        c, t = c + n, t + tiles
    return chunks, chunk_at, tile_at


SPLIT_CHUNKS, SPLIT_AT, TILE_AT = split_plan()


def table(entries):
    at, out = 0, {}
    for name, n in entries:
        out[name] = (at, at + n)
        at += n
    return out, at


CONST_COLS, N_CONST = table([("ident", P), ("ones", P), ("ones_head", P), ("rot_pair", P), ("cos", LAT), ("sin", LAT),
                             ("dft_ch", 2 * P), ("level0", LEVELS * 64), ("level1", LEVELS * 64)])
CONST2_COLS, N_CONST2 = table([("tri0", P), ("tri1", P), ("inv0", LEVELS * P), ("inv1", LEVELS * P),
                               ("window", 3 * P), ("rot_half", P), ("inv_freq", 1)])
PAR_COLS, N_PAR = table([("c", 2 * KT), ("norm_g", DEPTH * KT), ("b_mod", DEPTH * N_MOD), ("conv_w", DEPTH * 6),
                         ("q_g", DEPTH), ("k_g", DEPTH), ("lb", 8), ("hg_g", DEPTH * 2), ("final_g", KT),
                         ("g_mix_pre", KT), ("conv2", 60), ("a_log", 8), ("dt_bias", 8), ("g_dn", 1), ("sink", 8),
                         ("g_mix_post", KT), ("g_cross_pre", KT), ("g_mem", KT), ("g_cross_post", KT),
                         ("g_ffn_pre", KT), ("g_ffn_post", KT)])

SPLIT_STREAM = [where(name, n) for name in SPLIT_CHUNKS for n in range(SPLIT_CHUNKS[name])]


def evacuation_plan():
    at, plan = 0, {}
    for name, n in [("proj0", NPROJ), ("out0", KT), ("proj1", NPROJ), ("out1", KT), ("ck", KT), ("cv", KT),
                    ("proj_2", 22), ("ab_2", 1), ("out_2", KT), ("cq", KT), ("co", KT), ("gu", 44), ("down", KT)]:
        plan[name] = at
        at += n
    return plan


EVAC = evacuation_plan()
N_LAYER0, N_LAYER1, N_MEM, N_FINAL, N_MIX_PRE, N_MIX_POST, N_CROSS_PRE, N_CROSS_POST, N_FFN_PRE, N_FFN_POST = range(10)


def order(back, with_latent=True):
    return [5, 4, 3, 2, 1, 0] if back else [4, 5, 0, 1, 2, 3]


def halves(ap, b):
    return ap.rearrange("p (n two b) -> p n two b", two=2, b=b)


def build(nc, tokens, mem, positions, weights, const_d, const2_d, par_d, out):
    with ExitStack() as ctx:
        def sb(name, shape, dt=F32):
            return ctx.enter_context(nc.sbuf_tensor(name, shape, dt))

        def sem(name):
            return ctx.enter_context(nc.semaphore(name))

        h = sb("h", [P, KT, TOK])
        shapes = {"xn": [P, KT * TOK],
                  "proj": [P, NPROJ, TOK],
                  "ring": [P, RING, CHUNK],
                  "const_sb": [P, N_CONST],
                  "work": [P, 8, TOK],
                  "scratch": [P, 2 * CHUNK],
                  "state": [P, 2, NCH, HD],
                  "qe_2": [P, TOK],
                  "conv_tmp": [P, TOK]}
        with ExitStack() as same_place:
            bufs = {n: same_place.enter_context(nc.sbuf_tensor(n, shape, F32)) for n, shape in shapes.items()}
        rounded_bufs = {n: sb(n + "_r", shape, F32R) for n, shape in shapes.items()}
        xn, proj, ring, const, work, scratch, state, qe_2, conv_tmp = bufs.values()

        def as_r(ap):
            return bass.AP(tensor=rounded_bufs[ap.tensor.name], offset=ap.offset, ap=ap.ap)

        par = sb("par_sb", [P, N_PAR])
        zero = sb("zero", [P, P])
        eps = sb("eps", [P, 1])
        small = sb("small", [P, 520 + P])
        wide_ps = ctx.enter_context(nc.psum_tensor("wide_ps", [P, 2, 1024], F32))
        pair_ps = ctx.enter_context(nc.psum_tensor("pair_ps", [P, 1024], F32))
        duo_ps = ctx.enter_context(nc.psum_tensor("duo_ps", [P, 1024], F32))

        xn_t = xn[:, :].rearrange("p (k t) -> p k t", k=KT)
        cst = {n: const[:, a:b] for n, (a, b) in CONST_COLS.items()}
        prm = {n: par[:, a:b] for n, (a, b) in PAR_COLS.items()}
        c_act = small[:, 0:16]
        mod = small[:, 16:112].rearrange("p (l n s) -> p l n s", l=DEPTH, n=N_MOD)
        mod_scale = small[:, 112:144].rearrange("p (l n s) -> p l n s", l=DEPTH, n=KT)
        lb_e, lb_log, lb_log1m, lb_neg = (small[:, 144 + 4 * n:148 + 4 * n] for n in range(4))
        f_last = small[:, 160:166]
        row_max, neg_max, row_sum, row_inv = (small[:, 168 + 8 * n:176 + 8 * n] for n in range(4))
        masked = scratch[:, 0:4 * LEVELS * 64].rearrange("p (n t) -> p n t", n=4)
        w_lead = scratch[:, :].rearrange("p (n t) -> p n t", n=2)
        state_flat = state[:, :, :, :].rearrange("p d c f -> p (d c f)")
        sq = work[:, 0:2]
        root = work[:, 2]
        resid = work[:, 3:5]
        lf_b, a_b, e_b, m_b, ke_b, kt_b = (work[:, n] for n in range(6))
        v_tok = work[:, 6:8].rearrange("p j t -> p (j t)").rearrange("p (j c f) -> p j c f", j=2, c=NCH)
        k_tok = kt_b.rearrange("p (c f) -> p c f", c=NCH)

        def decay(u, l):
            if u % 2 == 0:
                return xn_t[:, l, :]
            return proj[:, CZ + l, :] if l < LEVELS - 1 else conv_tmp[:, :]

        def q_decayed(u):
            return qe_2[:, :] if u % 2 else xn_t[:, LEVELS, :]


        setup_landed = sem("setup_landed")
        tokens_landed = [sem(f"tokens_landed{n}") for n in range(KT // 2)]
        landed = [sem(f"chunk_landed{n}") for n in range(RING)]
        chunk_used = sem("chunk_used")
        evacuated = sem("evacuated")
        dve_chain, act_chain, pool_chain = sem("dve_chain"), sem("act_chain"), sem("pool_chain")
        ready = sem("fixed_ready")
        c_ready = sem("c_ready")
        mod_row_sum, mod_row, mod_row_used, mod_turned = (
            sem(n) for n in ("mod_row_sum", "mod_row", "mod_row_used", "mod_turned"))
        mod_ready = sem("mod_ready")
        lb_ready = sem("lb_ready")
        sq_ready, sq_used = sem("sq_ready"), sem("sq_used")
        root_ready = sem("root_ready")
        scaled = sem("scaled")
        xn_ready = sem("xn_ready")
        h_ready = sem("h_ready")
        vt_ps, vt_ready = sem("vt_ps"), sem("vt_ready")
        hg_soft, hg_lf, hg_k, hg_lb, hg_a = sem("hg_soft"), sem("hg_lf"), sem("hg_k"), sem("hg_lb"), sem("hg_a")
        hg_abs = sem("hg_abs")
        hg_ea, hg_qe, hg_ed0, hg_ed, hg_ke = sem("hg_ea"), sem("hg_qe"), sem("hg_ed0"), sem("hg_ed"), sem("hg_ke")
        hg_kt_ps, hg_kt, hg_u, hg_s = sem("hg_kt_ps"), sem("hg_kt"), sem("hg_u"), sem("hg_s")
        lev_diff, lev_exp, lev_ready = sem("lev_diff"), sem("lev_exp"), sem("lev_ready")
        sc_ps, sc_ready, sc_used = sem("sc_ps"), sem("sc_ready"), sem("sc_used")
        hg_o_ps, hg_qk, hg_diag, hg_o, hg_sq, hg_ms, hg_rt, hg_out = (
            sem(n) for n in ("hg_o_ps", "hg_qk", "hg_diag", "hg_o", "hg_sq", "hg_ms", "hg_rt", "hg_out"))
        qk_sq, qk_ms, qk_rt, qk_norm, qk_rot, qk_ready = (
            sem(n) for n in ("qk_sq", "qk_ms", "qk_rt", "qk_norm", "qk_rot", "qk_ready"))
        at_s, at_max, at_exp, at_p, at_pt_ps, at_pt, at_o_ps, at_out = (
            sem(n) for n in ("at_s", "at_max", "at_exp", "at_p", "at_pt_ps", "at_pt", "at_o_ps", "at_out"))
        ft_a_ps, ft_a, ft_y_ps, ft_out = (sem(n) for n in ("ft_a_ps", "ft_a", "ft_y_ps", "ft_out"))
        conv_out = sem("conv_out")
        w_lead_ready, w_split = sem("w_lead_ready"), sem("w_split")
        lead_ready = sem("lead_ready")
        x_lead, x_split = sem("x_lead"), sem("x_split")
        norm_lead = sem("norm_lead")
        mix_split_lead, mix_split = sem("mix_split_lead"), sem("mix_split")
        final_ready = sem("final_ready")
        stored = sem("stored")

        def width(ly, tile):
            return TOK if ly == 0 or tile in CTX_TILES_LAST else LAT

        def pieces(w):
            return [(0, w)] if w <= LAT else [(0, LAT), (LAT, TOK)]

        def chunk_list(ly):
            return range(NCH) if ly == 0 else range(NLAT)

        def att_units(ly):
            return [(i, r, c) for i in range(2) for r in range(2) for c in chunk_list(ly)]

        def keys_of(c):
            return (0, TOK) if c < NLAT else (LAT, TOK)

        ATT0 = {0: 0, 1: len(att_units(0))}
        SC0 = {u: sum(2 * len(chunk_list(v // 4)) for v in range(u)) for u in range(9)}
        qk_square, qk_root, qk_turned = root, qe_2[:, :], state_flat
        SILU_TILES = [t + j for t in (HQ, HZ, AZ, FZ, CZ) for j in range(2)]
        QK_STEP = 4

        def qk_tiles(ly):
            return [(AQ, width(ly, AQ)), (AQ + 1, width(ly, AQ)), (AK, TOK)]

        def hg_units(ly):
            return [(ly * 4 + 2 * j + d, j, d) for j in range(2) for d in range(2)]

        probs = lambda m: xn[:, TOK * (m % 3):TOK * (m % 3) + TOK]
        probs_t = lambda m: xn[:, TOK * (3 + m % 2):TOK * (4 + m % 2)]
        ft_buf = scratch[:, 0:1024].rearrange("p (t f) -> p t f", t=NLAT)

        def ft_steps(ly):
            return [(s, j, tt) for s in (0, 1)[:2 - ly] for j in range(2) for tt in range((NLAT, 2)[s])]

        FT0 = {0: 0, 1: 12}
        mod_ps = [duo_ps[:, 512 * ly:512 * ly + 2 * N_MOD] for ly in range(DEPTH)]
        mod_row_ps = lambda ly, n: wide_ps[0:2, n % 2, 0:P] if ly == 0 else duo_ps[0:2, 512 + P:512 + 2 * P]
        mod_row_sb = lambda ly, n: work[0:2, 3 + n % 2, 0:P] if ly == 0 else small[0:2, 520:520 + P]
        ft_bank = lambda s, j: wide_ps[:, j, :] if s else duo_ps[:, 512 * j:512 * j + 512]


        def lead_tile(k):
            return conv_tmp[:, :] if k == 2 else work[:, k, :]

        def mix_lead(k):
            return (xn_t[:, 5, :], xn_t[:, 6, :], state_flat, xn_t[:, 0, :], xn_t[:, 7, :], work[:, 5, :],
                    conv_tmp[:, :], qe_2[:, :])[k]

        X_SPLITS = {"proj0": 0, "out0": KT, "proj1": KT + 1, "out1": 2 * KT + 1, "proj_2": 2 * KT + 2,
                    "out_2": 3 * KT + 2, "cq": 3 * KT + 6, "gu": 4 * KT + 6, "down": 5 * KT + 6}
        MIX_ORDER = [0, 1, 4, 5, 6, 7, 2, 3]
        flat = proj[:, :, :].rearrange("p n t -> p (n t)")
        spot = [0]

        def place(n):
            spot[0] += n
            return flat[:, spot[0] - n:spot[0]]

        x_2 = h[:, :, 0:LAT]
        mem_x = h[:, :, LAT:TOK]
        tile_2 = place(22 * LAT).rearrange("p (n t) -> p n t", t=LAT)
        const2 = place(N_CONST2)
        cst2 = {n: const2[:, a:b] for n, (a, b) in CONST2_COLS.items()}
        key_c = place(KT * CTX).rearrange("p (k t) -> p k t", k=KT)
        val_c = place(2 * D).rearrange("p (t n) -> p t n", t=2)
        cos_2, sin_2 = place(LAT), place(LAT)
        o_dn = place(4 * LAT).rearrange("p (h t) -> p h t", h=4)
        q_c, o_c = tile_2[:, 0:KT, :], tile_2[:, KT:2 * KT, :]
        y_2 = xn_t[:, :, 0:LAT]
        pos_i = state_flat[:, 0:LAT].bitcast(I32)
        conv_y = [state_flat[:, 0:LAT], qe_2[:, 0:LAT]]
        l2_square, l2_root = o_dn[:, 0:2], o_dn[:, 2:4]
        squares = lambda n: o_dn[:, 0:2] if n == N_CROSS_POST else sq
        up_2 = conv_y

        def mix2_lead(k):
            return (tile_2[:, AK2, :], tile_2[:, AV2, :], conv_y[0], conv_y[1])[k] if k < 4 else tile_2[:, DQ2 + k, :]

        def hidden_lead(t):
            return flat[:, (22 + t) * LAT:(23 + t) * LAT] if t < 20 else cst[("cos", "sin")[t - 20]]

        quad = lambda m: wide_ps[:, m // 2 % 2, 512 * (m % 2):512 * (m % 2) + 512]
        twin = lambda m: pair_ps[:, 512 * (m % 2):512 * (m % 2) + 512]
        half_pi = small[:, 210:211]
        row_max2, neg_max2, row_sum2, row_inv2, sink_e = (small[:, 212 + 4 * n:216 + 4 * n] for n in range(5))
        ab = small[:, 240:304].rearrange("p (c n) -> p c n", c=NLAT)
        g_tok, g_soft, beta, g_cum, g_exp, beta_g = (
            small[:, 304 + 32 * n:336 + 32 * n].rearrange("p (c n) -> p c n", c=NLAT) for n in range(6))
        a_exp = small[:, 496:504]
        g_end = small[:, 504:512].rearrange("p (d n) -> p d n", d=2)
        s_decay = small[:, 512:520].rearrange("p (d n) -> p d n", d=2)
        dn_store = [xn[:, :].rearrange("p (n h t) -> p n h t", n=12, h=4),
                    work[:, :, :].rearrange("p n t -> p (n t)").rearrange("p (n h t) -> p n h t", n=12, h=4)]
        XT, T, R, Y, XM, QK, KBG, VB, KG, WT, VN, QG = range(12)
        s_dn = scratch[:, 0:1024].rearrange("p (d h v) -> p d h v", d=2, h=4)

        def dn(d, name):
            return dn_store[d][:, name]

        def dn_bank(d, n):
            ps = (wide_ps[:, n // 2, 512 * (n % 2):512 * (n % 2) + 512] if d == 0
                  else (pair_ps, duo_ps)[n // 2][:, 512 * (n % 2):512 * (n % 2) + 512])
            return ps.rearrange("p (h t) -> p h t", h=4)

        def chunk_at(d, s):
            return s if d == 0 else NLAT - 1 - s

        AQ2, AK2, AV2, DQ2, DK2, DV2, DG2 = 0, 4, 5, 6, 10, 14, 18
        MIX2 = [0, 1, 2, 3, DG2, DG2 + 1, DG2 + 2, DG2 + 3]
        WIN = [(i, r, c) for i in range(4) for r in range(2) for c in range(NLAT)]
        CROSS = [(hd, c) for hd in range(4) for c in range(NLAT)]

        def window_keys(c):
            a, b = max(c - 1, 0), min(c + 2, NLAT)
            return a * P, b * P, (a - c + 1) * P, (b - c + 1) * P

        const2_landed, mem_landed, pos_landed = sem("const2_landed"), sem("mem_landed"), sem("pos_landed")
        x_ready = sem("x_ready")
        rope_arg, rope_table = sem("rope_arg"), sem("rope_table")
        cv_sum, cv_ready = sem("cv_sum"), sem("cv_ready")
        l2_sq, l2_ss, l2_rt, l2_ready = sem("l2_sq"), sem("l2_ss"), sem("l2_rt"), sem("l2_ready")
        rp_rot, rp_ready = sem("rp_rot"), sem("rp_ready")
        v2_ps, v2_ready = sem("v2_ps"), sem("v2_ready")
        w_s, w_max, w_exp, w_p, w_pt_ps, w_pt, w_o_ps, w_out_s = (
            sem(n) for n in ("w_s", "w_max", "w_exp", "w_p", "w_pt_ps", "w_pt", "w_o_ps", "w_out"))
        g_x, g_l, g_ready, g_ps, g_c, g_e, g_b = (sem(n) for n in ("g_x", "g_l", "g_ready", "g_ps", "g_c", "g_e", "g_b"))
        dn_a, dn_diff, dn_exp, dn_x, dn_row, dn_tok_ps, dn_tok = (
            sem(n) for n in ("dn_a", "dn_diff", "dn_exp", "dn_x", "dn_row", "dn_tok_ps", "dn_tok"))
        dn_qg, dn_xm, dn_y_ps, dn_y, dn_z_ps, dn_t = (sem(n) for n in ("dn_qg", "dn_xm", "dn_y_ps", "dn_y", "dn_z_ps", "dn_t"))
        dn_w_ps, dn_w, dn_v_ps, dn_v, dn_o_ps, dn_s = (sem(n) for n in ("dn_w_ps", "dn_w", "dn_v_ps", "dn_v", "dn_o_ps", "dn_s"))
        do_sq, do_ss, do_rt, do_out = (sem(n) for n in ("do_sq", "do_ss", "do_rt", "do_out"))
        c_s, c_max, c_exp, c_p, c_pt_ps, c_pt, c_o_ps, c_out = (
            sem(n) for n in ("c_s", "c_max", "c_exp", "c_p", "c_pt_ps", "c_pt", "c_o_ps", "c_out"))
        ffn_ready = sem("ffn_ready")

        block = ctx.enter_context(nc.Block())

        @block.sync
        def _(sp):
            sp.dma_start(par[:, :], par_d).then_inc(setup_landed, 16)
            sp.dma_start(const[:, :], const_d).then_inc(setup_landed, 16)
            lead = -(-(N_MOD + 1) // RING) * RING
            for c in range(lead):
                if c >= RING:
                    sp.wait_ge(chunk_used, c - RING + 1)
                sp.dma_start(ring[:, c % RING, :], weights[c]).then_inc(landed[c % RING], 16)
                if c < KT // 2:
                    part = slice(2 * c, 2 * c + 2)
                    sp.dma_start(h[:, part, :], tokens[:, part, :]).then_inc(tokens_landed[c], 16)
            turns = (PLAN["end"] - lead) // RING
            with sp.Fori(0, turns) as turn:
                for s in range(RING):
                    sp.wait_ge(chunk_used, turn * RING + (lead - RING + s + 1))
                    sp.dma_start(ring[:, s, :], weights[turn * RING + (lead + s)]).then_inc(landed[s], 16)
            for c in range(lead + turns * RING, PLAN["end"]):
                sp.wait_ge(chunk_used, c - RING + 1)
                sp.dma_start(ring[:, c % RING, :], weights[c]).then_inc(landed[c % RING], 16)
            sp.wait_ge(final_ready, KT)
            sp.dma_start(out, h[:, :, 0:LAT]).then_inc(stored, 16)
            sp.wait_ge(stored, 16)

        @block.gpsimd
        def _(pool):
            def link(ins):
                pool_count[0] += 1
                ins.then_inc(pool_chain, 1)
                pool.wait_ge(pool_chain, pool_count[0])

            pool_count = [0]
            pool.memset(zero[:, :], 0.0).then_inc(ready, 1)
            pool.memset(eps[:, :], EPS).then_inc(ready, 1)

            lead_count = [0]

            def split(src, lead, done):
                lead_count[0] += 1
                pool.tensor_copy(as_r(lead), src).then_inc(lead_ready, 1)
                pool.wait_ge(lead_ready, lead_count[0])
                pool.tensor_tensor(as_r(src), src, as_r(lead).bitcast(F32), ALU.subtract).then_inc(done, 1)

            def split_weights(stage, chunks=None):
                for n in chunks or range(SPLIT_CHUNKS[stage]):
                    c, m = where(stage, n), SPLIT_AT[stage] + n
                    pool.wait_ge(w_lead_ready, m + 1)
                    wt = ring[:, c % RING, :]
                    pool.tensor_tensor(as_r(wt), wt, as_r(w_lead[:, m % 2, :]).bitcast(F32), ALU.subtract).then_inc(w_split, 1)

            def split_mix(ly):
                w = width(ly, HQ)
                split_weights(f"out{ly}", range(2))
                pool.wait_ge(hg_out, 2 * ly + 2)
                for k in MIX_ORDER[0:6]:
                    split(proj[:, MIX[k], 0:w], mix_lead(k)[:, 0:w], mix_split)
                pool.wait_ge(at_out, ATT0[ly] + len(att_units(ly)) // 2)
                split(proj[:, AZ, 0:w], mix_lead(2)[:, 0:w], mix_split)
                split_weights(f"out{ly}", range(2, KT))

            def conv(ly):
                w = width(ly, CB)
                taps = prm["conv_w"].rearrange("p (l t j) -> p l t j", l=DEPTH, t=3)
                for j in range(2):
                    cb, cc, cv, cz, tmp = proj[:, CB + j, 0:w], proj[:, CC + j, 0:w], proj[:, CV + j, 0:w], proj[:, CZ + j, 0:w], conv_tmp[:, 0:w]
                    pool.wait_ge(evacuated, EVAC[f"proj{ly}"] + NPROJ)
                    link(pool.tensor_tensor(cc, cc, cv, ALU.mult))
                    link(pool.tensor_scalar(cv, cc, taps[:, ly, 1, j:j + 1], None, ALU.mult))
                    for tap, to, frm in ((0, 1, 0), (2, 0, 1)):
                        link(pool.tensor_scalar(tmp, cc, taps[:, ly, tap, j:j + 1], None, ALU.mult))
                        for a, b in pieces(w):
                            n = b - a - 1
                            link(pool.tensor_tensor(cv[:, a + to:a + to + n], cv[:, a + to:a + to + n],
                                                    tmp[:, a + frm:a + frm + n], ALU.add))
                    link(pool.tensor_tensor(cv, cv, cb, ALU.mult))
                    pool.tensor_tensor(cb, cv, cz, ALU.mult).then_inc(conv_out, 1)
                    pool.wait_ge(conv_out, 2 * ly + j + 1)

            def level_differences(u, d, ly):
                w = TOK if ly == 0 else LAT
                pool.wait_ge(hg_a, u + 1)
                if u >= 2:
                    pool.wait_ge(sc_ps, SC0[u - 1])
                for l in range(LEVELS):
                    b = 1 << l
                    a, o = halves(a_b[:, 0:w], b), halves(decay(u, l)[:, 0:w], b)
                    q, k = (1, 0) if d == 0 else (0, 1)
                    ref = a[:, :, 0, b - 1:b] if d == 0 else a[:, :, 1, 0:1]
                    ref = ref.broadcast_to([P, w // (2 * b), b])
                    pool.tensor_tensor(o[:, :, q, :], a[:, :, q, :], ref, ALU.subtract).then_inc(lev_diff, 1)
                    pool.tensor_tensor(o[:, :, k, :], ref, a[:, :, k, :], ALU.subtract).then_inc(lev_diff, 1)

            def diagonal(ly, j):
                w = width(ly, HQ)
                u = ly * 4 + 2 * j + 1
                pool.wait_ge(lev_ready, LEVELS * (u + 1))
                pool.wait_ge(hg_ke, u + 1)
                link(pool.tensor_tensor(proj[:, FF + j, 0:w], proj[:, FF + j, 0:w], proj[:, FB + j, 0:w], ALU.add))
                pool.tensor_tensor(proj[:, FF + j, 0:w], proj[:, FF + j, 0:w], proj[:, HQ + j, 0:w], ALU.mult).then_inc(hg_qk, 1)

            for ly in range(DEPTH):
                split_weights(f"proj{ly}")
                for u, j, d in hg_units(ly):
                    level_differences(u, d, ly)
                    if d == 1:
                        diagonal(ly, j)
                    if u % 4 == 0:
                        conv(ly)
                        pool.wait_ge(conv_out, 2 * ly + 2)
                split_mix(ly)
            split_weights("proj_2")
            for s in range(NLAT):
                for l in range(LEVELS):
                    for d in range(2):
                        g, c = 2 * s + d, chunk_at(d, s)
                        if l == 0:
                            pool.wait_ge(dn_x, 2 * g + 2)
                        elif l == 1:
                            pool.wait_ge(dn_t, 2 * (LEVELS * s) + d + 1)
                        else:
                            pool.wait_ge(dn_y_ps, 2 * (6 * s + l - 2) + d + 1)
                        mask = cst2[f"inv{d}"][:, l * P:(l + 1) * P].unsqueeze(1).broadcast_to([P, 4, CH])
                        if l:
                            pool.tensor_tensor(dn(d, XM), dn(d, XT), mask, ALU.mult).then_inc(dn_xm, 1)
                        if l == 0:
                            q = tile_2[:, DQ2:DQ2 + 4, c * CH:(c + 1) * CH]
                            pool.tensor_tensor(dn(d, QG), dn(d, QG), q, ALU.mult).then_inc(dn_qg, 1)
                            pool.tensor_tensor(dn(d, QK), dn(d, QK), cst2[f"tri{d}"].unsqueeze(1).broadcast_to([P, 4, CH]),
                                               ALU.mult).then_inc(dn_qg, 1)
                pool.wait_ge(w_out_s, len(WIN))
                split(tile_2[:, MIX2[s], :], mix2_lead(s), mix_split)
            split_weights("out_2", range(2))
            split_weights("out_2", range(2, KT))
            split_weights("cq")
            split_weights("co", range(2))
            for k in range(KT):
                pool.wait_ge(c_out, NLAT * (k // 2 + 1))
                split(o_c[:, k, :], lead_tile(k)[:, 0:LAT], mix_split)
            split_weights("co", range(2, KT))
            for stage in ("gu", "down"):
                split_weights(stage)

        @block.scalar
        def _(act):
            act_count = [0]

            def link(ins):
                act_count[0] += 1
                ins.then_inc(act_chain, 1)
                act.wait_ge(act_chain, act_count[0])

            logs_loaded = [False]

            def logs_and_exps():
                if not logs_loaded[0]:
                    act.preload_act_table_set("natural_log_exp_and_others")
                    logs_loaded[0] = True

            def other(func):
                logs_loaded[0] = False
                return func

            def inverse_root(dst, src, scale, done):
                logs_and_exps()
                link(act.activation(dst, src, ACT.Ln, bias=eps[:, 0:1], scale=scale))
                act.activation(dst, dst, ACT.Exp, scale=-0.5).then_inc(done, 1)

            def square(n, k, src, w):
                if 8 * n + k >= 2:
                    act.wait_ge(sq_used, 8 * n + k - 1)
                act.activation(squares(n)[:, k % 2, 0:w], src, ACT.Square).then_inc(sq_ready, 1)

            def mean_root(n, w):
                logs_and_exps()
                act.wait_ge(sq_used, 8 * (n + 1))
                if n:
                    act.wait_ge(scaled, 8 * n)
                inverse_root(root[:, 0:w], pair_ps[:, 0:w], 1.0 / D, root_ready)

            def norm_root(n, src, w, source_ready):
                for k in range(KT):
                    source_ready(k)
                    square(n, k, src(k), w)
                mean_root(n, w)

            def modulation_row(ly, n):
                m = N_MOD * ly + n
                act.wait_ge(mod_row_sum, m + 1)
                if m >= 2:
                    act.wait_ge(mod_row_used, m - 1)
                act.activation(mod_row_sb(ly, n), mod_row_ps(ly, n), ACT.Copy).then_inc(mod_row, 1)

            def evacuate(stage, tile, chunks, w, dst, func=ACT.Copy):
                g = EVAC[stage] + tile
                act.wait_ge(chunk_used, chunks)
                act.activation(dst, wide_ps[:, g % 2, 0:w], func).then_inc(evacuated, 1)
                act.wait_ge(evacuated, g + 1)

            def weight_leads(stage, n, count=1):
                for i in range(n, n + count):
                    c, m = where(stage, i), SPLIT_AT[stage] + i
                    act.wait_ge(landed[c % RING], 16 * (c // RING + 1))
                    if m >= 2:
                        act.wait_ge(chunk_used, SPLIT_STREAM[m - 2] + 1)
                    act.activation(as_r(w_lead[:, m % 2, :]), ring[:, c % RING, :], ACT.Copy).then_inc(w_lead_ready, 1)

            def leads_after(stage, tile, following=None):
                n = SPLIT_CHUNKS[stage]
                step = 3 if stage == "down" else 1
                for i in range(step * tile + 2, step * tile + 2 + step):
                    if i < n:
                        weight_leads(stage, i)
                    elif following:
                        weight_leads(following, i - n)

            def modulate(ly):
                act.wait_ge(mod_ready, 2 * (ly + 1))
                for k in range(KT):
                    act.wait_ge(scaled, 8 * ly + k + 1)
                    for s, (a, b) in enumerate(pieces(TOK)):
                        act.activation(xn_t[:, k, a:b], xn_t[:, k, a:b], ACT.Identity, bias=mod[:, ly, k, s:s + 1],
                                       scale=mod_scale[:, ly, k, s:s + 1]).then_inc(xn_ready, 1)

            def lower_bounds():
                act.wait_ge(lb_ready, 1)
                logs_and_exps()
                link(act.activation(lb_log, lb_e, ACT.Abs))
                link(act.activation(lb_log, lb_log, ACT.Exp, scale=-1.0))
                act.activation(lb_log, lb_log, ACT.Ln, bias=1.0).then_inc(lb_ready, 1)

            def softplus(u, j, d):
                z = proj[:, (FF, FB)[d] + j, :]
                if u % 4:
                    act.wait_ge(hg_ke, u)
                logs_and_exps()
                link(act.activation(e_b, z, ACT.Abs))
                link(act.activation(e_b, e_b, ACT.Exp, scale=-1.0))
                act.activation(e_b, e_b, ACT.Ln, bias=1.0).then_inc(hg_soft, 1)

            def hgrn_unit_start(ly, u, j, d):
                z = proj[:, (FF, FB)[d] + j, :]
                act.wait_ge(hg_lf, u + 1)
                bias = 0.0 if ly == 0 else lb_log1m[:, 2 * d + j:2 * d + j + 1]
                act.activation(z, m_b, ACT.Exp, bias=bias, scale=-1.0).then_inc(hg_k, 1)
                if ly == 1:
                    act.wait_ge(hg_lb, 2 * (u - 4) + 1)
                    link(act.activation(e_b, lf_b, ACT.Abs, bias=lb_neg[:, 2 * d + j:2 * d + j + 1]))
                    link(act.activation(e_b, e_b, ACT.Exp, scale=-1.0))
                    act.activation(e_b, e_b, ACT.Ln, bias=1.0).then_inc(hg_abs, 1)
                act.wait_ge(hg_a, u + 1)
                act.wait_ge(hg_k, u + 1)
                act.activation(m_b, a_b, ACT.Exp).then_inc(hg_ea, 1)
                last = a_b.rearrange("p (c t) -> p c t", t=CH)[:, :, CH - 1 if d == 0 else 0]
                act.activation(f_last, last, ACT.Exp).then_inc(hg_ea, 1)
                act.wait_ge(hg_ed0, u + 1)
                act.activation(e_b, e_b, ACT.Exp).then_inc(hg_ed, 1)

            def level_decay(ly, u, l):
                w = TOK if ly == 0 else LAT
                act.wait_ge(lev_diff, 2 * (LEVELS * u + l + 1))
                act.activation(decay(u, l)[:, 0:w], decay(u, l)[:, 0:w], ACT.Exp).then_inc(lev_exp, 1)

            def keys_by_token(u):
                act.wait_ge(hg_kt_ps, u + 1)
                act.activation(kt_b, wide_ps[:, 0, 0:TOK], ACT.Copy).then_inc(hg_kt, 1)

            def head_square(ly, j):
                n = 2 * ly + j
                w = width(ly, HQ)
                act.wait_ge(hg_o, n + 1)
                act.activation(proj[:, HI + j, 0:w], proj[:, FF + j, 0:w], ACT.Square).then_inc(hg_sq, 1)

            def head_root(ly, j):
                n = 2 * ly + j
                w = width(ly, HQ)
                act.wait_ge(hg_ms, n + 1)
                inverse_root(proj[:, FB + j, 0:w], wide_ps[:, 1, 0:w], 1.0 / HD, hg_rt)

            def query_key_norm(ly, tile):
                n, step = divmod(tile - AK, QK_STEP)
                if tile < AK or n > 2:
                    return
                t, w = qk_tiles(ly)[n]
                m = 3 * ly + n
                if step == 0:
                    act.activation(qk_square[:, 0:w], proj[:, t, 0:w], ACT.Square).then_inc(qk_sq, 1)
                if step == 2:
                    act.wait_ge(qk_ms, m + 1)
                    if m:
                        act.wait_ge(qk_norm, m)
                    inverse_root(qk_root[:, 0:w], pair_ps[:, 0:w], 1.0 / HD, qk_rt)

            def attention(ly):
                act.wait_ge(vt_ps, 3 * ly + 3)
                act.activation(v_tok[:, 0], pair_ps[:, 0:TOK].rearrange("p (c f) -> p c f", c=NCH), ACT.Copy).then_inc(vt_ready, 1)
                units = att_units(ly)
                for n in range(len(units) + 2):
                    if n >= 2:
                        probs_transposed(ATT0[ly] + n - 2, keys_of(units[n - 2][2]))
                    if n >= len(units):
                        continue
                    m = ATT0[ly] + n
                    a, b = keys_of(units[n][2])
                    act.wait_ge(at_max, m + 1)
                    if n >= 3:
                        act.wait_ge(at_pt_ps, m - 2)
                    act.activation(probs(m)[:, a:b], wide_ps[:, m % 2, a:b], ACT.Exp, bias=neg_max[:, m % 4:m % 4 + 1],
                                   scale=HD ** -0.5, accum_out=row_sum[:, m % 4:m % 4 + 1]).then_inc(at_exp, 1)

            def probs_transposed(m, keys):
                a, b = keys
                act.wait_ge(at_pt_ps, m + 1)
                if m >= 2:
                    act.wait_ge(at_o_ps, m - 1)
                act.activation(probs_t(m)[:, a:b], pair_ps[:, a:b], ACT.Copy).then_inc(at_pt, 1)

            def fourier_step(ly, n):
                s, j, tt = ft_steps(ly)[n]
                m = FT0[ly] + n
                act.wait_ge(ft_a_ps, m + 1)
                if tt == 0 and (ly or s or j):
                    act.wait_ge(ft_y_ps, 4 * ly + 2 * s + j)
                act.activation(ft_buf[:, tt, :], pair_ps[:, 512 * (m % 2):512 * (m % 2) + 256], ACT.Copy).then_inc(ft_a, 1)

            def output(ly):
                for n in range(KT):
                    if ly and n < 4:
                        for k in (2 * n, 2 * n + 1):
                            if k == 0:
                                act.wait_ge(mem_landed, 16)
                            square(N_MEM, k, mem_x[:, k, :], CTX)
                    if ly and n == 4:
                        mean_root(N_MEM, CTX)
                    leads_after(f"out{ly}", n, "proj1" if ly == 0 else None)
                    g = EVAC[f"out{ly}"] + n
                    act.wait_ge(chunk_used, PLAN[f"out{ly}"] + n + 1)
                    if 8 * ly + n >= 2:
                        act.wait_ge(h_ready, 8 * ly + n - 1)
                    w = width(ly, HQ)
                    for s, (a, b) in enumerate(pieces(w)):
                        ins = act.activation(resid[:, n % 2, a:b], wide_ps[:, g % 2, a:b], ACT.Copy,
                                             scale=mod[:, ly, 2 * KT + n, s:s + 1])
                        if b == w:
                            ins.then_inc(evacuated, 1)
                    if ly == 0 and n:
                        square_of_stream(ly, n - 1, w)
                    if ly and n >= 5:
                        square_of_stream(ly, 2 * n - 10, w)
                        square_of_stream(ly, 2 * n - 9, w)
                for k in range(KT - 1 if ly == 0 else KT - 2, KT):
                    square_of_stream(ly, k, w)
                mean_root((N_LAYER1, N_FINAL)[ly], w)

            def square_of_stream(ly, k, w):
                act.wait_ge(h_ready, KT * ly + k + 1)
                square((N_LAYER1, N_FINAL)[ly], k, h[:, k, 0:w], w)

            act.wait_ge(setup_landed, 32)
            act.wait_ge(ready, 2)
            act.activation(c_act, prm["c"], other(ACT.Silu)).then_inc(c_ready, 1)
            lower_bounds()
            for ly in range(DEPTH):
                w = TOK
                if ly == 0:
                    for n in range(N_MOD):
                        k = n - 4
                        if 0 <= k < KT:
                            act.wait_ge(tokens_landed[k // 2], 16)
                            square(0, k, h[:, k, :], TOK)
                        if k == KT:
                            mean_root(0, TOK)
                        modulation_row(0, n)
                    weight_leads("proj0", 0, 2)
                modulate(ly)
                for t in range(NPROJ):
                    if ly == 0 and t < N_MOD:
                        modulation_row(1, t)
                    leads_after(f"proj{ly}", t)
                    evacuate(f"proj{ly}", t, where(f"proj{ly}", t) + 1, width(ly, t), proj[:, t, 0:width(ly, t)],
                             other(ACT.Silu) if t in SILU_TILES else ACT.Copy)
                    query_key_norm(ly, t)
                for j in range(2):
                    act.wait_ge(vt_ps, 3 * ly + j + 1)
                    act.activation(v_tok[:, j], duo_ps[:, 0:TOK].rearrange("p (c f) -> p c f", c=NCH), ACT.Copy).then_inc(vt_ready, 1)
                if ly:
                    act.dma_start(mem_x, mem).then_inc(mem_landed, 16)
                softplus(4 * ly, 0, 0)
                u, j, d = hg_units(ly)[0]
                steps = len(ft_steps(ly))
                for n in range(steps):
                    fourier_step(ly, n)
                    if n == 3:
                        hgrn_unit_start(ly, u, j, d)
                    if 4 <= n < 4 + LEVELS:
                        level_decay(ly, u, n - 4)
                for l in range(steps - 4, LEVELS):
                    level_decay(ly, u, l)
                keys_by_token(u)
                for u, j, d in hg_units(ly)[1:]:
                    if u % 4 == 3:
                        head_square(ly, 0)
                    softplus(u, j, d)
                    hgrn_unit_start(ly, u, j, d)
                    for l in range(LEVELS):
                        level_decay(ly, u, l)
                        if l == 1 and u % 4 == 3:
                            head_root(ly, 0)
                        if l == 2:
                            keys_by_token(u)
                head_square(ly, 1)
                head_root(ly, 1)
                act.wait_ge(sc_used, SC0[4 * ly + 4])
                weight_leads(f"out{ly}", 0, 2)
                attention(ly)
                output(ly)
            act.wait_ge(chunk_used, PLAN["out1"] + KT)
            act.dma_start(const2, const2_d).then_inc(const2_landed, 16)
            act.wait_ge(hg_out, 4)
            act.wait_ge(chunk_used, PLAN["out1"] + KT)
            act.dma_start(pos_i, positions).then_inc(pos_landed, 16)
            def norm_leads(n, tiles=range(KT)):
                for k in tiles:
                    act.wait_ge(scaled, 8 * n + k + 1)
                    act.activation(as_r(lead_tile(k)[:, 0:LAT]), y_2[:, k, :], ACT.Copy).then_inc(norm_lead, 1)

            for n in range(KT):
                evacuate("ck", n, PLAN["ck"] + n + 1, CTX, key_c[:, n, :])
                if n >= 4:
                    for k in (2 * n - 8, 2 * n - 7):
                        act.wait_ge(scaled, 8 * N_FINAL + k + 1)
                        square(N_MIX_PRE, k, x_2[:, k, :], LAT)
            for n in range(KT):
                g = EVAC["cv"] + n
                act.wait_ge(chunk_used, PLAN["cv"] + n + 1)
                act.activation(val_c[:, :, n * P:(n + 1) * P], wide_ps[:, g % 2, 0:2 * P].rearrange("p (t n) -> p t n", t=2),
                               ACT.Copy).then_inc(evacuated, 1)
                if n == 0:
                    mean_root(N_MIX_PRE, LAT)
                if n >= 3:
                    norm_leads(N_MIX_PRE, (2 * n - 6, 2 * n - 5) if n < 7 else ())
                if n == KT - 3:
                    weight_leads("proj_2", 0, 2)
            act.wait_ge(rope_arg, 2)
            link(act.activation(cos_2, sin_2, ACT.Abs))
            link(act.activation(cos_2, cos_2, other(ACT.Sin), bias=half_pi, scale=-1.0))
            act.activation(sin_2, sin_2, other(ACT.Sin)).then_inc(rope_table, 1)
            for t in range(22):
                leads_after("proj_2", t)
                evacuate("proj_2", t, PLAN["proj_2"] + t + 1, LAT, tile_2[:, t, :], ACT.Copy if t < DG2 else other(ACT.Silu))
                q = t - DQ2 - 2
                if 0 <= q < 12:
                    act.wait_ge(cv_sum, q + 1)
                    act.activation(tile_2[:, DQ2 + q, :], conv_y[q % 2], other(ACT.Silu)).then_inc(cv_ready, 1)
                n = t - DQ2 - 3
                if 0 <= n < 8:
                    act.wait_ge(cv_ready, n + 1)
                    if n >= 2:
                        act.wait_ge(l2_ss, n - 1)
                    act.activation(l2_square[:, n % 2, :], tile_2[:, DQ2 + n, :], ACT.Square).then_inc(l2_sq, 1)
                n = t - DQ2 - 5
                if 0 <= n < 8:
                    act.wait_ge(l2_ss, n + 1)
                    if n >= 2:
                        act.wait_ge(l2_ready, n - 1)
                    inverse_root(l2_root[:, n % 2, :], pair_ps[:, 512 * (n % 2):512 * (n % 2) + LAT], 1.0, l2_rt)
            evacuate("ab_2", 0, PLAN["ab_2"] + 1, 64, small[:, 240:304])
            act.wait_ge(evacuated, EVAC["ab_2"] + 1)
            act.wait_ge(g_x, 1)
            logs_and_exps()
            act.activation(beta, ab[:, :, 8:16], ACT.Exp, scale=-1.0).then_inc(g_l, 1)
            link(act.activation(g_soft, g_tok, ACT.Abs))
            link(act.activation(g_soft, g_soft, ACT.Exp, scale=-1.0))
            act.activation(g_soft, g_soft, ACT.Ln, bias=1.0).then_inc(g_l, 1)
            act.activation(a_exp, prm["a_log"], ACT.Exp).then_inc(g_l, 1)
            act.wait_ge(g_c, 2)
            act.activation(g_exp, g_cum, ACT.Exp).then_inc(g_e, 1)
            act.wait_ge(v2_ps, 1)
            act.activation(v_tok[:, 0, 0:NLAT, :], duo_ps[:, 0:LAT].rearrange("p (c f) -> p c f", c=NLAT), ACT.Copy).then_inc(v2_ready, 1)

            def window_transposed(m):
                a, b, _, _ = window_keys(WIN[m][2])
                act.wait_ge(w_pt_ps, m + 1)
                if m >= 2:
                    act.wait_ge(w_o_ps, m - 1)
                act.activation(probs_t(m)[:, 0:b - a], twin(m)[:, 0:b - a], ACT.Copy).then_inc(w_pt, 1)

            for m in range(len(WIN) + 2):
                if m >= 2:
                    window_transposed(m - 2)
                if m >= len(WIN):
                    continue
                i, r, c = WIN[m]
                a, b, _, _ = window_keys(c)
                one = slice(m % 4, m % 4 + 1)
                act.wait_ge(w_max, m + 1)
                p = probs(m)[:, 0:b - a]
                act.activation(p, p, ACT.Exp, bias=neg_max2[:, one], accum_out=row_sum2[:, one]).then_inc(w_exp, 1)
                act.activation(sink_e[:, one], prm["sink"][:, i + 4 * r:i + 4 * r + 1], ACT.Exp,
                               bias=neg_max2[:, one]).then_inc(w_exp, 1)
            for s in range(NLAT):
                for d in range(2):
                    g = 2 * s + d
                    last = CH - 1 if d == 0 else 0
                    act.wait_ge(dn_diff, g + 1)
                    act.activation(dn(d, XM), dn(d, XM), ACT.Exp).then_inc(dn_exp, 1)
                    act.activation(g_end[:, d], g_end[:, d], ACT.Exp).then_inc(dn_exp, 1)
                    act.activation(dn(d, QG), dn_bank(d, 0), ACT.Exp).then_inc(dn_exp, 1)
                    act.activation(s_decay[:, d], dn_bank(d, 0)[:, :, last], ACT.Exp).then_inc(dn_exp, 1)
                for l in range(1, LEVELS):
                    for d in range(2):
                        at = 2 * (6 * s + l - 1) + d
                        act.wait_ge(dn_y_ps, at + 1)
                        act.activation(dn(d, Y), dn_bank(d, 3), ACT.Copy).then_inc(dn_y, 1)
                for d in range(2):
                    act.wait_ge(dn_w_ps, 2 * s + d + 1)
                    act.activation(dn(d, WT), dn_bank(d, 0), ACT.Copy, scale=-1.0).then_inc(dn_w, 1)
                for d in range(2):
                    act.wait_ge(dn_v_ps, 2 * s + d + 1)
                    act.activation(dn(d, VN), dn_bank(d, 1), ACT.Copy).then_inc(dn_v, 1)
            act.wait_ge(dn_s, 2 * NLAT)
            for n in range(5):
                if n < 4:
                    if n >= 2:
                        act.wait_ge(do_ss, n - 1)
                    act.activation(sq[:, n % 2, 0:LAT], o_dn[:, n, :], ACT.Square).then_inc(do_sq, 1)
                if n:
                    m = n - 1
                    act.wait_ge(do_ss, m + 1)
                    if m >= 2:
                        act.wait_ge(do_out, m - 1)
                    inverse_root(work[:, 2 + m % 2, 0:LAT], pair_ps[:, 512 * (m % 2):512 * (m % 2) + LAT], 1.0 / P, do_rt)
                if n in (1, 2):
                    weight_leads("out_2", n - 1)

            def closed(stage, n, chunks, following=None):
                for t in range(KT):
                    leads_after(stage, t, following)
                    evacuate(stage, t, PLAN[stage] + chunks * (t + 1), LAT, y_2[:, t, :])
                    square(n, t, y_2[:, t, :], LAT)
                mean_root(n, LAT)

            closed("out_2", N_MIX_POST, 1, "cq")
            norm_root(N_CROSS_PRE, lambda k: x_2[:, k, :], LAT, lambda k: act.wait_ge(x_ready, k + 1))
            norm_leads(N_CROSS_PRE)
            for t in range(KT):
                leads_after("cq", t, "co")
                evacuate("cq", t, PLAN["cq"] + t + 1, LAT, q_c[:, t, :])
            for m in range(len(CROSS) + 2):
                if m >= 2:
                    act.wait_ge(c_pt_ps, m - 1)
                    if m >= 4:
                        act.wait_ge(c_o_ps, m - 3)
                    act.activation(probs_t(m - 2)[:, 0:CTX], twin(m - 2)[:, 0:CTX], ACT.Copy).then_inc(c_pt, 1)
                if m < len(CROSS):
                    one = slice(m % 4, m % 4 + 1)
                    act.wait_ge(c_max, m + 1)
                    if m >= 3:
                        act.wait_ge(c_pt_ps, m - 2)
                    act.activation(probs(m)[:, 0:CTX], quad(m)[:, 0:CTX], ACT.Exp, bias=neg_max2[:, one],
                                   scale=256 ** -0.5, accum_out=row_sum2[:, one]).then_inc(c_exp, 1)
            closed("co", N_CROSS_POST, 1, "gu")
            norm_root(N_FFN_PRE, lambda k: x_2[:, k, :], LAT, lambda k: act.wait_ge(x_ready, KT + k + 1))
            norm_leads(N_FFN_PRE)
            for t in range(44):
                leads_after("gu", t, "down")
                if t % 2 == 0:
                    evacuate("gu", t, PLAN["gu"] + t + 1, LAT, tile_2[:, t // 2, :], other(ACT.Silu))
                else:
                    if t >= 5:
                        act.wait_ge(ffn_ready, t // 2 - 1)
                    evacuate("gu", t, PLAN["gu"] + t + 1, LAT, up_2[t // 2 % 2])
            closed("down", N_FFN_POST, 3)

        @block.vector
        def _(dve):
            dve_count = [0]

            def link(ins):
                dve_count[0] += 1
                ins.then_inc(dve_chain, 1)
                dve.wait_ge(dve_chain, dve_count[0])

            def modulation(ly):
                dve.wait_ge(mod_turned, ly + 1)
                bias = prm["b_mod"][:, ly * N_MOD:(ly + 1) * N_MOD].unsqueeze(2).broadcast_to([P, N_MOD, 2])
                dve.tensor_tensor(mod[:, ly], mod_ps[ly].rearrange("p (n s) -> p n s", s=2), bias,
                                  ALU.add).then_inc(mod_ready, 1)
                dve.wait_ge(mod_ready, 2 * ly + 1)
                gain = prm["norm_g"][:, ly * KT:(ly + 1) * KT].unsqueeze(2).broadcast_to([P, KT, 2])
                dve.scalar_tensor_tensor(out=mod_scale[:, ly], in0=mod[:, ly, KT:2 * KT], scalar=1.0, in1=gain, op0=ALU.add,
                                         op1=ALU.mult).then_inc(mod_ready, 1)

            x_count = [0]

            def split(src, lead):
                x_count[0] += 1
                dve.tensor_copy(as_r(lead), src).then_inc(x_lead, 1)
                dve.wait_ge(x_lead, x_count[0])
                dve.tensor_tensor(as_r(src), src, as_r(lead).bitcast(F32), ALU.subtract).then_inc(x_split, 1)

            def lower_bounds():
                dve.wait_ge(setup_landed, 32)
                dve.tensor_tensor(lb_e, prm["lb"][:, 4:8], prm["lb"][:, 0:4], ALU.subtract).then_inc(lb_ready, 1)
                dve.wait_ge(lb_ready, 2)
                link(dve.scalar_tensor_tensor(out=lb_log1m, in0=lb_e, scalar=0.0, in1=lb_log, op0=ALU.max, op1=ALU.add))
                link(dve.tensor_scalar(lb_log1m, lb_log1m, -1.0, None, ALU.mult))
                link(dve.scalar_tensor_tensor(out=lb_log, in0=lb_e, scalar=0.0, in1=lb_log, op0=ALU.min, op1=ALU.subtract))
                dve.tensor_scalar(lb_neg, lb_log, -1.0, None, ALU.mult).then_inc(lb_ready, 1)
                dve.wait_ge(lb_ready, 3)

            PARTS = 13

            def hgrn_part(ly, u, j, d, part):
                z = proj[:, (FF, FB)[d] + j, :]
                w = width(ly, HQ)
                q = proj[:, HQ + j, 0:w]
                one = 2 * d + j
                if part == 0:
                    dve.wait_ge(hg_soft, u + 1)
                    link(dve.scalar_tensor_tensor(out=lf_b, in0=z, scalar=0.0, in1=e_b, op0=ALU.min, op1=ALU.subtract))
                    dve.scalar_tensor_tensor(out=m_b, in0=z, scalar=0.0, in1=e_b, op0=ALU.max, op1=ALU.add).then_inc(hg_lf, 1)
                    if ly == 1:
                        dve.wait_ge(hg_lf, u + 1)
                        dve.tensor_scalar(lf_b, lf_b, lb_log1m[:, one:one + 1], None, ALU.add).then_inc(hg_lb, 1)
                if part == 1 and ly == 1:
                    dve.wait_ge(hg_abs, u - 3)
                    dve.scalar_tensor_tensor(out=lf_b, in0=lf_b, scalar=lb_log[:, one:one + 1], in1=e_b, op0=ALU.max,
                                             op1=ALU.add).then_inc(hg_lb, 1)
                    dve.wait_ge(hg_lb, 2 * (u - 4) + 2)
                if part in (1, 2):
                    if u:
                        dve.wait_ge(lev_diff, 2 * LEVELS * u)
                    for c in ((0, 1, 2), (3, 4, 5))[part - 1]:
                        run = slice(c * CH, (c + 1) * CH)
                        src, dst = lf_b[:, run], a_b[:, run]
                        if d:
                            src, dst = src[:, ::-1], dst[:, ::-1]
                        ins = dve.tensor_tensor_scan(dst, cst["ones"], src, 0.0, ALU.mult, ALU.add)
                        if c < NCH - 1:
                            link(ins)
                        else:
                            ins.then_inc(hg_a, 1)
                if part == 3:
                    dve.wait_ge(hg_a, u + 1)
                    a_c = a_b.rearrange("p (c t) -> p c t", t=CH)
                    last = a_c[:, :, CH - 1:CH] if d == 0 else a_c[:, :, 0:1]
                    dve.tensor_tensor(e_b.rearrange("p (c t) -> p c t", t=CH), last.broadcast_to([P, NCH, CH]), a_c,
                                      ALU.subtract).then_inc(hg_ed0, 1)
                if part == 4:
                    if u >= 2:
                        dve.wait_ge(hg_o_ps, u - 1)
                    dve.wait_ge(hg_ea, 2 * u + 2)
                    dve.tensor_tensor(q_decayed(u)[:, 0:w], q, m_b[:, 0:w], ALU.mult).then_inc(hg_qe, 1)
                    dve.wait_ge(hg_ed, u + 1)
                    dve.tensor_tensor(ke_b, z, e_b, ALU.mult).then_inc(hg_ke, 1)
                q_side, k_side = (1, 0) if d == 0 else (0, 1)
                if 5 <= part < 5 + LEVELS:
                    l = part - 5
                    b = 1 << l
                    o, kk, qq = halves(decay(u, l)[:, 0:w], b), halves(z[:, 0:w], b), halves(q, b)
                    dve.wait_ge(lev_exp, LEVELS * u + l + 1)
                    link(dve.tensor_tensor(o[:, :, q_side, :], o[:, :, q_side, :], qq[:, :, q_side, :], ALU.mult))
                    dve.tensor_tensor(o[:, :, k_side, :], o[:, :, k_side, :], kk[:, :, k_side, :], ALU.mult).then_inc(lev_ready, 1)
                if part == PARTS - 1:
                    dve.wait_ge(hg_u, u + 1)
                    seq = order(d)
                    st = state[:, u % 2]
                    link(dve.memset(st[:, seq[0], :], 0.0))
                    for n in range(1, NCH):
                        was, now = seq[n - 1], seq[n]
                        for r in range(2):
                            rows = slice(64 * r, 64 * r + 64)
                            ins = dve.scalar_tensor_tensor(
                                out=st[rows, now, :], in0=st[rows, was, :], scalar=f_last[rows, was:was + 1],
                                in1=wide_ps[rows, 1, was * CH + 64 * r:was * CH + 64 * r + 64], op0=ALU.mult, op1=ALU.add)
                            if n == NCH - 1 and r == 1:
                                ins.then_inc(hg_s, 1)
                            else:
                                link(ins)

            def hgrn_masks(ly, u, d, following):
                level = cst[f"level{d}"]
                n_tiles = 2 * len(chunk_list(ly))
                for n in range(n_tiles):
                    m = SC0[u] + n
                    dve.wait_ge(sc_ps, m + 1)
                    if m >= 4:
                        dve.wait_ge(sc_used, m - 3)
                    dve.tensor_tensor(masked[:, m % 4, :], duo_ps[:, 512 * (m % 2):512 * (m % 2) + 448], level,
                                      ALU.mult).then_inc(sc_ready, 1)
                    for part in range(PARTS):
                        if following and part * n_tiles // PARTS == n:
                            hgrn_part(ly, *following, part)

            def hgrn_out(ly, j):
                n = 2 * ly + j
                w = width(ly, HQ)
                dve.wait_ge(hg_diag, n + 1)
                dve.wait_ge(hg_o_ps, 4 * ly + 2 * j + 2)
                o, t = proj[:, FF + j, 0:w], proj[:, FB + j, 0:w]
                link(dve.tensor_tensor(t, wide_ps[:, 0, 0:w], proj[:, HI + j, 0:w], ALU.mult))
                dve.tensor_tensor(o, pair_ps[:, 0:w], t, ALU.add).then_inc(hg_o, 1)

            def hgrn_close(ly, j):
                n = 2 * ly + j
                w = width(ly, HQ)
                o, t = proj[:, FF + j, 0:w], proj[:, FB + j, 0:w]
                dve.wait_ge(hg_rt, n + 1)
                link(dve.tensor_tensor(o, o, t, ALU.mult))
                gz = proj[:, HZ + j, 0:w]
                dve.scalar_tensor_tensor(out=gz, in0=o, scalar=prm["hg_g"][:, n:n + 1], in1=gz, op0=ALU.mult,
                                         op1=ALU.mult).then_inc(hg_out, 1)

            def queries_keys(ly):
                for n, (t, w) in enumerate(qk_tiles(ly)):
                    x = proj[:, t, 0:w]
                    gain = prm["k_g" if t == AK else "q_g"][:, ly:ly + 1]
                    dve.wait_ge(qk_rt, 3 * ly + n + 1)
                    dve.scalar_tensor_tensor(out=x, in0=x, scalar=gain, in1=qk_root[:, 0:w], op0=ALU.mult,
                                             op1=ALU.mult).then_inc(qk_norm, 1)
                    dve.wait_ge(qk_rot, 3 * ly + n + 1)
                    link(dve.tensor_tensor(qk_turned[:, 0:LAT], duo_ps[:, 0:LAT], cst["sin"], ALU.mult))
                    link(dve.tensor_tensor(x[:, 0:LAT], x[:, 0:LAT], cst["cos"], ALU.mult))
                    dve.tensor_tensor(x[:, 0:LAT], x[:, 0:LAT], qk_turned[:, 0:LAT], ALU.add).then_inc(qk_ready, 1)

            def attention(ly):
                units = att_units(ly)
                for n in range(len(units) + 4):
                    if n < len(units):
                        m = ATT0[ly] + n
                        a, b = keys_of(units[n][2])
                        one = slice(m % 4, m % 4 + 1)
                        dve.wait_ge(at_s, m + 1)
                        link(dve.tensor_reduce(row_max[:, one], wide_ps[:, m % 2, a:b], AX.X, ALU.max))
                        dve.tensor_scalar(neg_max[:, one], row_max[:, one], -HD ** -0.5, None, ALU.mult).then_inc(at_max, 1)
                    if n >= 1 and n <= len(units):
                        m = ATT0[ly] + n - 1
                        a, b = keys_of(units[n - 1][2])
                        one = slice(m % 4, m % 4 + 1)
                        dve.wait_ge(at_exp, m + 1)
                        link(dve.reciprocal(row_inv[:, one], row_sum[:, one]))
                        dve.tensor_scalar(probs(m)[:, a:b], probs(m)[:, a:b], row_inv[:, one], None, ALU.mult).then_inc(at_p, 1)
                    if n >= 4:
                        m = ATT0[ly] + n - 4
                        i, r, c = units[n - 4]
                        rows = slice(64 * r, 64 * r + 64)
                        az = proj[rows, AZ + i, c * CH:(c + 1) * CH]
                        dve.wait_ge(at_o_ps, m + 1)
                        dve.tensor_tensor(az, duo_ps[rows, 512 * (m % 2):512 * (m % 2) + CH], az, ALU.mult).then_inc(at_out, 1)

            def fourier(ly):
                for s in (0, 1)[:2 - ly]:
                    a, b = ((0, LAT), (LAT, TOK))[s]
                    for j in range(2):
                        fz = proj[:, FZ + j, a:b]
                        dve.wait_ge(ft_y_ps, 4 * ly + 2 * s + j + 1)
                        dve.tensor_tensor(fz, ft_bank(s, j)[:, 0:b - a], fz, ALU.mult).then_inc(ft_out, 1)

            def memory_norm():
                dve.wait_ge(root_ready, N_MEM + 1)
                for k in range(KT):
                    dve.scalar_tensor_tensor(out=mem_x[:, k, :], in0=mem_x[:, k, :], scalar=prm["g_mem"][:, k:k + 1],
                                             in1=root[:, 0:CTX], op0=ALU.mult, op1=ALU.mult).then_inc(scaled, 1)

            def residual(ly):
                w = width(ly, HQ)
                for n in range(KT):
                    dve.wait_ge(evacuated, EVAC[f"out{ly}"] + n + 1)
                    dve.tensor_tensor(h[:, n, 0:w], h[:, n, 0:w], resid[:, n % 2, 0:w], ALU.add).then_inc(h_ready, 1)
                    if ly and n == 4:
                        memory_norm()

            lower_bounds()
            modulation(0)
            for ly in range(DEPTH):
                dve.wait_ge(root_ready, ly + 1)
                for k in range(KT + 2):
                    if k < KT:
                        dve.tensor_tensor(xn_t[:, k, :], h[:, k, :], root[:, :], ALU.mult).then_inc(scaled, 1)
                    if k >= 2:
                        dve.wait_ge(xn_ready, 16 * ly + 2 * k - 2)
                        split(xn_t[:, k - 2, :], lead_tile(k - 2))
                queries_keys(ly)
                if ly == 0:
                    modulation(1)
                units = hg_units(ly)
                for part in range(PARTS):
                    if part == PARTS - 1:
                        fourier(ly)
                    hgrn_part(ly, *units[0], part)
                for n, (u, j, d) in enumerate(units):
                    hgrn_masks(ly, u, d, units[n + 1] if n < 3 else None)
                    if d == 1:
                        hgrn_out(ly, j)
                    if n == 2:
                        hgrn_close(ly, 0)
                hgrn_close(ly, 1)
                attention(ly)
                dve.wait_ge(at_out, ATT0[ly] + len(att_units(ly)))
                w = width(ly, HQ)
                split(proj[:, AZ + 1, 0:w], mix_lead(3)[:, 0:w])
                residual(ly)
            dve.wait_ge(root_ready, N_FINAL + 1)
            for k in range(KT):
                dve.scalar_tensor_tensor(out=h[:, k, 0:LAT], in0=h[:, k, 0:LAT], scalar=prm["final_g"][:, k:k + 1],
                                         in1=root[:, 0:LAT], op0=ALU.mult, op1=ALU.mult).then_inc(scaled, 1)
            def half_turn():
                dve.memset(half_pi, float(np.pi / 2)).then_inc(rope_arg, 1)
                dve.wait_ge(const2_landed, 16)
                dve.wait_ge(pos_landed, 16)
                turn = 2 * np.pi
                c1 = 6.28125
                c2 = float(np.float32(round((turn - c1) * 2 ** 20) / 2 ** 20))
                link(dve.tensor_copy(sin_2, pos_i))
                link(dve.tensor_scalar(sin_2, sin_2, cst2["inv_freq"], None, ALU.mult))
                link(dve.tensor_scalar(cos_2, sin_2, 1.0 / turn, 12582912.0, ALU.mult, ALU.add))
                link(dve.tensor_scalar(cos_2, cos_2, 12582912.0, None, ALU.subtract))
                for part in (c1, c2, turn - c1 - c2):
                    link(dve.scalar_tensor_tensor(out=sin_2, in0=cos_2, scalar=-part, in1=sin_2, op0=ALU.mult, op1=ALU.add))
                dve.tensor_scalar(sin_2, sin_2, 3.1415925, -3.1415925, ALU.min, ALU.max).then_inc(rope_arg, 1)

            NORM_LEADS = {N_MIX_PRE: 0, N_CROSS_PRE: KT, N_FFN_PRE: 2 * KT}

            def scale_and_split(n, gain):
                for k in range(KT + 2):
                    if k < KT:
                        dve.scalar_tensor_tensor(out=y_2[:, k, :], in0=x_2[:, k, :], scalar=prm[gain][:, k:k + 1],
                                                 in1=root[:, 0:LAT], op0=ALU.mult, op1=ALU.mult).then_inc(scaled, 1)
                    if k >= 2:
                        y, lead = y_2[:, k - 2, :], as_r(lead_tile(k - 2)[:, 0:LAT]).bitcast(F32)
                        dve.wait_ge(norm_lead, NORM_LEADS[n] + k - 1)
                        dve.tensor_tensor(as_r(y), y, lead, ALU.subtract).then_inc(x_split, 1)

            dve.wait_ge(root_ready, N_MIX_PRE + 1)
            scale_and_split(N_MIX_PRE, "g_mix_pre")
            half_turn()
            taps = prm["conv2"].rearrange("p (n t) -> p n t", t=5)
            def query_key_length(n):
                x, r = tile_2[:, DQ2 + n, :], l2_root[:, n % 2, :]
                dve.wait_ge(l2_rt, n + 1)
                dve.scalar_tensor_tensor(out=x, in0=x, scalar=P ** -0.5 if n < 4 else 1.0, in1=r, op0=ALU.mult,
                                         op1=ALU.mult).then_inc(l2_ready, 1)

            def rope(n):
                x, t = tile_2[:, n, :], work[:, 2, 0:LAT]
                dve.wait_ge(rp_rot, n + 1)
                link(dve.tensor_tensor(t, pair_ps[:, 512 * (n % 2):512 * (n % 2) + LAT], sin_2, ALU.mult))
                link(dve.tensor_tensor(x, x, cos_2, ALU.mult))
                dve.tensor_tensor(x, x, t, ALU.add).then_inc(rp_ready, 1)

            dve.wait_ge(rope_table, 1)
            for q in range(12):
                if q < 5:
                    rope(q)
                x, y = tile_2[:, DQ2 + q, :], conv_y[q % 2]
                dve.wait_ge(evacuated, EVAC["proj_2"] + DQ2 + q + 1)
                if q >= 2:
                    dve.wait_ge(cv_ready, q - 1)
                link(dve.tensor_scalar(y, x, taps[:, q, 2:3], None, ALU.mult))
                for t in (0, 1, 3, 4):
                    off = t - 2
                    a, b = max(0, -off), LAT - max(0, off)
                    ins = dve.scalar_tensor_tensor(out=y[:, a:b], in0=x[:, a + off:b + off], scalar=taps[:, q, t:t + 1],
                                                   in1=y[:, a:b], op0=ALU.mult, op1=ALU.add)
                    if t < 4:
                        link(ins)
                    else:
                        ins.then_inc(cv_sum, 1)
                if q >= 5:
                    query_key_length(q - 5)
            query_key_length(7)
            dve.wait_ge(evacuated, EVAC["ab_2"] + 1)
            dve.tensor_tensor(g_tok, ab[:, :, 0:8], prm["dt_bias"].unsqueeze(1).broadcast_to([P, NLAT, 8]), ALU.add).then_inc(g_x, 1)
            dve.wait_ge(g_l, 3)
            link(dve.scalar_tensor_tensor(out=g_tok, in0=g_tok, scalar=0.0, in1=g_soft, op0=ALU.max, op1=ALU.add))
            dve.scalar_tensor_tensor(out=g_tok, in0=g_tok, scalar=-1.0, in1=a_exp.unsqueeze(1).broadcast_to([P, NLAT, 8]),
                                     op0=ALU.mult, op1=ALU.mult).then_inc(g_ready, 1)
            link(dve.tensor_scalar(beta, beta, 1.0, None, ALU.add))
            link(dve.reciprocal(beta, beta))
            dve.wait_ge(g_ps, 1)
            for d in range(2):
                dve.tensor_copy(g_cum[:, :, 4 * d:4 * d + 4], duo_ps[:, 16 * d:16 * d + 16].rearrange("p (c n) -> p c n", c=NLAT)).then_inc(g_c, 1)
            dve.wait_ge(g_e, 1)
            dve.tensor_tensor(beta_g, beta, g_exp, ALU.mult).then_inc(g_b, 1)
            for m in range(len(WIN) + 4):
                if m < len(WIN):
                    i, r, c = WIN[m]
                    a, b, ma, mb = window_keys(c)
                    one = slice(m % 4, m % 4 + 1)
                    dve.wait_ge(w_s, m + 1)
                    if m >= 3:
                        dve.wait_ge(w_pt_ps, m - 2)
                    head = i + 4 * r
                    link(dve.tensor_tensor_reduce(probs(m)[:, 0:b - a], quad(m)[:, 0:b - a], cst2["window"][:, ma:mb],
                                                  HD ** -0.5, prm["sink"][:, head:head + 1], ALU.add, ALU.max,
                                                  row_max2[:, one]))
                    dve.tensor_scalar(neg_max2[:, one], row_max2[:, one], -1.0, None, ALU.mult).then_inc(w_max, 1)
                if 1 <= m <= len(WIN):
                    n = m - 1
                    a, b, _, _ = window_keys(WIN[n][2])
                    one = slice(n % 4, n % 4 + 1)
                    dve.wait_ge(w_exp, 2 * n + 2)
                    link(dve.tensor_tensor(row_sum2[:, one], row_sum2[:, one], sink_e[:, one], ALU.add))
                    link(dve.reciprocal(row_inv2[:, one], row_sum2[:, one]))
                    dve.tensor_scalar(probs(n)[:, 0:b - a], probs(n)[:, 0:b - a], row_inv2[:, one], None, ALU.mult).then_inc(w_p, 1)
                if m >= 4:
                    n = m - 4
                    i, r, c = WIN[n]
                    rows = slice(64 * r, 64 * r + 64)
                    dve.wait_ge(w_o_ps, n + 1)
                    dve.tensor_copy(tile_2[rows, i, c * CH:(c + 1) * CH], duo_ps[rows, 512 * (n % 2):512 * (n % 2) + CH]).then_inc(w_out_s, 1)

            def heads(v):
                return v.unsqueeze(2).broadcast_to([P, 4, CH])

            ident_4 = cst["ident"].unsqueeze(1).broadcast_to([P, 4, CH])
            def differences(s, d):
                g, c = 2 * s + d, chunk_at(d, s)
                last = CH - 1 if d == 0 else 0
                mine = slice(4 * d, 4 * d + 4)
                dve.wait_ge(dn_a, g + 1)
                link(dve.tensor_tensor(dn(d, XM), dn_bank(d, 0), heads(g_cum[:, c, mine]), ALU.subtract))
                link(dve.tensor_tensor(g_end[:, d], dn_bank(d, 0)[:, :, last], g_cum[:, c, mine], ALU.subtract))
                dve.tensor_tensor(dn(d, XM), dn(d, XM), cst2[f"tri{d}"].unsqueeze(1).broadcast_to([P, 4, CH]), ALU.mult).then_inc(dn_diff, 1)

            def decayed_products(s, d):
                g = 2 * s + d
                dve.wait_ge(dn_exp, 4 * g + 4)
                link(dve.tensor_tensor(dn(d, XT), dn_bank(d, 1), dn(d, XM), ALU.mult))
                dve.tensor_tensor(dn(d, QK), dn_bank(d, 3), dn(d, XM), ALU.mult).then_inc(dn_x, 1)
                dve.tensor_tensor(dn(d, XT), dn(d, XT), dn_bank(d, 2), ALU.mult).then_inc(dn_x, 1)
                dve.wait_ge(dn_x, 2 * g + 2)
                mask = cst2[f"inv{d}"][:, 0:P].unsqueeze(1).broadcast_to([P, 4, CH])
                dve.tensor_tensor(dn(d, XM), dn(d, XT), mask, ALU.mult).then_inc(dn_xm, 1)

            def keys_values_by_token(s, d):
                g, c = 2 * s + d, chunk_at(d, s)
                mine = slice(4 * d, 4 * d + 4)
                dve.wait_ge(dn_tok_ps, g + 1)
                dve.tensor_tensor(dn(d, KBG), dn_bank(d, 0), heads(beta_g[:, c, mine]), ALU.mult).then_inc(dn_tok, 1)
                dve.tensor_tensor(dn(d, KG), dn_bank(d, 0), heads(g_end[:, d]), ALU.mult).then_inc(dn_tok, 1)
                dve.tensor_tensor(dn(d, VB), dn_bank(d, 1), heads(beta[:, c, mine]), ALU.mult).then_inc(dn_tok, 1)

            for s in range(NLAT):
                for d in range(2):
                    differences(s, d)
                for d in range(2):
                    decayed_products(s, d)
                for l in range(LEVELS):
                    for d in range(2):
                        at = 2 * (LEVELS * s + l) + d
                        dve.wait_ge(dn_z_ps, at + 1)
                        if l == 0:
                            link(dve.scalar_tensor_tensor(out=dn(d, T), in0=dn_bank(d, 2), scalar=-1.0, in1=ident_4, op0=ALU.mult, op1=ALU.add))
                            dve.scalar_tensor_tensor(out=dn(d, R), in0=dn(d, XM), scalar=-1.0, in1=ident_4, op0=ALU.mult, op1=ALU.add).then_inc(dn_t, 1)
                        else:
                            if l < LEVELS - 1:
                                link(dve.tensor_tensor(dn(d, T), dn(d, T), dn_bank(d, 2), ALU.subtract))
                            dve.tensor_tensor(dn(d, R), dn(d, R), dn_bank(d, 3), ALU.subtract).then_inc(dn_t, 1)
                    if l in (1, 2):
                        keys_values_by_token(s, l - 1)
                for d in range(2):
                    c = chunk_at(d, s)
                    o = o_dn[:, :, c * CH:(c + 1) * CH]
                    dve.wait_ge(dn_o_ps, 2 * s + d + 1)
                    if s < NLAT // 2:
                        link(dve.tensor_copy(o, dn_bank(d, 2)))
                        if s == 0:
                            dve.tensor_copy(s_dn[:, d], dn_bank(d, 3)).then_inc(dn_s, 1)
                    if s >= NLAT // 2:
                        ins = dve.tensor_tensor(o, o, dn_bank(d, 2), ALU.add)
                        if s == NLAT - 1:
                            ins.then_inc(dn_s, 1)
                        else:
                            link(ins)
                    if 0 < s < NLAT - 1:
                        link(dve.tensor_tensor(s_dn[:, d], s_dn[:, d], heads(s_decay[:, d]), ALU.mult))
                        dve.tensor_tensor(s_dn[:, d], s_dn[:, d], dn_bank(d, 3), ALU.add).then_inc(dn_s, 1)
            for n in range(4):
                o, r, gate = o_dn[:, n, :], work[:, 2 + n % 2, 0:LAT], tile_2[:, DG2 + n, :]
                dve.wait_ge(do_rt, n + 1)
                link(dve.tensor_tensor(o, o, r, ALU.mult))
                dve.scalar_tensor_tensor(out=gate, in0=o, scalar=prm["g_dn"], in1=gate, op0=ALU.mult, op1=ALU.mult).then_inc(do_out, 1)
                dve.wait_ge(do_out, n + 1)
                split(gate, mix2_lead(4 + n))

            def add_closed(n, gain, done):
                dve.wait_ge(root_ready, n + 1)
                for k in range(KT + 1):
                    if k < KT:
                        dve.scalar_tensor_tensor(out=y_2[:, k, :], in0=y_2[:, k, :], scalar=prm[gain][:, k:k + 1],
                                                 in1=root[:, 0:LAT], op0=ALU.mult, op1=ALU.mult).then_inc(scaled, 1)
                    if k:
                        dve.wait_ge(scaled, 8 * n + k)
                        dve.tensor_tensor(x_2[:, k - 1, :], x_2[:, k - 1, :], y_2[:, k - 1, :], ALU.add).then_inc(done, 1)

            add_closed(N_MIX_POST, "g_mix_post", x_ready)
            dve.wait_ge(root_ready, N_CROSS_PRE + 1)
            scale_and_split(N_CROSS_PRE, "g_cross_pre")
            for m in range(len(CROSS) + 4):
                if m < len(CROSS):
                    one = slice(m % 4, m % 4 + 1)
                    dve.wait_ge(c_s, m + 1)
                    link(dve.tensor_reduce(row_max2[:, one], quad(m)[:, 0:CTX], AX.X, ALU.max))
                    dve.tensor_scalar(neg_max2[:, one], row_max2[:, one], -256 ** -0.5, None, ALU.mult).then_inc(c_max, 1)
                if 1 <= m <= len(CROSS):
                    n = m - 1
                    one = slice(n % 4, n % 4 + 1)
                    dve.wait_ge(c_exp, n + 1)
                    link(dve.reciprocal(row_inv2[:, one], row_sum2[:, one]))
                    dve.tensor_scalar(probs(n)[:, 0:CTX], probs(n)[:, 0:CTX], row_inv2[:, one], None, ALU.mult).then_inc(c_p, 1)
                if m >= 4:
                    n = m - 4
                    hd, c = CROSS[n]
                    dve.wait_ge(c_o_ps, n + 1)
                    dve.tensor_copy(o_c[:, 2 * hd:2 * hd + 2, c * CH:(c + 1) * CH],
                                    duo_ps[:, 512 * (n % 2):512 * (n % 2) + 256].rearrange("p (e t) -> p e t", e=2)).then_inc(c_out, 1)
            add_closed(N_CROSS_POST, "g_cross_post", x_ready)
            dve.wait_ge(root_ready, N_FFN_PRE + 1)
            scale_and_split(N_FFN_PRE, "g_ffn_pre")
            for t in range(22):
                dve.wait_ge(evacuated, EVAC["gu"] + 2 * t + 2)
                dve.tensor_tensor(tile_2[:, t, :], tile_2[:, t, :], up_2[t % 2], ALU.mult).then_inc(ffn_ready, 1)
                dve.wait_ge(ffn_ready, t + 1)
                split(tile_2[:, t, :], hidden_lead(t))
            add_closed(N_FFN_POST, "g_ffn_post", final_ready)

        @block.tensor
        def _(pe):
            def use_chunk(c):
                pe.wait_ge(landed[c % RING], 16 * (c // RING + 1))
                return ring[:, c % RING, :]

            def project(stage, tile, chunk, k_tiles, rhs, w, rhs_ready=None):
                g = EVAC[stage] + tile
                if g >= 2:
                    pe.wait_ge(evacuated, g - 1)
                for k in range(k_tiles):
                    if k % KT == 0:
                        wt = use_chunk(chunk + k // KT)
                    if rhs_ready:
                        rhs_ready(k)
                    for a, b in pieces(w):
                        last = pe.matmul(wide_ps[:, g % 2, a:b], wt[:, k % KT * P:(k % KT + 1) * P], rhs(k)[:, a:b],
                                         start=k == 0, stop=k == k_tiles - 1)
                    if k % KT == KT - 1 or k == k_tiles - 1:
                        last.then_inc(chunk_used, 1)

            def project_split(stage, tile, k_order, lead, rest, w, input_ready=None):
                g = EVAC[stage] + tile
                if g >= 2:
                    pe.wait_ge(evacuated, g - 1)
                for n, k in enumerate(k_order):
                    if n % KT == 0:
                        at = tile * -(-len(k_order) // KT) + n // KT
                        m = SPLIT_AT[stage] + at
                        pe.wait_ge(w_split, m + 1)
                        w_rest = as_r(ring[:, where(stage, at) % RING, :])
                        w_first = as_r(w_lead[:, m % 2, :])
                    if input_ready:
                        input_ready(n)
                    cols = slice(k % KT * P, (k % KT + 1) * P)
                    for a, b in pieces(w):
                        for p, (wt, x) in enumerate(((w_first, lead(k)), (w_first, rest(k)), (w_rest, lead(k)))):
                            last = pe.matmul(wide_ps[:, g % 2, a:b], wt[:, cols], as_r(x[:, a:b]),
                                             start=n == 0 and p == 0, stop=n == len(k_order) - 1 and p == 2)
                    if n % KT == KT - 1 or n == len(k_order) - 1:
                        last.then_inc(chunk_used, 1)

            def after(before):
                return lambda n: pe.wait_ge(x_split, before + n + 1)

            def mix_ready(ly):
                return lambda n: (pe.wait_ge(mix_split, 7 * ly + n + 1) if n < KT - 1 else
                                  pe.wait_ge(x_split, X_SPLITS[f"out{ly}"] + 1))

            def modulation_tile(ly, n):
                if n:
                    modulation_turn(ly, n - 1)
                wt = use_chunk(where(f"mod{ly}", n))
                for k in range(KT):
                    last = pe.matmul(mod_row_ps(ly, n), c_act[:, 2 * k:2 * k + 2], wt[:, k * P:(k + 1) * P],
                                     start=k == 0, stop=k == KT - 1, skip_group_check=True)
                last.then_inc(chunk_used, 1)
                pe.matmul(mod_row_ps(ly, n)[:, 0:64], zero[0:1, 0:2], cst["cos"][0:1, 0:64], start=False, stop=True,
                          skip_group_check=True).then_inc(mod_row_sum, 1)

            def modulation_turn(ly, n):
                pe.wait_ge(mod_row, N_MOD * ly + n + 1)
                pe.matmul(mod_ps[ly][:, 2 * n:2 * n + 2], mod_row_sb(ly, n), cst["ident"][0:2, 0:2], start=True, stop=True,
                          skip_group_check=True).then_inc(mod_row_used, 1)
                if n == N_MOD - 1:
                    pe.matmul(mod_ps[ly][:, 2 * n:2 * n + 2], zero[0:1, :], cst["cos"][0:1, 0:2], start=False, stop=True,
                              skip_group_check=True).then_inc(mod_turned, 1)

            def norm_step(n, k, w):
                pe.wait_ge(sq_ready, 8 * n + k + 1)
                for a, b in pieces(w):
                    last = pe.matmul(pair_ps[:, a:b], cst["ones"], squares(n)[:, k % 2, a:b], start=k == 0, stop=k == KT - 1)
                last.then_inc(sq_used, 1)

            def norm_sum(n, w):
                for k in range(KT):
                    norm_step(n, k, w)

            def by_token(src, ps, done):
                for c in range(NCH):
                    last = pe.transpose(ps[:, c * CH:(c + 1) * CH], src[:, c * CH:(c + 1) * CH], cst["ident"])
                last.then_inc(done, 1)

            def keys_by_token(u):
                pe.wait_ge(hg_ke, u + 1)
                by_token(ke_b, wide_ps[:, 0], hg_kt_ps)

            def updates(u, j):
                pe.wait_ge(hg_kt, u + 1)
                if u:
                    pe.wait_ge(hg_s, u)
                if u % 4 == 3:
                    pe.wait_ge(hg_rt, u // 2)
                for c in range(NCH):
                    last = pe.matmul(wide_ps[:, 1, c * CH:(c + 1) * CH], k_tok[:, c, :], v_tok[:, j, c, :], start=True, stop=True)
                last.then_inc(hg_u, 1)

            def hgrn_unit(ly, u, j, d, following):
                if d == 0:
                    if j:
                        pe.wait_ge(hg_o, 2 * ly + j)
                    for a, b in pieces(width(ly, HQ)):
                        pe.matmul(pair_ps[:, a:b], zero[0:1, :], cst["cos"][0:1, 0:b - a], start=True, stop=False,
                                  skip_group_check=True)
                pe.wait_ge(lev_ready, LEVELS * (u + 1))
                pe.wait_ge(hg_qe, u + 1)
                pe.wait_ge(hg_s, u + 1)
                side = 1 if d == 0 else 0
                tiles = [(c, r) for c in chunk_list(ly) for r in range(2)]

                def scores(n):
                    c, r = tiles[n]
                    m = SC0[u] + n
                    rows = slice(64 * r, 64 * r + 64)
                    if m >= 2:
                        pe.wait_ge(sc_ready, m - 1)
                    for l in range(LEVELS):
                        w = decay(u, l)[rows, c * CH:(c + 1) * CH]
                        last = pe.matmul(duo_ps[:, 512 * (m % 2) + 64 * l:512 * (m % 2) + 64 * l + 64], w,
                                         halves(w, 1 << l)[:, :, side, :], start=True, stop=True, skip_group_check=True)
                    last.then_inc(sc_ps, 1)

                def values(n):
                    c, r = tiles[n]
                    m = SC0[u] + n
                    rows = slice(64 * r, 64 * r + 64)
                    pe.wait_ge(sc_ready, m + 1)
                    o = pair_ps[rows, c * CH:(c + 1) * CH]
                    if c != order(d)[0]:
                        pe.matmul(o, state[rows, u % 2, c, :], q_decayed(u)[rows, c * CH:(c + 1) * CH], start=False,
                                  stop=False, skip_group_check=True)
                    for l in range(LEVELS):
                        last = pe.matmul(halves(o, 1 << l)[:, :, side, :], v_tok[:, j, c, rows],
                                         masked[:, m % 4, 64 * l:64 * l + 64], start=False, stop=l == LEVELS - 1,
                                         skip_group_check=True)
                    last.then_inc(sc_used, 1)
                    if n == len(tiles) - 1:
                        pe.matmul(pair_ps[:, c * CH:c * CH + 64], zero[0:1, :], cst["cos"][0:1, 0:64], start=False, stop=True,
                                  skip_group_check=True).then_inc(hg_o_ps, 1)

                for n in range(len(tiles) + 1):
                    if n < len(tiles):
                        scores(n)
                    if n:
                        values(n - 1)
                    if j == 1 and d == 0 and n == 2:
                        head_mean(ly, 0)
                    if following and n == len(tiles) * 7 // 12:
                        keys_by_token(following[0])
                    if following and n == len(tiles) * 10 // 12:
                        updates(following[0], following[1])

            def diagonal(ly, j):
                w = width(ly, HQ)
                n = 2 * ly + j
                pe.wait_ge(hg_qk, n + 1)
                if j == 0:
                    pe.wait_ge(hg_kt, 4 * ly + 3)
                for a, b in pieces(w):
                    last = pe.matmul(wide_ps[:, 0, a:b], cst["ones_head"], proj[:, FF + j, a:b], start=True, stop=True)
                last.then_inc(hg_diag, 1)

            def head_mean(ly, j):
                w = width(ly, HQ)
                n = 2 * ly + j
                pe.wait_ge(hg_sq, n + 1)
                pe.wait_ge(hg_s, 4 * ly + 3 + j)
                for a, b in pieces(w):
                    last = pe.matmul(wide_ps[:, 1, a:b], cst["ones_head"], proj[:, HI + j, a:b], start=True, stop=True)
                last.then_inc(hg_ms, 1)

            def query_key_sums(ly, tile):
                n, step = divmod(tile - AK - 2, QK_STEP)
                if tile < AK + 2 or n > 2:
                    return
                t, w = qk_tiles(ly)[n]
                m = 3 * ly + n
                if step == 0:
                    pe.wait_ge(qk_sq, m + 1)
                    for a, b in pieces(w):
                        last = pe.matmul(pair_ps[:, a:b], cst["ones_head"], qk_square[:, a:b], start=True, stop=True)
                    last.then_inc(qk_ms, 1)
                if step == 2:
                    pe.wait_ge(qk_norm, m + 1)
                    if m:
                        pe.wait_ge(qk_ready, m)
                    pe.matmul(duo_ps[:, 0:LAT], cst["rot_pair"], proj[:, t, 0:LAT], start=True, stop=True).then_inc(qk_rot, 1)

            def attention(ly):
                pe.wait_ge(hg_o, 2 * ly + 2)
                by_token(proj[:, AV, :], pair_ps, vt_ps)
                pe.wait_ge(vt_ready, 3 * ly + 3)
                pe.wait_ge(qk_ready, 3 * ly + 3)
                units = att_units(ly)
                for n in range(len(units) + 3):
                    if n < len(units):
                        i, r, c = units[n]
                        m = ATT0[ly] + n
                        rows = slice(64 * r, 64 * r + 64)
                        if n >= 2:
                            pe.wait_ge(at_exp, m - 1)
                        for a, b in ([(0, LAT)] if c < NLAT else []) + [(LAT, TOK)]:
                            last = pe.matmul(wide_ps[:, m % 2, a:b], proj[rows, AQ + i, c * CH:(c + 1) * CH],
                                             proj[rows, AK, a:b], start=True, stop=True)
                        last.then_inc(at_s, 1)
                    if 2 <= n <= len(units) + 1:
                        m = ATT0[ly] + n - 2
                        a, b = keys_of(units[n - 2][2])
                        pe.wait_ge(at_p, m + 1)
                        if n >= 3:
                            pe.wait_ge(at_pt, m)
                        for t in range(a // P, b // P):
                            last = pe.transpose(pair_ps[:, t * P:(t + 1) * P], probs(m)[:, t * P:(t + 1) * P], cst["ident"])
                        last.then_inc(at_pt_ps, 1)
                    if n >= 3:
                        m = ATT0[ly] + n - 3
                        i, r, c = units[n - 3]
                        a, b = keys_of(c)
                        pe.wait_ge(at_pt, m + 1)
                        if n >= 5:
                            pe.wait_ge(at_out, m - 1)
                        for t in range(a // P, b // P):
                            last = pe.matmul(duo_ps[64 * r:64 * r + 64, 512 * (m % 2):512 * (m % 2) + CH],
                                             v_tok[:, 0, t, 64 * r:64 * r + 64], probs_t(m)[:, t * P:(t + 1) * P],
                                             start=t == a // P, stop=t == b // P - 1)
                        last.then_inc(at_o_ps, 1)

            def fourier(ly):
                chunk = PLAN[f"dft{ly}"]
                m = FT0[ly]
                for s in (0, 1)[:2 - ly]:
                    lo, n_t = ((0, NLAT), (LAT, 2))[s]
                    size = n_t * P
                    chunks = NLAT if s == 0 else 1
                    for j in range(2):
                        for tt in range(n_t):
                            if m - FT0[ly] >= 2:
                                pe.wait_ge(ft_a, m - 1)
                            pe.matmul(pair_ps[:, 512 * (m % 2):512 * (m % 2) + 256],
                                      proj[:, FU + j, lo + tt * P:lo + (tt + 1) * P], cst["dft_ch"], start=True,
                                      stop=True).then_inc(ft_a_ps, 1)
                            m += 1
                        pe.wait_ge(ft_a, m)
                        for tt in range(n_t):
                            at = chunk + (tt if s == 0 else 0)
                            wt = use_chunk(at)
                            base = 0 if s == 0 else tt * 2 * size
                            for part in range(2):
                                last = pe.matmul(ft_bank(s, j)[:, 0:size], ft_buf[:, tt, part * P:(part + 1) * P],
                                                 wt[:, base + part * size:base + (part + 1) * size],
                                                 start=tt == 0 and part == 0, stop=tt == n_t - 1 and part == 1,
                                                 skip_group_check=True)
                            if j and (s == 0 or tt == n_t - 1):
                                last.then_inc(chunk_used, 1)
                        pe.matmul(ft_bank(s, j)[:, 0:64], zero[0:1, :], cst["cos"][0:1, 0:64], start=False, stop=True,
                                  skip_group_check=True).then_inc(ft_y_ps, 1)
                    chunk += chunks

            pe.wait_ge(setup_landed, 32)
            pe.wait_ge(ready, 2)
            pe.wait_ge(c_ready, 1)
            for n in range(N_MOD):
                modulation_tile(0, n)
                if 5 <= n < 5 + KT:
                    norm_step(0, n - 5, TOK)
            modulation_turn(0, N_MOD - 1)
            for ly in range(DEPTH):
                for t in range(NPROJ):
                    if ly == 0 and t < N_MOD:
                        modulation_tile(1, t)
                    if ly == 0 and t == N_MOD:
                        modulation_turn(1, N_MOD - 1)
                    query_key_sums(ly, t)
                    project_split(f"proj{ly}", t, range(KT), lead_tile, lambda k: xn_t[:, k, :], width(ly, t),
                                  after(X_SPLITS[f"proj{ly}"]) if t == 0 else None)
                for j in range(2):
                    pe.wait_ge(evacuated, EVAC[f"proj{ly}"] + NPROJ)
                    pe.wait_ge(qk_ready, 3 * ly + 3)
                    pe.wait_ge(mod_ready, 4)
                    if j:
                        pe.wait_ge(vt_ready, 3 * ly + 1)
                    by_token(proj[:, HI + j, :], duo_ps, vt_ps)
                pe.wait_ge(vt_ready, 3 * ly + 2)
                fourier(ly)
                units = hg_units(ly)
                pe.wait_ge(ft_out, (4, 6)[ly])
                keys_by_token(units[0][0])
                updates(units[0][0], 0)
                for n, (u, j, d) in enumerate(units):
                    hgrn_unit(ly, u, j, d, units[n + 1] if n < 3 else None)
                    if d == 1:
                        diagonal(ly, j)
                head_mean(ly, 1)
                attention(ly)
                for n in range(KT):
                    project_split(f"out{ly}", n, MIX_ORDER, mix_lead, lambda k: proj[:, MIX[k], :], width(ly, HQ),
                                  mix_ready(ly) if n == 0 else None)
                    if ly == 0 and n >= 2:
                        norm_step(N_LAYER1, n - 2, TOK)
                    if ly and n < 4:
                        norm_step(N_MEM, 2 * n, CTX)
                        norm_step(N_MEM, 2 * n + 1, CTX)
                    if ly and n >= 5:
                        if n == 5:
                            pe.wait_ge(root_ready, N_MEM + 1)
                        norm_step(N_FINAL, 2 * n - 10, LAT)
                        if n < KT - 1:
                            norm_step(N_FINAL, 2 * n - 9, LAT)
                for k in (KT - 2, KT - 1) if ly == 0 else (KT - 3, KT - 2, KT - 1):
                    norm_step((N_LAYER1, N_FINAL)[ly], k, width(ly, HQ))
            def scaled_by(n):
                return lambda k: pe.wait_ge(scaled, 8 * n + k + 1)

            def mix2_ready(k):
                if k < 4:
                    pe.wait_ge(mix_split, 14 + k + 1)
                else:
                    pe.wait_ge(x_split, X_SPLITS["out_2"] + k - 3)

            def ck(n):
                project("ck", n, PLAN["ck"] + n, KT, lambda k: mem_x[:, k, :], CTX, scaled_by(N_MEM) if n == 0 else None)

            pe.wait_ge(const2_landed, 16)
            for n in range(KT):
                ck(n)
                if n >= 4:
                    if n == 4:
                        pe.wait_ge(root_ready, N_FINAL + 1)
                    norm_step(N_MIX_PRE, 2 * n - 8, LAT)
                    norm_step(N_MIX_PRE, 2 * n - 7, LAT)
            for n in range(KT):
                g = EVAC["cv"] + n
                pe.wait_ge(evacuated, g - 1)
                wt = use_chunk(PLAN["cv"] + n)
                for t in range(2):
                    for k in range(KT):
                        last = pe.matmul(wide_ps[:, g % 2, t * P:(t + 1) * P], mem_x[:, k, t * P:(t + 1) * P],
                                         wt[:, k * P:(k + 1) * P], start=k == 0, stop=k == KT - 1)
                last.then_inc(chunk_used, 1)
            for t in range(22):
                n = t - 6
                if 0 <= n < 5:
                    pe.wait_ge(evacuated, EVAC["proj_2"] + n + 1)
                    if n >= 2:
                        pe.wait_ge(rp_ready, n - 1)
                    pe.matmul(pair_ps[:, 512 * (n % 2):512 * (n % 2) + LAT], cst2["rot_half"], tile_2[:, n, :], start=True,
                              stop=True).then_inc(rp_rot, 1)
                n = t - 11
                if 0 <= n < 8:
                    pe.wait_ge(l2_sq, n + 1)
                    if n >= 2:
                        pe.wait_ge(l2_rt, n - 1)
                    else:
                        pe.wait_ge(rp_ready, 5 - n)
                    pe.matmul(pair_ps[:, 512 * (n % 2):512 * (n % 2) + LAT], cst["ones"], l2_square[:, n % 2, :], start=True,
                              stop=True).then_inc(l2_ss, 1)
                project_split("proj_2", t, range(KT), lead_tile, lambda k: y_2[:, k, :], LAT,
                              after(X_SPLITS["proj_2"]) if t == 0 else None)
            wt = use_chunk(PLAN["ab_2"])
            g = EVAC["ab_2"]
            pe.wait_ge(evacuated, g - 1)
            for c in range(NLAT):
                for k in range(KT):
                    for p, x in enumerate((as_r(lead_tile(k)).bitcast(F32), as_r(y_2[:, k, :]).bitcast(F32))):
                        last = pe.matmul(wide_ps[:, g % 2, 16 * c:16 * c + 16], x[:, c * CH:(c + 1) * CH],
                                         wt[:, k * P:k * P + 16], start=k == 0 and p == 0, stop=k == KT - 1 and p == 1)
            last.then_inc(chunk_used, 1)
            pe.wait_ge(g_ready, 1)
            pe.wait_ge(const2_landed, 16)
            for d in range(2):
                last = pe.matmul(duo_ps[:, 16 * d:16 * d + 16], cst2[f"tri{d}"], g_tok[:, :, 4 * d:4 * d + 4], start=True, stop=True)
            last.then_inc(g_ps, 1)
            pe.wait_ge(l2_rt, 8)
            pe.wait_ge(g_c, 2)
            for c in range(NLAT):
                last = pe.transpose(duo_ps[:, c * CH:(c + 1) * CH], tile_2[:, AV2, c * CH:(c + 1) * CH], cst["ident"])
            last.then_inc(v2_ps, 1)
            pe.wait_ge(v2_ready, 1)
            pe.wait_ge(rp_ready, 5)
            for m in range(len(WIN) + 3):
                if m < len(WIN):
                    i, r, c = WIN[m]
                    rows = slice(64 * r, 64 * r + 64)
                    a, b, _, _ = window_keys(c)
                    if m >= 4:
                        pe.wait_ge(w_max, m - 3)
                    pe.matmul(quad(m)[:, 0:b - a], tile_2[rows, i, c * CH:(c + 1) * CH], tile_2[rows, AK2, a:b],
                              start=True, stop=True).then_inc(w_s, 1)
                if 2 <= m <= len(WIN) + 1:
                    n = m - 2
                    a, b, _, _ = window_keys(WIN[n][2])
                    pe.wait_ge(w_p, n + 1)
                    if n >= 2:
                        pe.wait_ge(w_pt, n - 1)
                    for t in range((b - a) // P):
                        last = pe.transpose(twin(n)[:, t * P:(t + 1) * P], probs(n)[:, t * P:(t + 1) * P], cst["ident"])
                    last.then_inc(w_pt_ps, 1)
                if m >= 3:
                    n = m - 3
                    i, r, c = WIN[n]
                    a, b, _, _ = window_keys(c)
                    pe.wait_ge(w_pt, n + 1)
                    if n >= 2:
                        pe.wait_ge(w_out_s, n - 1)
                    for t in range((b - a) // P):
                        last = pe.matmul(duo_ps[64 * r:64 * r + 64, 512 * (n % 2):512 * (n % 2) + CH],
                                         v_tok[:, 0, a // P + t, 64 * r:64 * r + 64], probs_t(n)[:, t * P:(t + 1) * P],
                                         start=t == 0, stop=t == (b - a) // P - 1)
                    last.then_inc(w_o_ps, 1)

            def four(out_ap, lhs, rhs, **flags):
                for hd in range(4):
                    last = pe.matmul(out_ap[:, hd, :], lhs(hd), rhs(hd), start=True, stop=True, **flags)
                return last

            pe.wait_ge(w_out_s, len(WIN))
            pe.wait_ge(l2_ready, 8)
            pe.wait_ge(g_b, 1)
            for s in range(NLAT):
                for d in range(2):
                    g, c = 2 * s + d, chunk_at(d, s)
                    run = slice(c * CH, (c + 1) * CH)
                    if s:
                        pe.wait_ge(dn_s, g - 1)
                    wide = lambda v: v.broadcast_to([P, P])
                    four(dn_bank(d, 0), lambda hd: wide(g_tok[:, c, 4 * d + hd:4 * d + hd + 1]), lambda hd: cst2[f"tri{d}"])
                    four(dn_bank(d, 1), lambda hd: tile_2[:, DK2 + hd, run], lambda hd: tile_2[:, DK2 + hd, run])
                    four(dn_bank(d, 2), lambda hd: wide(beta[:, c, 4 * d + hd:4 * d + hd + 1]), lambda hd: cst["ident"])
                    four(dn_bank(d, 3), lambda hd: tile_2[:, DK2 + hd, run], lambda hd: tile_2[:, DQ2 + hd, run]).then_inc(dn_a, 1)
                for d in range(2):
                    g, c = 2 * s + d, chunk_at(d, s)
                    pe.wait_ge(dn_x, 2 * g + 2)
                    for hd in range(4):
                        pe.transpose(dn_bank(d, 0)[:, hd, :], tile_2[:, DK2 + hd, c * CH:(c + 1) * CH], cst["ident"])
                    for hd in range(4):
                        last = pe.transpose(dn_bank(d, 1)[:, hd, :], tile_2[:, DV2 + hd, c * CH:(c + 1) * CH], cst["ident"])
                    last.then_inc(dn_tok_ps, 1)
                    pe.wait_ge(dn_xm, 2 * (LEVELS * s) + d + 1)
                    four(dn_bank(d, 2), lambda hd: dn(d, XM)[:, hd, :], lambda hd: cst["ident"]).then_inc(dn_z_ps, 1)
                for l in range(1, LEVELS):
                    for d in range(2):
                        pe.wait_ge(dn_xm, 2 * (LEVELS * s + l) + d + 1)
                        pe.wait_ge(dn_t, 2 * (LEVELS * s + l - 1) + d + 1)
                        four(dn_bank(d, 3), lambda hd: dn(d, XM)[:, hd, :], lambda hd: dn(d, T)[:, hd, :]).then_inc(dn_y_ps, 1)
                    for d in range(2):
                        pe.wait_ge(dn_y, 2 * (6 * s + l - 1) + d + 1)
                        if l < LEVELS - 1:
                            four(dn_bank(d, 2), lambda hd: dn(d, R)[:, hd, :], lambda hd: dn(d, Y)[:, hd, :])
                        four(dn_bank(d, 3), lambda hd: dn(d, Y)[:, hd, :], lambda hd: dn(d, R)[:, hd, :]).then_inc(dn_z_ps, 1)
                for d in range(2):
                    pe.wait_ge(dn_t, 2 * (LEVELS * s + LEVELS - 1) + d + 1)
                    pe.wait_ge(dn_tok, 3 * (2 * s + d) + 3)
                    four(dn_bank(d, 0), lambda hd: dn(d, KBG)[:, hd, :], lambda hd: dn(d, R)[:, hd, :]).then_inc(dn_w_ps, 1)
                for d in range(2):
                    pe.wait_ge(dn_w, 2 * s + d + 1)
                    for hd in range(4):
                        last = pe.matmul(dn_bank(d, 1)[:, hd, :], dn(d, R)[:, hd, :], dn(d, VB)[:, hd, :], start=True, stop=s == 0)
                        if s:
                            last = pe.matmul(dn_bank(d, 1)[:, hd, :], dn(d, WT)[:, hd, :], s_dn[:, d, hd, :], start=False, stop=True)
                    last.then_inc(dn_v_ps, 1)
                for d in range(2):
                    pe.wait_ge(dn_v, 2 * s + d + 1)
                    pe.wait_ge(dn_qg, 2 * (2 * s + d) + 2)
                    four(dn_bank(d, 3), lambda hd: dn(d, KG)[:, hd, :], lambda hd: dn(d, VN)[:, hd, :])
                    for hd in range(4):
                        if s:
                            pe.matmul(dn_bank(d, 2)[:, hd, :], s_dn[:, d, hd, :], dn(d, QG)[:, hd, :], start=True, stop=False)
                        last = pe.matmul(dn_bank(d, 2)[:, hd, :], dn(d, VN)[:, hd, :], dn(d, QK)[:, hd, :], start=s == 0, stop=True)
                    last.then_inc(dn_o_ps, 1)
            for n in range(4):
                pe.wait_ge(do_sq, n + 1)
                if n >= 2:
                    pe.wait_ge(do_rt, n - 1)
                pe.matmul(pair_ps[:, 512 * (n % 2):512 * (n % 2) + LAT], cst["ones"], sq[:, n % 2, 0:LAT], start=True,
                          stop=True).then_inc(do_ss, 1)
            for n in range(KT):
                project_split("out_2", n, range(KT), mix2_lead, lambda k: tile_2[:, MIX2[k], :], LAT, mix2_ready if n == 0 else None)
                if n:
                    norm_step(N_MIX_POST, n - 1, LAT)
            norm_step(N_MIX_POST, KT - 1, LAT)
            norm_sum(N_CROSS_PRE, LAT)
            for n in range(KT):
                project_split("cq", n, range(KT), lead_tile, lambda k: y_2[:, k, :], LAT, after(X_SPLITS["cq"]) if n == 0 else None)
            pe.wait_ge(evacuated, EVAC["cq"] + KT)
            for m in range(len(CROSS) + 3):
                if m < len(CROSS):
                    hd, c = CROSS[m]
                    if m >= 4:
                        pe.wait_ge(c_exp, m - 3)
                    for e in range(2):
                        last = pe.matmul(quad(m)[:, 0:CTX], q_c[:, 2 * hd + e, c * CH:(c + 1) * CH], key_c[:, 2 * hd + e, :],
                                         start=e == 0, stop=e == 1)
                    last.then_inc(c_s, 1)
                if 2 <= m <= len(CROSS) + 1:
                    n = m - 2
                    pe.wait_ge(c_p, n + 1)
                    if n >= 2:
                        pe.wait_ge(c_pt, n - 1)
                    for t in range(2):
                        last = pe.transpose(twin(n)[:, t * P:(t + 1) * P], probs(n)[:, t * P:(t + 1) * P], cst["ident"])
                    last.then_inc(c_pt_ps, 1)
                if m >= 3:
                    n = m - 3
                    hd, c = CROSS[n]
                    pe.wait_ge(c_pt, n + 1)
                    if n >= 2:
                        pe.wait_ge(c_out, n - 1)
                    for e in range(2):
                        for t in range(2):
                            last = pe.matmul(duo_ps[:, 512 * (n % 2) + e * P:512 * (n % 2) + (e + 1) * P],
                                             val_c[:, t, (2 * hd + e) * P:(2 * hd + e + 1) * P], probs_t(n)[:, t * P:(t + 1) * P],
                                             start=t == 0, stop=t == 1)
                    last.then_inc(c_o_ps, 1)
            for n in range(KT):
                project_split("co", n, range(KT), lead_tile, lambda k: o_c[:, k, :], LAT,
                              (lambda k: pe.wait_ge(mix_split, 18 + k + 1)) if n == 0 else None)
                if n:
                    norm_step(N_CROSS_POST, n - 1, LAT)
            norm_step(N_CROSS_POST, KT - 1, LAT)
            norm_sum(N_FFN_PRE, LAT)
            for n in range(44):
                project_split("gu", n, range(KT), lead_tile, lambda k: y_2[:, k, :], LAT, after(X_SPLITS["gu"]) if n == 0 else None)
            for n in range(KT):
                project_split("down", n, range(22), hidden_lead, lambda k: tile_2[:, k, :], LAT,
                              after(X_SPLITS["down"]) if n == 0 else None)
                if n:
                    norm_step(N_FFN_POST, n - 1, LAT)
            norm_step(N_FFN_POST, KT - 1, LAT)


def tiles_of_rows(v):
    return np.ascontiguousarray(np.moveaxis(np.asarray(v).reshape(-1, P), 1, 0))


def feature_major(x):
    t, f = x.shape
    return x.T.reshape(f // P, P, t).transpose(1, 0, 2)


def chunks_of(w):
    k, n = w.shape
    return w.reshape(k // P, P, n // P, P).transpose(2, 1, 0, 3).reshape(n // P, P, k)


def head_pairs(heads, width=HD):
    return np.concatenate([np.arange(h * width, (h + 1) * width) for h in heads])


def in_order():
    start = dict(zip(("cb", "cc", "cv", "cz", "aq", "ak", "av", "az", "hq", "ff", "fb", "hi", "hz", "fu", "fz"),
                     np.cumsum([0, 256, 256, 256, 256, 256, 128, 128, 256, 256, 256, 256, 256, 256, 256])))
    whole = lambda name, n=256: start[name] + np.arange(n)
    heads = head_pairs((0, 2, 1, 3))
    return np.concatenate([whole("hq"), whole("hz"), whole("ff"), whole("fb"), whole("hi"), start["aq"] + heads,
                           whole("ak", 128), whole("av", 128), start["az"] + heads, whole("fu"), whole("fz"),
                           whole("cb"), whole("cz"), whole("cc"), whole("cv")])


def dft(n):
    k = np.outer(np.arange(n), np.arange(n)) % n
    return np.cos(2 * np.pi * k / n) / np.sqrt(n), np.sin(2 * np.pi * k / n) / np.sqrt(n)


def dft_chunks():
    c, s = dft(LAT)
    lat = np.concatenate([c.reshape(NLAT, P, LAT), -s.reshape(NLAT, P, LAT)], axis=2)
    c, s = dft(CTX)
    ctx = np.concatenate([c.reshape(2, P, CTX), -s.reshape(2, P, CTX)], axis=2).transpose(1, 0, 2).reshape(1, P, CHUNK)
    return lat, ctx


def half_mask(b, back):
    s, t = np.arange(P)[:, None], np.arange(P)[None, :]
    read, written = (t % (2 * b) >= b, s % (2 * b) < b) if not back else (t % (2 * b) < b, s % (2 * b) >= b)
    return (s // (2 * b) == t // (2 * b)) & read & written


def level_masks(back):
    t = np.arange(P)
    return np.concatenate([half_mask(1 << l, back)[:, ((t >> l) & 1) == (0 if back else 1)] for l in range(LEVELS)], 1)


def rotation(pairs):
    r = np.zeros((P, P))
    for a, b in pairs:
        r[b, a] = -1.0
        r[a, b] = 1.0
    return r


def constants():
    n = HD // 4
    rows, cols = np.divmod(np.arange(LAT), 64)
    freqs = (10000.0 ** (-np.arange(n, dtype=np.float32) / n)).astype(np.float32)
    ang = np.concatenate([rows[:, None].astype(np.float32) * freqs, cols[:, None].astype(np.float32) * freqs], 1)
    wide = lambda f: np.tile(np.repeat(f(ang.astype(np.float64)), 2, axis=1), (1, 2)).T
    head = np.kron(np.eye(2), np.ones((HD, HD)))
    c, s = dft(HD)
    ch = np.concatenate([np.kron(np.eye(2), c), np.kron(np.eye(2), s)], 1)
    pairs = [(64 * h + 2 * i, 64 * h + 2 * i + 1) for h in range(2) for i in range(32)]
    c1 = np.concatenate([np.eye(P), np.ones((P, P)), head, rotation(pairs), wide(np.cos), wide(np.sin), ch,
                         level_masks(False), level_masks(True)], 1)
    s, t = np.arange(P)[:, None], np.arange(P)[None, :]
    halves = [(64 * h + i, 64 * h + 32 + i) for h in range(2) for i in range(32)]
    inv_freq = (10000.0 ** (-np.arange(32, dtype=np.float32) / 32)).astype(np.float32)
    c2 = np.concatenate([(s <= t), (s >= t)] + [half_mask(1 << l, back) for back in (False, True) for l in range(LEVELS)]
                        + [np.where(t >= s, 0, NEG), np.zeros((P, P)), np.where(t <= s, 0, NEG), rotation(halves),
                           np.tile(inv_freq, 4)[:, None]], 1)
    assert c1.shape[1] == N_CONST and c2.shape[1] == N_CONST2
    return c1.astype(np.float32), c2.astype(np.float32)


def in_2_order():
    return np.concatenate([head_pairs([h for i in range(4) for h in (i, i + 4)]), np.arange(512, 2816)])


def lay_out(i):
    a = {k: np.asarray(v) for k, v in i.items()}
    lat, ctx = dft_chunks()
    heads = head_pairs((0, 2, 1, 3))
    out_rows = np.concatenate([np.arange(256), 256 + heads, np.arange(512, 1024)])
    dn_rows = np.concatenate([head_pairs([h for k in range(4) for h in (k, k + 4)]), np.arange(512, 1024)])
    stream = [chunks_of(a["w_mod"][0])]
    for ly in range(DEPTH):
        proj = chunks_of(a["w_in"][ly][:, in_order()])
        if ly == 0:
            pairs = np.stack([chunks_of(a["w_mod"][1]), proj[0:N_MOD]], 1).reshape(2 * N_MOD, P, CHUNK)
            proj = np.concatenate([pairs, proj[N_MOD:]], 0)
        stream += [proj, lat.astype(np.float32)]
        stream += [ctx.astype(np.float32)] if ly == 0 else []
        stream += [chunks_of(a["w_out"][ly][out_rows])]
    w_in_2 = a["w_in_2"][0]
    ab = np.zeros((D, P), np.float32)
    ab[:, 0:16] = w_in_2[:, 2816:2832]
    down = np.zeros((24 * P, D), np.float32)
    down[0:2816] = a["w_down_2"][0]
    ckv = a["w_ckv_2"][0]
    gu = a["w_gate_up_2"][0].reshape(D, 2, 22, P).transpose(0, 2, 1, 3).reshape(D, 44 * P)
    stream += [chunks_of(ckv[:, 0:D]), chunks_of(ckv[:, D:]), chunks_of(w_in_2[:, in_2_order()]), chunks_of(ab),
               chunks_of(a["w_out_2"][0][dn_rows]), chunks_of(a["w_cq_2"][0]), chunks_of(a["w_co_2"][0]),
               chunks_of(gu), chunks_of_down(down)]
    weights = np.concatenate(stream, 0)
    assert weights.shape == (PLAN["end"], P, CHUNK)
    wide = lambda v: np.broadcast_to(v.reshape(1, -1), (P, v.size))
    par = {
        "c": np.stack([a["c"][0].reshape(KT, P), a["c_ctx"].reshape(KT, P)], 2).transpose(1, 0, 2).reshape(P, 2 * KT),
        "norm_g": tiles_of_rows(a["norm_g"]), "b_mod": tiles_of_rows(a["b_mod"]), "conv_w": tiles_of_rows(a["conv_w"]),
        "q_g": np.tile(a["q_norm_g"], (1, 2)).T, "k_g": np.tile(a["k_norm_g"], (1, 2)).T,
        "lb": tiles_of_rows(a["hgrn_lb"].transpose(1, 0, 2)), "hg_g": tiles_of_rows(a["hgrn_norm_g"]),
        "final_g": tiles_of_rows(a["final_g"]), "g_mix_pre": tiles_of_rows(a["g_mix_pre_2"]),
        "conv2": a["conv_w_2"][0].reshape(5, 12, P).transpose(2, 1, 0).reshape(P, 60), "a_log": wide(a["a_log_2"]),
        "dt_bias": wide(a["dt_bias_2"]), "g_dn": a["g_dn_out_2"].T, "sink": wide(a["attn_sink_2"]),
        "g_mix_post": tiles_of_rows(a["g_mix_post_2"]), "g_cross_pre": tiles_of_rows(a["g_cross_pre_2"]),
        "g_mem": tiles_of_rows(a["g_mem_2"]), "g_cross_post": tiles_of_rows(a["g_cross_post_2"]),
        "g_ffn_pre": tiles_of_rows(a["g_ffn_pre_2"]), "g_ffn_post": tiles_of_rows(a["g_ffn_post_2"]),
    }
    const, const2 = constants()
    return {
        "tokens": np.concatenate([feature_major(a["x"][0]), feature_major(a["ctx"][0])], 2),
        "mem": feature_major(a["mem_2"][0]), "positions": np.broadcast_to(a["positions_2"], (P, LAT)),
        "weights": weights, "const": const, "const2": const2,
        "par": np.concatenate([par[n] for n in PAR_COLS], 1),
    }


def chunks_of_down(w):
    return w.reshape(3, KT, P, KT, P).transpose(3, 0, 2, 1, 4).reshape(3 * KT, P, CHUNK)


def kernel(**inputs):
    import concourse.bacc as bacc
    from concourse.bass_utils import run_bass_kernel_spmd

    nc = bacc.Bacc("TRN2", target_bir_lowering=False, num_devices=1)
    arrays = {n: np.ascontiguousarray(v) for n, v in lay_out(inputs).items()}
    args = [nc.dram_tensor(n, v.shape, mybir.dt.from_np(v.dtype), kind="ExternalInput").ap() for n, v in arrays.items()]
    out = nc.dram_tensor("out", (P, KT, LAT), F32, kind="ExternalOutput").ap()
    build(nc, *args, out)
    got = run_bass_kernel_spmd(nc, [arrays], core_ids=[0]).results[0]["out"]
    return np.ascontiguousarray(got.transpose(2, 1, 0).reshape(1, LAT, D))
```
